# Optimizing a Trainium2 kernel written in Bass

```python
import jax, jax.numpy as jnp
from jax import lax
import numpy as np

D_MODEL = 1024
BATCH = 1
SEQ = 256
DEPTH = 2
DEC_BATCH = 8
DEC_SEQ = 1
PAST_LEN = 256
PAGE_SIZE = 128

N_A_LAYERS = DEPTH // 2
N_B_LAYERS = DEPTH - N_A_LAYERS
N_DENSE_LAYERS = (DEPTH + 1) // 2
N_MOE_LAYERS = DEPTH // 2

CHUNK = 128
D_A = D_MODEL
A_GROUPS = 8
A_GROUP_DIM = D_A // A_GROUPS

N_HEADS = 16
HEAD_DIM = D_MODEL // N_HEADS
N_KV_GROUPS = 4
Q_PER_GROUP = N_HEADS // N_KV_GROUPS
CMP_LEN = 32
CMP_STRIDE = 16
CMP_HIDDEN = HEAD_DIM
SLC_BLOCK = 64
N_TOP = 16
WINDOW = 512
Q_BLOCK = 64
N_BRANCH_KV = 6
N_PAGED_KV = 4
N_WIN_KV = 2

D_FF = 2816
N_EXPERTS = 8
TOP_K = 2
MOE_ROWS = 128

RMS_EPS = 1e-6
LN_EPS = 1e-5
NEG_INF = -1e30
FORCE_SCORE = 1e4
F32 = jnp.float32

kernel_name = 'yoco_gmlp_nsa_hybrid_step'

def rmsnorm(x, g):
    xf = x.astype(F32)
    y = xf * lax.rsqrt(jnp.mean(xf * xf, axis=-1, keepdims=True) + RMS_EPS)
    return (y * g.astype(F32)).astype(x.dtype)

def layernorm(x, g, b):
    xf = x.astype(F32)
    mu = jnp.mean(xf, axis=-1, keepdims=True)
    var = jnp.mean(jnp.square(xf - mu), axis=-1, keepdims=True)
    y = (xf - mu) * lax.rsqrt(var + LN_EPS)
    return (y * g.astype(F32) + b.astype(F32)).astype(x.dtype)

def masked_softmax(s, mask):
    s = jnp.where(mask, s.astype(F32), NEG_INF)
    return jnp.where(mask, jax.nn.softmax(s, axis=-1), 0.0)

def alibi_slopes():
    h = np.arange(1, N_HEADS + 1, dtype=np.float32)
    return jnp.asarray(2.0 ** (-8.0 * h / N_HEADS), dtype=F32).reshape(N_KV_GROUPS, Q_PER_GROUP)

def swiglu(x, wg, wu, wd):
    return (jax.nn.silu(x @ wg) * (x @ wu)) @ wd

def moe_swiglu(x, w_router, b_router, w_gate, w_up, w_down):
    bsz, L, d = x.shape
    xt = x.reshape(-1, d)
    n = xt.shape[0]
    logits = (xt @ w_router + b_router).astype(F32)
    top_val, top_idx = lax.top_k(logits, TOP_K)
    gate = jax.nn.softmax(top_val, axis=-1)
    a = n * TOP_K
    expert = top_idx.reshape(a)
    token = jnp.arange(a, dtype=jnp.int32) // TOP_K
    order = jnp.argsort(expert)
    e_sorted = expert[order]
    counts = jnp.bincount(expert, length=N_EXPERTS)
    padded = (counts + MOE_ROWS - 1) // MOE_ROWS * MOE_ROWS
    pad_end = jnp.cumsum(padded)
    pad_start = pad_end - padded
    start = jnp.cumsum(counts) - counts
    dest = pad_start[e_sorted] + jnp.arange(a, dtype=jnp.int32) - start[e_sorted]
    n_rows = (-(-a // MOE_ROWS) + N_EXPERTS) * MOE_ROWS
    row_token = jnp.full((n_rows,), n, jnp.int32).at[dest].set(token[order])
    row_gate = jnp.zeros((n_rows,), F32).at[dest].set(gate.reshape(a)[order])
    x_rows = jnp.concatenate([xt, jnp.zeros((1, d), xt.dtype)], axis=0)[row_token]
    x_rows = x_rows.reshape(n_rows // MOE_ROWS, MOE_ROWS, d)
    blk_start = jnp.arange(n_rows // MOE_ROWS, dtype=jnp.int32) * MOE_ROWS
    blk_expert = jnp.minimum(jnp.sum(pad_end[None, :] <= blk_start[:, None], axis=1), N_EXPERTS - 1)

    def expert_block(args):
        xb, e = args
        return swiglu(xb, w_gate[e], w_up[e], w_down[e])

    y_rows = lax.map(expert_block, (x_rows, blk_expert)).reshape(n_rows, d)
    y = jnp.zeros((n + 1, d), F32).at[row_token].add(y_rows.astype(F32) * row_gate[:, None])
    return y[:n].astype(x.dtype).reshape(bsz, L, d)

def chunk_gmlp(h, w_in, ln_g, ln_b, w_s, b_s, w_out):
    bsz, L, _ = h.shape
    z = jax.nn.gelu(h @ w_in)
    u, v = jnp.split(z, 2, axis=-1)
    v = layernorm(v, ln_g, ln_b)
    n_chunks = -(-L // CHUNK)
    vc = jnp.pad(v, ((0, 0), (0, n_chunks * CHUNK - L), (0, 0)))
    vc = vc.reshape(bsz, n_chunks, CHUNK, A_GROUPS, A_GROUP_DIM)
    causal = jnp.tril(jnp.ones((CHUNK, CHUNK), w_s.dtype))
    mixed = jnp.einsum('gts,bcsge->bctge', w_s * causal, vc) + b_s.T[:, :, None]
    mixed = mixed.reshape(bsz, n_chunks * CHUNK, D_A)[:, :L]
    out = (u * mixed) @ w_out
    last = ((L - 1) // CHUNK) * CHUNK
    return out, v[:, last:]

def compress_blocks(x_raw, pe, w1, w2):
    Lk = x_raw.shape[1]
    n_cmp = (Lk - CMP_LEN) // CMP_STRIDE + 1
    idx = np.arange(n_cmp)[:, None] * CMP_STRIDE + np.arange(CMP_LEN)[None, :]
    blocks = x_raw[:, idx] + pe[None, None, :, None, :]
    hid = jax.nn.gelu(jnp.einsum('bnlgd,lde->bnge', blocks, w1))
    return jnp.einsum('bnge,ed->bngd', hid, w2)

def cmp_to_sel_overlap(n_cmp, n_sel):
    c0 = np.arange(n_cmp)[:, None] * CMP_STRIDE
    s0 = np.arange(n_sel)[None, :] * SLC_BLOCK
    return jnp.asarray(((c0 < s0 + SLC_BLOCK) & (c0 + CMP_LEN > s0)).astype(np.float32))

def build_nsa_shared(rows, win_rows, cmp_pe, cmp_w1, cmp_w2):
    bsz, Lk = rows.shape[:2]
    kc = compress_blocks(rows[:, :, 0], cmp_pe[0], cmp_w1[0], cmp_w2[0])
    vc = compress_blocks(rows[:, :, 1], cmp_pe[1], cmp_w1[1], cmp_w2[1])
    n_sel = -(-Lk // SLC_BLOCK)
    slc = jnp.pad(rows[:, :, 2:4], ((0, 0), (0, n_sel * SLC_BLOCK - Lk), (0, 0), (0, 0), (0, 0)))
    slc = slc.reshape(bsz, n_sel, SLC_BLOCK, 2, N_KV_GROUPS, HEAD_DIM).transpose(3, 0, 4, 1, 2, 5)
    win = jnp.pad(win_rows, ((0, 0), (WINDOW, Q_BLOCK), (0, 0), (0, 0), (0, 0)))
    return (kc, vc, slc[0], slc[1], win[:, :, 0], win[:, :, 1])

def nsa_layer(h, q_pos0, w_pos0, shared, w_in, b_gate, w_out):
    kc, vc, ks, vs, kw, vw = shared
    bsz, Lq, _ = h.shape
    proj = h @ w_in
    q = proj[..., :N_HEADS * HEAD_DIM].reshape(bsz, Lq, N_KV_GROUPS, Q_PER_GROUP, HEAD_DIM) * (HEAD_DIM ** -0.5)
    gates = jax.nn.sigmoid(proj[..., N_HEADS * HEAD_DIM:] + b_gate).reshape(bsz, Lq, N_KV_GROUPS, Q_PER_GROUP, 3)
    qb = min(Q_BLOCK, Lq)
    nqb = -(-Lq // qb)
    pad = nqb * qb - Lq

    def to_blocks(a):
        a = jnp.pad(a, ((0, 0), (0, pad)) + ((0, 0),) * (a.ndim - 2))
        return a.reshape((bsz, nqb, qb) + a.shape[2:]).swapaxes(0, 1)

    slopes = alibi_slopes()
    n_cmp = kc.shape[1]
    n_sel = ks.shape[2]
    n_top = min(N_TOP, n_sel)
    cmp_end = jnp.asarray(np.arange(n_cmp) * CMP_STRIDE + CMP_LEN - 1, jnp.int32)
    overlap = cmp_to_sel_overlap(n_cmp, n_sel)
    sel_ids = jnp.arange(n_sel, dtype=jnp.int32)
    b_ix = jnp.arange(bsz)[:, None, None, None]
    g_ix = jnp.arange(N_KV_GROUPS)[None, :, None, None]
    wb = WINDOW + qb - 1

    def attend_block(args):
        qblk, gblk, j0 = args
        t = q_pos0 + j0 + jnp.arange(qb, dtype=jnp.int32)
        s_c = jnp.einsum('bqgrd,bngd->bgrqn', qblk, kc).astype(F32)
        d_c = t[:, None] - cmp_end[None, :]
        p_c = masked_softmax(s_c - slopes[:, :, None, None] * d_c, d_c >= 0)
        o_c = jnp.einsum('bgrqn,bngd->bqgrd', p_c.astype(vc.dtype), vc)
        imp = jnp.einsum('bgrqn,nj->bgqj', p_c, overlap)
        cur = t // SLC_BLOCK
        valid = sel_ids[None, :] <= cur[:, None]
        forced = (sel_ids[None, :] == 0) | (sel_ids[None, :] == cur[:, None]) | (sel_ids[None, :] == cur[:, None] - 1)
        score = jnp.where(valid, jnp.where(forced, FORCE_SCORE, imp), NEG_INF)
        _, top = lax.top_k(score, n_top)
        k_sel = ks[b_ix, g_ix, top]
        v_sel = vs[b_ix, g_ix, top].reshape(bsz, N_KV_GROUPS, qb, n_top * SLC_BLOCK, HEAD_DIM)
        pos_s = top[..., None] * SLC_BLOCK + jnp.arange(SLC_BLOCK, dtype=jnp.int32)
        d_s = (t[:, None, None] - pos_s).reshape(bsz, N_KV_GROUPS, qb, n_top * SLC_BLOCK)[:, :, None]
        s_s = jnp.einsum('bqgrd,bgqnkd->bgrqnk', qblk, k_sel).astype(F32)
        s_s = s_s.reshape(bsz, N_KV_GROUPS, Q_PER_GROUP, qb, n_top * SLC_BLOCK)
        p_s = masked_softmax(s_s - slopes[None, :, :, None, None] * d_s, d_s >= 0)
        o_s = jnp.einsum('bgrqk,bgqkd->bqgrd', p_s.astype(v_sel.dtype), v_sel)
        k0 = q_pos0 + j0 - WINDOW + 1
        start = k0 - w_pos0 + WINDOW
        kwb = lax.dynamic_slice_in_dim(kw, start, wb, axis=1)
        vwb = lax.dynamic_slice_in_dim(vw, start, wb, axis=1)
        pos_w = k0 + jnp.arange(wb, dtype=jnp.int32)
        d_w = t[:, None] - pos_w[None, :]
        m_w = (d_w >= 0) & (d_w < WINDOW) & (pos_w >= w_pos0)[None, :]
        s_w = jnp.einsum('bqgrd,bkgd->bgrqk', qblk, kwb).astype(F32)
        p_w = masked_softmax(s_w - slopes[:, :, None, None] * d_w, m_w)
        o_w = jnp.einsum('bgrqk,bkgd->bqgrd', p_w.astype(vwb.dtype), vwb)
        return gblk[..., 0:1] * o_c + gblk[..., 1:2] * o_s + gblk[..., 2:3] * o_w

    j0s = jnp.arange(nqb, dtype=jnp.int32) * qb
    out = lax.map(attend_block, (to_blocks(q), to_blocks(gates), j0s))
    out = out.swapaxes(0, 1).reshape(bsz, nqb * qb, N_HEADS * HEAD_DIM)[:, :Lq]
    return out @ w_out

def run_trunk(x, q_pos0, past_rows, past_win,
              norm_mix, norm_ffn, norm_final,
              a_w_in, a_ln_g, a_ln_b, a_w_s, a_b_s, a_w_out,
              kv_norm, w_kv, cmp_pe, cmp_w1, cmp_w2,
              b_w_in, b_b_gate, b_w_out,
              f_w_gate, f_w_up, f_w_down,
              m_w_router, m_b_router, m_w_gate, m_w_up, m_w_down):
    bsz, L = x.shape[:2]
    a_states = []
    shared = None
    w_pos0 = 0
    for layer in range(DEPTH):
        if layer == N_A_LAYERS:
            kv = (rmsnorm(x, kv_norm) @ w_kv).reshape(bsz, L, N_BRANCH_KV, N_KV_GROUPS, HEAD_DIM)
            new_rows = kv[:, :, :N_PAGED_KV]
            new_win = kv[:, :, N_PAGED_KV:]
            if past_rows is None:
                rows, win = new_rows, new_win
                w_pos0 = 0
            else:
                rows = jnp.concatenate([past_rows.astype(new_rows.dtype), new_rows], axis=1)
                win = jnp.concatenate([past_win.astype(new_win.dtype), new_win], axis=1)
                w_pos0 = q_pos0 - past_win.shape[1]
            win_state = win[:, win.shape[1] - min(WINDOW, win.shape[1]):]
            shared = build_nsa_shared(rows, win, cmp_pe, cmp_w1, cmp_w2)
        h = rmsnorm(x, norm_mix[layer])
        if layer < N_A_LAYERS:
            mix, v_rows = chunk_gmlp(h, a_w_in[layer], a_ln_g[layer], a_ln_b[layer], a_w_s[layer], a_b_s[layer], a_w_out[layer])
            a_states.append(v_rows)
        else:
            i = layer - N_A_LAYERS
            mix = nsa_layer(h, q_pos0, w_pos0, shared, b_w_in[i], b_b_gate[i], b_w_out[i])
        x = x + mix
        h = rmsnorm(x, norm_ffn[layer])
        j = layer // 2
        if layer % 2 == 0:
            x = x + swiglu(h, f_w_gate[j], f_w_up[j], f_w_down[j])
        else:
            x = x + moe_swiglu(h, m_w_router[j], m_b_router[j], m_w_gate[j], m_w_up[j], m_w_down[j])
    return rmsnorm(x, norm_final), new_rows, win_state, jnp.stack(a_states)

def setup_inputs(seed: int = 0) -> dict:
    key = jax.random.key(seed)
    keys = iter(jax.random.split(key, 40))

    def nrm(shape, scale):
        return jax.random.normal(next(keys), shape, F32) * scale

    n_pages = PAST_LEN // PAGE_SIZE
    n_used = DEC_BATCH * n_pages
    n_phys = n_used + (n_used + 3) // 4
    page_table = jax.random.permutation(next(keys), n_phys)[:n_used].reshape(DEC_BATCH, n_pages).astype(jnp.int32)
    gate_cols = N_HEADS * HEAD_DIM + 3 * N_HEADS
    return {
        'x_prompt': nrm((BATCH, SEQ, D_MODEL), 1.0),
        'x_sample': nrm((DEC_BATCH, DEC_SEQ, D_MODEL), 1.0),
        'cache_kv': nrm((n_phys, PAGE_SIZE, N_PAGED_KV, N_KV_GROUPS, HEAD_DIM), 1.0),
        'state_win_kv': nrm((DEC_BATCH, min(WINDOW, PAST_LEN), N_WIN_KV, N_KV_GROUPS, HEAD_DIM), 1.0),
        'page_table': page_table,
        'norm_mix': 1.0 + nrm((DEPTH, D_MODEL), 0.1),
        'norm_ffn': 1.0 + nrm((DEPTH, D_MODEL), 0.1),
        'norm_final': 1.0 + nrm((D_MODEL,), 0.1),
        'a_w_in': nrm((N_A_LAYERS, D_MODEL, 2 * D_A), D_MODEL ** -0.5),
        'a_ln_g': 1.0 + nrm((N_A_LAYERS, D_A), 0.1),
        'a_ln_b': nrm((N_A_LAYERS, D_A), 0.02),
        'a_w_s': nrm((N_A_LAYERS, A_GROUPS, CHUNK, CHUNK), CHUNK ** -0.5),
        'a_b_s': 1.0 + nrm((N_A_LAYERS, A_GROUPS, CHUNK), 0.1),
        'a_w_out': nrm((N_A_LAYERS, D_A, D_MODEL), D_A ** -0.5),
        'kv_norm': 1.0 + nrm((D_MODEL,), 0.1),
        'w_kv': nrm((D_MODEL, N_BRANCH_KV * N_KV_GROUPS * HEAD_DIM), D_MODEL ** -0.5),
        'cmp_pe': nrm((2, CMP_LEN, HEAD_DIM), 0.1),
        'cmp_w1': nrm((2, CMP_LEN, HEAD_DIM, CMP_HIDDEN), (CMP_LEN * HEAD_DIM) ** -0.5),
        'cmp_w2': nrm((2, CMP_HIDDEN, HEAD_DIM), CMP_HIDDEN ** -0.5),
        'b_w_in': nrm((N_B_LAYERS, D_MODEL, gate_cols), D_MODEL ** -0.5),
        'b_b_gate': nrm((N_B_LAYERS, 3 * N_HEADS), 0.1),
        'b_w_out': nrm((N_B_LAYERS, N_HEADS * HEAD_DIM, D_MODEL), (N_HEADS * HEAD_DIM) ** -0.5),
        'f_w_gate': nrm((N_DENSE_LAYERS, D_MODEL, D_FF), D_MODEL ** -0.5),
        'f_w_up': nrm((N_DENSE_LAYERS, D_MODEL, D_FF), D_MODEL ** -0.5),
        'f_w_down': nrm((N_DENSE_LAYERS, D_FF, D_MODEL), D_FF ** -0.5),
        'm_w_router': nrm((N_MOE_LAYERS, D_MODEL, N_EXPERTS), D_MODEL ** -0.5),
        'm_b_router': nrm((N_MOE_LAYERS, N_EXPERTS), 0.01),
        'm_w_gate': nrm((N_MOE_LAYERS, N_EXPERTS, D_MODEL, D_FF), D_MODEL ** -0.5),
        'm_w_up': nrm((N_MOE_LAYERS, N_EXPERTS, D_MODEL, D_FF), D_MODEL ** -0.5),
        'm_w_down': nrm((N_MOE_LAYERS, N_EXPERTS, D_FF, D_MODEL), D_FF ** -0.5),
    }

def reference(x_prompt, x_sample, cache_kv, state_win_kv, page_table,
              norm_mix, norm_ffn, norm_final,
              a_w_in, a_ln_g, a_ln_b, a_w_s, a_b_s, a_w_out,
              kv_norm, w_kv, cmp_pe, cmp_w1, cmp_w2,
              b_w_in, b_b_gate, b_w_out,
              f_w_gate, f_w_up, f_w_down,
              m_w_router, m_b_router, m_w_gate, m_w_up, m_w_down):
    weights = (norm_mix, norm_ffn, norm_final,
               a_w_in, a_ln_g, a_ln_b, a_w_s, a_b_s, a_w_out,
               kv_norm, w_kv, cmp_pe, cmp_w1, cmp_w2,
               b_w_in, b_b_gate, b_w_out,
               f_w_gate, f_w_up, f_w_down,
               m_w_router, m_b_router, m_w_gate, m_w_up, m_w_down)
    y_prompt, kv_rows_prompt, win_prompt, gmlp_v_prompt = run_trunk(x_prompt, 0, None, None, *weights)
    n_pages = page_table.shape[1]
    past_rows = cache_kv[page_table].reshape(x_sample.shape[0], n_pages * cache_kv.shape[1], N_PAGED_KV, N_KV_GROUPS, HEAD_DIM)
    y_sample, kv_rows_sample, win_sample, gmlp_v_sample = run_trunk(x_sample, past_rows.shape[1], past_rows, state_win_kv, *weights)
    return (y_prompt, y_sample, kv_rows_prompt, kv_rows_sample, win_prompt, win_sample, gmlp_v_prompt, gmlp_v_sample)


_drawn_inputs = setup_inputs


def setup_inputs(seed=0):
    import zlib

    import numpy as np

    out = dict(_drawn_inputs(seed))
    spreads = {}
    factors = {'a_ln_b': 2.933, 'm_b_router': 2.879}
    for name, (base, spread) in spreads.items():
        noise = np.random.default_rng([zlib.crc32(name.encode()), seed]).standard_normal(out[name].shape)
        drawn = base * np.exp(spread * noise) if base else spread * noise
        out[name] = __import__('jax').numpy.asarray(drawn.astype(out[name].dtype))
    for name, factor in factors.items():
        out[name] = (out[name] * factor).astype(out[name].dtype)
    return out
```

```python
from contextlib import ExitStack

import numpy as np

import concourse.bass as bass
from concourse import mybir

F32 = mybir.dt.float32
I32 = mybir.dt.int32
F32R = mybir.dt.float32r
ALU = mybir.AluOpType
ACT = mybir.ActivationFunctionType
AX_X = mybir.AxisListType.X

P = 128
DM = 1024
KC = DM // P
NP = 256
NS = 8
NT = NP + NS
PAST = 256
HD = 64
NH = 16
NG = 4
FF = 2816
FC = FF // P
FT = FF // 256
NE = 8
ROWS = 128
MAXB = 12
NCMP = 15
CMP_LEN, CMP_STRIDE = 32, 16
RMS_EPS, LN_EPS = 1e-6, 1e-5
BIG = 1e30
SLOT = 4096
UNIT, ITEM = 2048, 1024
USE = [(f, kind) for f in range(FT + 2) for kind in "abd" if (f < FT if kind != "d" else f >= 2)]
UNITS = len(USE)
ITEMS = 2 * UNITS
UP_END = {f: 2 * u + 2 for u, (f, kind) in enumerate(USE) if kind == "b"}
DOWN_END = {f - 2: 2 * u + 2 for u, (f, kind) in enumerate(USE) if kind == "d"}
NRAW = 11
NSPLIT = 6
PAGES = 2

SLOPE = [2.0 ** (-8.0 * (h + 1) / NH) for h in range(NH)]


def layout(widths):
    at, out = 0, {}
    for name, w in widths:
        out[name] = (at, at + w)
        at += w
    return out, at


CONSTS, NC_ = layout([("ident", P), ("mean", P), ("ones", NT), ("before", P), ("upto", P), ("dist", 414),
                      ("cmpmask", 30), ("sdist", PAST + NS), ("scdist", NS * NCMP), ("negslope", 1),
                      ("iota", P), ("down8", NE), ("blk", MAXB * NE), ("eps", 2)])
PARAMS, NPAR = layout([("mix0", 8), ("mix1", 8), ("ffn0", 8), ("lng", 8), ("lnb", 8), ("kvn", 8),
                       ("pe", 32), ("w00", 8), ("gate", 8 * 48), ("w1", 2048),
                       ("w2k", 256), ("w2v", 64), ("wst", 1024)])
LATE, NLATE = layout([("ffn1", 8), ("final", 8), ("router", 64), ("brouter", 8)])
ROW, NROW = layout([("bs", 8 * NT), ("bgate", 48)])


def constants():
    c = np.zeros((P, NC_), np.float32)

    def put(name, v):
        a, b = CONSTS[name]
        c[:, a:b] = v

    p = np.arange(P)[:, None]
    f = np.arange(P)[None, :]
    put("ident", p == f)
    put("mean", 1.0 / DM)
    put("ones", 1.0)
    put("before", p < f)
    put("upto", p <= f)
    ends = np.arange(NCMP) * CMP_STRIDE + CMP_LEN - 1
    d = np.concatenate([p - f, p + P - np.arange(NP)[None, :], p - ends[None, :], p + P - ends[None, :]], axis=1)
    put("dist", np.where(d >= 0, d, BIG))
    put("cmpmask", d[:, 384:414] >= 0)
    own = (p // NH) == np.arange(NS)[None, :]
    put("sdist", np.concatenate([np.broadcast_to(PAST - np.arange(PAST)[None, :], (P, PAST)), np.where(own, 0.0, BIG)], axis=1))
    put("scdist", np.where(np.repeat(own, NCMP, axis=1), np.tile(PAST - ends, NS)[None, :], BIG))
    put("negslope", -np.array(SLOPE, np.float32)[np.arange(P) % NH][:, None])
    put("iota", f)
    put("down8", NE - np.arange(NE)[None, :])
    put("eps", np.array([[RMS_EPS, LN_EPS]]))
    put("blk", np.repeat(np.arange(MAXB), NE)[None, :])
    return c


TILES = (["v0", "v1", "u0", "u1", "ao0", "ao1"] + [f"gu{i}" for i in range(FT)]
         + [f"dn{i}" for i in range(6)] + ["kv0", "kv1", "kv2", "bi0", "bi1", "SK", "WK", "SV", "WV", "bo0", "bo1"])
WTILES = [t for t in TILES if t[1] not in "KV"]
INDEX = {t: n for n, t in enumerate(TILES)}
NSLOT = 3


def build(nc, xT, wd, moe, params, late_in, rows, consts, cmp_pages, k_pages, v_pages, win_k, win_v, state_win, page_table,
          y_out, v_out, kv_out, past_out):
    with ExitStack() as ctx:
        def sb(name, shape, dt=F32):
            return ctx.enter_context(nc.sbuf_tensor(name, shape, dt))

        def sem(name):
            return ctx.enter_context(nc.semaphore(name))

        C = sb("consts_sb", [P, NC_])
        LT = sb("late_sb", [P, NLATE])
        x = sb("x", [P, KC, NT])
        hB = sb("hB", [P, KC, NT])
        rstd = sb("rstd", [P, NT])
        pages = sb("pages", [1, NS * PAGES], I32)
        blkinfo = sb("blkinfo", [1, 16], I32)

        dense_memory = ctx.enter_context(ExitStack())

        def sbd(name, shape, dt=F32):
            return dense_memory.enter_context(nc.sbuf_tensor(name, shape, dt))

        ARENA = 24200
        arena = sbd("arena", [P, ARENA])
        PR = sbd("params_sb", [P, NPAR])
        RW = sbd("rows_sb", [1, NROW])
        hA = sbd("hA", [P, KC, NT])
        sq = sbd("sq", [P, KC, NT])
        ring = sbd("ring", [P, NSLOT, SLOT])
        top = [0]

        def carve(*shape):
            n = int(np.prod(shape))
            v = arena[:, top[0]:top[0] + n]
            top[0] += n
            assert top[0] <= ARENA, top[0]
            if len(shape) == 2:
                v = v.rearrange("p (a b) -> p a b", b=shape[1])
            if len(shape) == 3:
                v = v.rearrange("p (a b c) -> p a b c", b=shape[1], c=shape[2])
            return v

        uT = carve(KC, NT)
        vT = carve(KC, NT)
        vtok = carve(3, DM)
        wsT = carve(8, P)
        dg = carve(8, NS)
        mu = carve(NT)
        top[0] = 0
        hF = carve(FC, NT)
        sil = carve(2, NT)
        top[0] = 0
        kvT = carve(12, NT)
        Q = carve(NH, NT)
        Qz = carve(2, NS, P)
        Qc = carve(2, P)
        vtp = carve(2, 2, 2 * P)
        vnew = carve(2, 2 * P)
        gT = carve(NT)
        gtok = carve(2, 48)
        gsam = carve(48)
        grow = carve(3)
        hidb = carve(580)
        hid = carve(36, NCMP)
        cbias = carve(1)
        kcT = carve(18, NCMP)
        vcs = carve(2 * P)
        vcp = carve(2 * P)
        x2_at = top[0]
        X2 = carve(2, 8 * PAGES * NG * 64 + NG * P + 16)
        top[0] = x2_at
        Sh = carve(3, 828)
        mx = carve(3, 6)
        sm = carve(3, 6)
        wt = carve(3, 6)
        PT = carve(2, 2, 512)
        Ss = carve(2 * (PAST + NS) + NS * NCMP)
        smx, ssm, swt = carve(3), carve(3), carve(3)
        PTs = carve(7, P)
        dense_memory.close()
        raw = sb("raw", [P, NRAW, UNIT])
        w_hi = sb("w_hi", [P, NSPLIT, ITEM], F32R)
        w_lo = sb("w_lo", [P, NSPLIT, ITEM], F32R)
        xg_hi = sb("xg_hi", [P, KC, P], F32R)
        xg_lo = sb("xg_lo", [P, KC, P], F32R)
        hm_hi = sb("hm_hi", [P, 2, 2, P], F32R)
        hm_lo = sb("hm_lo", [P, 2, 2, P], F32R)
        htok = sb("htok", [P, 3, DM])
        yrow = sb("yrow", [P, DM])
        Gm = sb("Gm", [P, 3, P])
        Gw = sb("Gw", [P, 3, P])
        Gt = sb("Gt", [P, P])
        GwT = sb("GwT", [P, NT])
        sg = sb("sg", [P, 2, 256])
        hm = sb("hm", [P, 2, 256])
        lgT = sb("lgT", [NE, NT])
        lg = sb("lg", [P, 3, 64])
        sc = sb("sc", [P, 3, 16])
        cnt = sb("cnt", [P, 64])
        bcmp = sb("bcmp", [1, MAXB * NE])
        bout = sb("bout", [1, 16])
        sq_last = htok[:].rearrange("p a b -> p (a b)")[:, 0:KC * NT].rearrange("p (k t) -> p k t", t=NT)

        def const(name):
            a, b = CONSTS[name]
            return C[:, a:b]

        def par(name):
            a, b = PARAMS[name]
            return PR[:, a:b]

        def late(name):
            a, b = LATE[name]
            return LT[:, a:b]

        ident = const("ident")
        w1 = par("w1").rearrange("p (v m e) -> p v m e", v=2, e=P)
        w_gate = par("gate").rearrange("p (k n) -> p k n", k=KC)
        w_router = late("router").rearrange("p (k n) -> p k n", k=KC)
        w2k = par("w2k").rearrange("p (a n) -> p a n", a=2)
        b_s = RW[:, ROW["bs"][0]:ROW["bs"][1]].rearrange("o (g t) -> o g t", g=8)
        b_gate = RW[:, ROW["bgate"][0]:ROW["bgate"][1]]
        b_router = late("brouter")[0:1, :]
        ones_row = C[0:1, CONSTS["ones"][0]:CONSTS["ones"][1]]

        B = [ctx.enter_context(nc.psum_tensor(f"bank{i}", [P, 512], F32)) for i in range(8)]
        STAT, T0, T1, MISC = B[4], B[5], B[6], B[7]
        HT = [B[0], B[1], B[2], B[3], T0, T1]

        slot_in = [sem(f"slot_in{i}") for i in range(NSLOT)]
        setup_in = sem("setup_in")
        x_in = sem("x_in")
        pages_in = sem("pages_in")
        cmp_in = sem("cmp_in")
        x_ready = sem("x_ready")
        sq_ready = sem("sq_ready")
        std_ready = sem("std_ready")
        stat_ready = sem("stat_ready")
        h_ready = sem("h_ready")
        dve_step = sem("dve_step")
        act_step = sem("act_step")
        acc_done = sem("acc_done")
        v_ready, u_ready = sem("v_ready"), sem("u_ready")
        mu_stat, ctr_ready, csq_ready, var_stat, vn_ready = (sem("mu_stat"), sem("ctr_ready"), sem("csq_ready"),
                                                            sem("var_stat"), sem("vn_ready"))
        vt_done, vt_ready, ws_ready = sem("vt_done"), sem("vt_ready"), sem("ws_ready")
        mix_done, gated = sem("mix_done"), sem("gated")
        ao_done = sem("ao_done")
        gate_done, up_done, sil_ready, hF_ready = sem("gate_done"), sem("up_done"), sem("sil_ready"), sem("hF_ready")
        down_done, down_part = sem("down_done"), sem("down_part")
        kv_done, kv_ready = sem("kv_done"), sem("kv_ready")
        q_done, q_even, q_odd = sem("q_done"), sem("q_even"), sem("q_odd")
        gp_done, sig_ready, gt_done, gtok_ready, grow_in = (sem("gp_done"), sem("sig_ready"), sem("gt_done"),
                                                            sem("gtok_ready"), sem("grow_in"))
        vp_done, vp_ready = sem("vp_done"), sem("vp_ready")
        q_zero, q_rows = sem("q_zero"), sem("q_rows")
        x2_ready = sem("x2_ready")
        cmp_done, bhalf_ready, pre_ready, hid_ready, cmp2_done, cmp2_ready = (
            sem("cmp_done"), sem("bhalf_ready"), sem("pre_ready"), sem("hid_ready"), sem("cmp2_done"), sem("cmp2_ready"))
        s_done, s_biased, neg_max, exps, p_ready, pt_done, pt_ready, o_done, o_ready = (
            sem("s_done"), sem("s_biased"), sem("neg_max"), sem("exps"), sem("p_ready"), sem("pt_done"),
            sem("pt_ready"), sem("o_done"), sem("o_ready"))
        ss_done, ss_max, ss_exp, sp_ready, spt_done, spt_ready, so_done, so_ready = (
            sem("ss_done"), sem("ss_max"), sem("ss_exp"), sem("sp_ready"), sem("spt_done"), sem("spt_ready"),
            sem("so_done"), sem("so_ready"))
        bo_done = sem("bo_done")
        sk_used, t_zeroed, lT_done, lT_ready = sem("sk_used"), sem("t_zeroed"), sem("lT_done"), sem("lT_ready")
        route_done, ht_done, ht_ready, rank_in, rank_done, blk_ready, exp_ready = (
            sem("route_done"), sem("ht_done"), sem("ht_ready"), sem("rank_in"), sem("rank_done"), sem("blk_ready"), sem("exp_ready"))
        raw_in = [sem(f"raw_in{i}") for i in range(NRAW)]
        hi_ready, lo_ready, item_used = sem("hi_ready"), sem("lo_ready"), sem("item_used")
        dve_sel = sem("dve_sel")
        sel_ready, gw_done, gwT_ready, xg_done, xg_hi_ready, xg_lo_ready = (sem("sel_ready"), sem("gw_done"), sem("gwT_ready"),
                                                            sem("xg_done"), sem("xg_hi_ready"), sem("xg_lo_ready"))
        sg_ready, hm_ready, hmT_done, hmT_hi, hmT_lo, yrow_ready = (
            sem("sg_ready"), sem("hm_ready"), sem("hmT_done"), sem("hmT_hi"), sem("hmT_lo"),
            sem("yrow_ready"))
        comb_done, comb_added = sem("comb_done"), sem("comb_added")
        v_stored, kv_stored, past_stored, y_stored = sem("v_stored"), sem("kv_stored"), sem("past_stored"), sem("y_stored")

        used = {"v0": (acc_done, 4), "v1": (acc_done, 8), "u0": (acc_done, 12), "u1": (acc_done, 16),
                "ao0": (ao_done, 4), "ao1": (ao_done, 8), "dn0": (down_part, 1), "dn1": (down_part, 2),
                "dn2": (down_done, 4), "dn3": (down_part, 3), "dn4": (down_part, 4), "dn5": (down_done, 8),
                "kv0": (kv_done, 4), "kv1": (kv_done, 8), "kv2": (kv_done, 12), "bi0": (q_done, 4), "bi1": (q_done, 8),
                "SK": (sk_used, 1), "WK": (sk_used, 2), "SV": (so_done, 1), "WV": (so_done, 1),
                **{f"gu{i}": (up_done, 2 * i + 2) for i in range(FT)}}

        landed, filled = {}, [0] * NSLOT
        for n, t in enumerate(TILES):
            filled[n % NSLOT] += 16 * {"SK": NS * PAGES, "SV": NS * PAGES}.get(t, 1)
            landed[t] = filled[n % NSLOT]

        def arrived(eng, t):
            eng.wait_ge(slot_in[INDEX[t] % NSLOT], landed[t])

        def tile(t):
            return ring[:, INDEX[t] % NSLOT, :]

        def wtile(t):
            return tile(t).rearrange("p (k n) -> p k n", n=512)

        block = ctx.enter_context(nc.Block())

        @block.sync
        def _(sp):
            sp.dma_start(x[:], xT).then_inc(x_in, 16)
            sp.dma_start(C[:], consts).then_inc(setup_in, 16)
            sp.dma_start(PR[:], params).then_inc(setup_in, 16)
            sp.dma_start(RW[:], rows).then_inc(setup_in, 16)
            sp.dma_start(LT[:], late_in).then_inc(setup_in, 16)
            sp.dma_start(pages[:], page_table).then_inc(pages_in, 16)
            wn = 0
            for n, t in enumerate(TILES):
                if n >= NSLOT:
                    sp.wait_ge(*used[TILES[n - NSLOT]])
                done = slot_in[n % NSLOT]
                if t in ("SK", "SV"):
                    if t == "SK":
                        sp.wait_ge(pages_in, 16)
                    for b in range(NS):
                        for i in range(PAGES):
                            pg = sp.value_load(pages[0:1, b * PAGES + i:b * PAGES + i + 1], min_val=0,
                                               max_val=k_pages.shape[0] - 1)
                            if t == "SK":
                                dst = tile(t).rearrange("p (b c i k) -> p b c i k", b=NS, c=2, i=PAGES)[:, b, :, i, :]
                                sp.dma_start(dst, k_pages[bass.ds(pg, 1)].rearrange("o p c k -> p (o c) k")).then_inc(done, 16)
                            else:
                                dst = tile(t).rearrange("p (b i v) -> p b i v", b=NS, i=PAGES)[:, b, i, :]
                                sp.dma_start(dst, v_pages[bass.ds(pg, 1)].rearrange("o p v -> (o p) v")).then_inc(done, 16)
                elif t == "WK":
                    sp.dma_start(tile(t), win_k).then_inc(done, 16)
                elif t == "WV":
                    sp.dma_start(tile(t), win_v).then_inc(done, 16)
                else:
                    w = 6 * 512 if t in ("dn2", "dn5") else SLOT
                    sp.dma_start(ring[:, n % NSLOT, 0:w], wd[wn, :, 0:w]).then_inc(done, 16)
                    wn += 1
            sp.sem_inc(lo_ready, 2 * NRAW)
            sp.sem_inc(item_used, NSPLIT)
            sp.wait_ge(so_done, 1)
            sp.wait_ge(so_ready, 1)
            sp.wait_ge(kv_stored, 16)
            for u in range(UNITS):
                if u >= NRAW:
                    sp.wait_ge(lo_ready, 2 * u + 2)
                sp.dma_start(raw[:, u % NRAW, :], moe[0, u]).then_inc(raw_in[u % NRAW], 16)
            sp.wait_ge(blk_ready, 1)
            nblk = sp.value_load(blkinfo[0:1, MAXB:MAXB + 1], min_val=2, max_val=MAXB)
            with sp.Fori(1, nblk) as t:
                e = sp.value_load(blkinfo[0:1, bass.ds(t, 1)], min_val=0, max_val=NE - 1)
                for u in range(UNITS):
                    sp.wait_ge(lo_ready, t * ITEMS + 2 * u + 2)
                    sp.dma_start(raw[:, u % NRAW, :], moe[bass.ds(e, 1), u].rearrange("o p n -> (o p) n"))\
                      .then_inc(raw_in[u % NRAW], 16)
            sp.wait_ge(h_ready, 48)
            sp.dma_start(y_out, hB[:]).then_inc(y_stored, 16)
            for stored in (y_stored, v_stored, kv_stored, past_stored):
                sp.wait_ge(stored, 16)

        @block.gpsimd
        def _(pool):
            pool.dma_start(past_out, state_win).then_inc(past_stored, 16)
            pool.wait_ge(vn_ready, 8)
            pool.dma_start(v_out, vT).then_inc(v_stored, 16)
            pool.wait_ge(pages_in, 16)
            pool.wait_ge(down_done, 8)
            for b in range(NS):
                for i in range(PAGES):
                    pg = pool.value_load(pages[0:1, b * PAGES + i:b * PAGES + i + 1], min_val=0,
                                         max_val=cmp_pages.shape[0] - 1)
                    c = (b * PAGES + i) * NG * 64
                    pool.dma_start(X2[:, :, c:c + NG * 64],
                                   cmp_pages[bass.ds(pg, 1)].rearrange("o p v n -> (o p) v n")).then_inc(cmp_in, 16)
            pool.wait_ge(kv_ready, 12)
            pool.dma_start(kv_out, kvT).then_inc(kv_stored, 16)
            pool.wait_ge(gtok_ready, 2)
            pool.dma_start(grow[:], gsam[0:NS, :]).then_inc(grow_in, 16)

        @block.scalar
        def _(act):
            nstep = [0]

            def settle(ins):
                nstep[0] += 1
                ins.then_inc(act_step, 1)
                act.wait_ge(act_step, nstep[0])

            def std(ready, n, eps):
                act.wait_ge(ready, n)
                nc.scalar.activation(rstd[:, :], STAT[:, 0:NT], ACT.Sqrt, bias=const("eps")[:, eps:eps + 1]).then_inc(std_ready, 1)

            def squares(norm):
                for k in range(KC):
                    act.wait_ge(x_ready, 8 * norm + k - 7)
                    if k == 0 and norm:
                        act.wait_ge(stat_ready, norm)
                    nc.scalar.activation(sq[:, k, :], x[:, k, :], ACT.Square).then_inc(sq_ready, 1)
                std(stat_ready, norm + 1, 0)

            act.wait_ge(setup_in, 64)
            act.wait_ge(x_in, 16)
            for k in range(KC):
                nc.scalar.activation(sq[:, k, :], x[:, k, :], ACT.Square).then_inc(sq_ready, 1)
            std(stat_ready, 1, 0)
            for c in range(KC):
                act.wait_ge(acc_done, c + 1)
                nc.scalar.activation(vT[:, c, :], B[c % 4][:, 0:NT], ACT.Gelu_apprx_tanh).then_inc(v_ready, 1)
            for c in range(KC):
                act.wait_ge(acc_done, KC + c + 1)
                nc.scalar.activation(uT[:, c, :], B[c % 4][:, 0:NT], ACT.Gelu_apprx_tanh).then_inc(u_ready, 1)
                if c < 4:
                    for k in (2 * c, 2 * c + 1):
                        act.wait_ge(ctr_ready, k + 1)
                        nc.scalar.activation(sq[:, k, :], vT[:, k, :], ACT.Square).then_inc(csq_ready, 1)
            std(var_stat, 1, 1)
            for i in range(6):
                if i % 2:
                    r = P if i < 4 else NS
                    act.wait_ge(vt_done, i + 1)
                    nc.scalar.copy(vtok[0:r, i // 2, 512:1024], T1[0:r, :]).then_inc(vt_ready, 1)
            squares(1)
            for f in range(FC):
                act.wait_ge(gate_done, f + 1)
                if f >= 2:
                    act.wait_ge(hF_ready, f - 1)
                nc.scalar.activation(sil[:, f % 2, :], B[2 * (f % 2)][:, 0:NT], ACT.Silu).then_inc(sil_ready, 1)
            squares(2)
            for c in range(12):
                act.wait_ge(kv_done, c + 1)
                nc.scalar.copy(kvT[:, c, :], B[c % 4][:, 0:NT]).then_inc(kv_ready, 1)
            act.wait_ge(q_zero, 1)
            for c in range(KC):
                half = 64 * ((c // 2) % 2)
                act.wait_ge(q_done, c + 1)
                nc.scalar.mul(Q[half:half + 64, 2 * c + 1, :], B[c % 4][64:128, 0:NT], HD ** -0.5).then_inc(q_odd, 1)
            act.wait_ge(gp_done, 1)
            nc.scalar.activation(gT[0:48, :], MISC[0:48, 0:NT], ACT.Sigmoid).then_inc(sig_ready, 1)
            for v in range(2):
                act.wait_ge(cmp_done, v + 1)
                if v:
                    act.wait_ge(pre_ready, 1)
                nc.scalar.copy(hidb[0:64, 0:512], B[0][64:128, :]).then_inc(bhalf_ready, 1)
                nc.scalar.copy(hidb[0:64, 512:578], B[1][64:128, 0:66]).then_inc(bhalf_ready, 1)
                act.wait_ge(pre_ready, v + 1)
                nc.scalar.activation(hid[0:64], hid[0:64], ACT.Gelu_apprx_tanh, bias=cbias[0:64, :]).then_inc(hid_ready, 1)
            act.wait_ge(ss_max, 1)
            W = PAST + NS
            for j, (a, z) in enumerate([(0, W), (W, 2 * W), (2 * W, 2 * W + NS * NCMP)]):
                i = nc.scalar.activation(Ss[:, a:z], Ss[:, a:z], ACT.Exp, bias=smx[:, j:j + 1], accum_out=ssm[:, j:j + 1])
            i.then_inc(ss_exp, 1)

            def exp_head(h):
                b = h % 3
                act.wait_ge(neg_max, h + 1)
                S = Sh[:, b, :]
                for j, (a, z) in enumerate([(0, 128), (414, 542), (128, 384), (542, 798), (384, 399), (399, 414)]):
                    i = nc.scalar.activation(S[:, a:z], S[:, a:z], ACT.Exp, bias=mx[:, b, j:j + 1],
                                             accum_out=sm[:, b, j:j + 1])
                i.then_inc(exps, 1)

            def head_out(h):
                act.wait_ge(o_done, h + 1)
                half = 64 * (h % 2)
                nc.scalar.copy(hA[half:half + 64, h // 2, 0:NP], (STAT, MISC)[h % 2][0:64, 0:NP]).then_inc(o_ready, 1)

            exp_head(0)
            exp_head(1)
            for h in range(NH):
                act.wait_ge(pt_done, 2 * h + 2)
                if h >= 2:
                    act.wait_ge(o_done, h - 1)
                nc.scalar.copy(PT[:, h % 2, 0, :], T0[:, :]).then_inc(pt_ready, 1)
                nc.scalar.copy(PT[:, h % 2, 1, :], T1[:, :]).then_inc(pt_ready, 1)
                if h + 2 < NH:
                    exp_head(h + 2)
                if h >= 1:
                    head_out(h - 1)
            head_out(NH - 1)
            squares(3)
            act.wait_ge(lT_done, 1)
            nc.scalar.copy(lgT[:, :], MISC[0:NE, 0:NT]).then_inc(lT_ready, 1)
            act.wait_ge(kv_stored, 16)
            for t in range(3):
                r = P if t < 2 else NS
                for half in range(2):
                    act.wait_ge(ht_done, 2 * t + half + 1)
                    nc.scalar.copy(htok[0:r, t, 512 * half:512 * half + 512], HT[2 * t + half][0:r, :]).then_inc(ht_ready, 1)
            act.wait_ge(rank_in, 1)
            nc.scalar.activation(sc[:, :, 4:5], sc[:, :, 3:4], ACT.Exp).then_inc(exp_ready, 1)
            act.wait_ge(blk_ready, 1)
            nblk = act.value_load(blkinfo[0:1, MAXB:MAXB + 1], min_val=1, max_val=MAXB)

            def gathered(t):
                for half, bank in enumerate((STAT, MISC)):
                    act.wait_ge(xg_done, 2 * t + half + 1)
                    nc.scalar.copy(xg_hi[:, 4 * half:4 * half + 4, :], bank[:, :].rearrange("p (k n) -> p k n", n=P))\
                        .then_inc(xg_hi_ready, 1)

            def rows_out(t):
                act.wait_ge(item_used, t * ITEMS + NSPLIT)
                act.wait_ge(comb_done, t * KC)
                nc.scalar.copy(yrow[:, 0:512], B[2][:, :]).then_inc(yrow_ready, 1)

            gathered(0)
            with act.Fori(0, nblk) as t:
                def round_item(i):
                    u = i // 2
                    if i % 2 == 0:
                        act.wait_ge(raw_in[u % NRAW], t * (16 * UNITS // NRAW) + 16 * (u // NRAW + 1))
                    act.wait_ge(item_used, t * ITEMS + i + 1)
                    nc.scalar.copy(w_hi[:, i % NSPLIT, :], raw[:, u % NRAW, ITEM * (i % 2):ITEM * (i % 2) + ITEM])\
                        .then_inc(hi_ready, 1)

                def transposed(f):
                    act.wait_ge(hmT_done, t * FT + f + 1)
                    if f >= 2:
                        act.wait_ge(item_used, t * ITEMS + NSPLIT + DOWN_END[f - 2])
                    nc.scalar.copy(hm_hi[:, f % 2, :, :], (T0, T1)[f % 2][:, 0:256].rearrange("p (k n) -> p k n", n=P))\
                        .then_inc(hmT_hi, 1)

                n = 0
                for _ in range(4):
                    round_item(n)
                    n += 1
                rows_out(t)
                for f in range(FT):
                    for _ in range(2 * (f >= 2) + 4 * (f + 1 < FT)):
                        round_item(n)
                        n += 1
                    act.wait_ge(item_used, t * ITEMS + NSPLIT + UP_END[f])
                    nc.scalar.activation(sg[:, f % 2, :], B[f % 2][:, 0:256], ACT.Silu).then_inc(sg_ready, 1)
                    if f:
                        transposed(f - 1)
                for _ in range(2):
                    round_item(n)
                    n += 1
                gathered(t + 1)
                transposed(FT - 1)
                for _ in range(2):
                    round_item(n)
                    n += 1
            rows_out(nblk)
            act.wait_ge(comb_added, nblk * KC + KC)
            for k in range(KC):
                nc.scalar.activation(sq_last[:, k, :], x[:, k, :], ACT.Square).then_inc(sq_ready, 1)
            std(stat_ready, 5, 0)

        @block.vector
        def _(dve):
            V = nc.vector
            nstep = [0]

            def settle(ins):
                nstep[0] += 1
                ins.then_inc(dve_step, 1)
                dve.wait_ge(dve_step, nstep[0])

            nstd = [0]

            def inv_std():
                nstd[0] += 1
                dve.wait_ge(std_ready, nstd[0])
                settle(V.reciprocal(rstd[:, :], rstd[:, :]))

            def normed(dst, weight):
                for k in range(KC):
                    V.scalar_tensor_tensor(dst[:, k, :], x[:, k, :], weight[:, k:k + 1], rstd[:, :], ALU.mult, ALU.mult)\
                        .then_inc(h_ready, 1)

            dve.wait_ge(setup_in, 64)
            dve.wait_ge(x_in, 16)
            inv_std()
            normed(hA, par("mix0"))
            upto = const("upto").unsqueeze(1).to_broadcast([P, 8, P])
            V.tensor_tensor(wsT[:], par("wst").rearrange("p (g t) -> p g t", g=8), upto, ALU.mult).then_inc(ws_ready, 1)
            V.tensor_tensor(dg[0:NS], ident[0:NS, 0:NS].unsqueeze(1).to_broadcast([NS, 8, NS]),
                            par("w00")[0:NS, :].unsqueeze(2).to_broadcast([NS, 8, NS]), ALU.mult).then_inc(ws_ready, 1)
            dve.wait_ge(mu_stat, 1)
            settle(V.tensor_copy(mu[:, :], STAT[:, 0:NT]))
            for k in range(KC):
                V.tensor_tensor(vT[:, k, :], vT[:, k, :], mu[:, :], ALU.subtract).then_inc(ctr_ready, 1)
            inv_std()
            for k in range(KC):
                V.scalar_tensor_tensor(vT[:, k, :], vT[:, k, :], par("lng")[:, k:k + 1], rstd[:, :], ALU.mult, ALU.mult)\
                    .then_inc(dve_step, 1)
                nstep[0] += 1
            dve.wait_ge(dve_step, nstep[0])
            for k in range(KC):
                V.tensor_scalar(vT[:, k, :], vT[:, k, :], par("lnb")[:, k:k + 1], None, ALU.add).then_inc(vn_ready, 1)
            for i in range(0, 6, 2):
                r = P if i < 4 else NS
                dve.wait_ge(vt_done, i + 1)
                V.tensor_copy(vtok[0:r, i // 2, 0:512], T0[0:r, :]).then_inc(vt_ready, 1)
            for g in range(8):
                dve.wait_ge(mix_done, g + 1)
                dve.wait_ge(u_ready, g + 1)
                V.tensor_tensor(hB[:, g, :], uT[:, g, :], B[g % 4][:, 0:NT], ALU.mult).then_inc(gated, 1)
            for c in range(KC):
                dve.wait_ge(ao_done, c + 1)
                V.tensor_tensor(x[:, c, :], x[:, c, :], B[c % 4][:, 0:NT], ALU.add).then_inc(x_ready, 1)
            inv_std()
            normed(hA, par("ffn0"))
            dve.wait_ge(v_stored, 16)
            for f in range(FC):
                dve.wait_ge(up_done, f + 1)
                dve.wait_ge(sil_ready, f + 1)
                V.tensor_tensor(hF[:, f, :], sil[:, f % 2, :], B[2 * (f % 2) + 1][:, 0:NT], ALU.mult).then_inc(hF_ready, 1)
            for c in range(KC):
                dve.wait_ge(down_done, c + 1)
                V.tensor_tensor(x[:, c, :], x[:, c, :], B[c % 4][:, 0:NT], ALU.add).then_inc(x_ready, 1)
            V.memset(Q[:], 0.0).then_inc(q_zero, 1)
            V.memset(Qz[:], 0.0)
            V.memset(Qc[:], 0.0)
            inv_std()
            normed(hA, par("kvn"))
            normed(hB, par("mix1"))
            for v in range(2):
                for g in range(NG):
                    c = 2 * v + g // 2
                    dve.wait_ge(kv_ready, c + 1)
                    for r in range(2):
                        src = kvT[64 * (g % 2):64 * (g % 2) + 64, c, r:NP:2]
                        o = NS * PAGES * NG * 64 + g * P
                        V.tensor_copy(X2[64 * r:64 * r + 64, v, o:o + P], src).then_inc(x2_ready, 1)
                o = NS * PAGES * NG * 64 + NG * P
                V.tensor_copy(X2[:, v, o:o + 16], par("pe")[:, 16 * v:16 * v + 16]).then_inc(x2_ready, 1)
            dve.wait_ge(q_zero, 1)
            for c in range(KC):
                half = 64 * ((c // 2) % 2)
                dve.wait_ge(q_done, c + 1)
                V.tensor_scalar(Q[half:half + 64, 2 * c, :], B[c % 4][0:64, 0:NT], HD ** -0.5, None, ALU.mult).then_inc(q_even, 1)
            dve.wait_ge(q_even, KC)
            dve.wait_ge(q_odd, KC)
            for gp in range(2):
                src = Q[:, 8 * gp:8 * gp + 8, NP:NT].rearrange("p h b -> p b h")
                qz = Qz[:, gp, :, :].rearrange("p b n -> p (b n)")
                for b in range(NS):
                    V.tensor_copy(Qz[:, gp, b, b * NH + 8 * gp:b * NH + 8 * gp + 8], src[:, b, :])
                V.tensor_copy(Qc[:, gp, :].rearrange("p (b h) -> p b h", h=NH)[:, :, 8 * gp:8 * gp + 8], src).then_inc(q_rows, 1)
            dve.wait_ge(gt_done, 1)
            V.tensor_copy(gtok[:, :, :], MISC[:, 0:96].rearrange("p (t n) -> p t n", n=48)).then_inc(gtok_ready, 1)
            V.tensor_copy(gsam[0:NS, :], MISC[0:NS, 96:144]).then_inc(gtok_ready, 1)
            for t in range(3):
                r = P if t < 2 else NS
                dve.wait_ge(vp_done, t + 1)
                dst = vtp[:, t, :, :] if t < 2 else vnew[0:NS]
                V.tensor_copy(dst, (T0, T1)[t % 2][0:r, :].rearrange("p (a n) -> p a n", a=2)).then_inc(vp_ready, 1)
            for v in range(2):
                dve.wait_ge(bhalf_ready, 2 * v + 2)
                if v:
                    dve.wait_ge(cmp2_done, 1)
                A0 = B[0][0:64, :].rearrange("p (b i g s) -> p b i g s", b=NS, i=PAGES, g=NG)
                H0 = hidb[0:64, 0:512].rearrange("p (b i g s) -> p b i g s", b=NS, i=PAGES, g=NG)
                out = hid[0:64, 0:32, :].rearrange("p (g b) n -> p b g n", g=NG)
                V.tensor_tensor(out[:, :, :, 0:7], A0[:, :, 0, :, 0:7], H0[:, :, 0, :, 1:8], ALU.add)
                V.tensor_tensor(out[:, :, :, 7:8], A0[:, :, 0, :, 7:8], H0[:, :, 1, :, 0:1], ALU.add)
                V.tensor_tensor(out[:, :, :, 8:15], A0[:, :, 1, :, 0:7], H0[:, :, 1, :, 1:8], ALU.add)
                A1 = B[1][0:64, 0:64].rearrange("p (g s) -> p g s", g=NG)
                H1 = hidb[0:64, 512:576].rearrange("p (g s) -> p g s", g=NG)
                V.tensor_tensor(hid[0:64, 32:36, :], A1[:, :, 0:15], H1[:, :, 1:16], ALU.add)
                V.tensor_tensor(cbias[0:64, :], B[1][0:64, 64:65], hidb[0:64, 577:578], ALU.add).then_inc(pre_ready, 1)
                dve.wait_ge(cmp2_done, v + 1)
                if v == 0:
                    V.tensor_copy(kcT[:], B[2][:, 0:270].rearrange("p (a n) -> p a n", n=NCMP)).then_inc(cmp2_ready, 1)
                else:
                    V.tensor_copy(vcs[0:NS * NCMP, :], B[2][0:NS * NCMP, 0:256])
                    V.tensor_copy(vcp[0:NCMP, :], B[3][0:NCMP, 0:256]).then_inc(cmp2_ready, 1)
            V.memset(T0[:, 384:512], 0.0).then_inc(t_zeroed, 1)
            V.memset(T1[:, 384:512], 0.0).then_inc(t_zeroed, 1)
            dist = const("dist")
            W = PAST + NS
            slope = const("negslope")
            dve.wait_ge(ss_done, 1)
            V.scalar_tensor_tensor(Ss[:, 0:W], const("sdist"), slope, B[0][:, 0:W], ALU.mult, ALU.add)
            V.scalar_tensor_tensor(Ss[:, W:2 * W], const("sdist"), slope, B[1][:, 0:W], ALU.mult, ALU.add)
            settle(V.scalar_tensor_tensor(Ss[:, 2 * W:2 * W + 120], const("scdist"), slope, B[2][:, 0:120], ALU.mult, ALU.add))
            parts = [(0, W), (W, 2 * W), (2 * W, 2 * W + NS * NCMP)]
            for j, (a, z) in enumerate(parts):
                i = V.tensor_reduce(smx[:, j:j + 1], Ss[:, a:z], AX_X, ALU.max)
            settle(i)
            V.tensor_scalar(smx[:, :], smx[:, :], -1.0, None, ALU.mult).then_inc(ss_max, 1)
            dve.wait_ge(ss_exp, 1)
            settle(V.reciprocal(ssm[:, :], ssm[:, :]))
            dve.wait_ge(grow_in, 16)
            V.tensor_tensor(swt[:, 0:2], ssm[:, 0:2], grow[:, 1:3], ALU.mult)
            settle(V.tensor_tensor(swt[:, 2:3], ssm[:, 2:3], grow[:, 0:1], ALU.mult))
            for j, (a, z) in enumerate(parts):
                i = V.tensor_scalar(Ss[:, a:z], Ss[:, a:z], swt[:, j:j + 1], None, ALU.mult)
            i.then_inc(sp_ready, 1)

            def by_two(h, a, w):
                return Sh[:, h % 3, 0:828].rearrange("p (n c) -> p n c", n=2)[:, :, a:a + w]

            def biased_max(h):
                b = h % 3
                S = Sh[:, b, :]
                dve.wait_ge(s_done, h + 1)
                if h >= 3:
                    dve.wait_ge(pt_done, 2 * h - 4)
                V.scalar_tensor_tensor(S[:, 0:414], dist, -SLOPE[h], B[2 * (h % 2)][:, 0:414], ALU.mult, ALU.add)
                V.scalar_tensor_tensor(S[:, 414:798], dist[:, 0:384], -SLOPE[h], B[2 * (h % 2) + 1][:, 0:384], ALU.mult, ALU.add)\
                    .then_inc(s_biased, 1)
                dve.wait_ge(s_biased, h + 1)
                V.tensor_reduce(mx[:, b, 0:2], by_two(h, 0, P), AX_X, ALU.max)
                V.tensor_reduce(mx[:, b, 2:4], by_two(h, P, NP), AX_X, ALU.max)
                settle(V.tensor_reduce(mx[:, b, 4:6], S[:, 384:414].rearrange("p (t n) -> p t n", n=NCMP), AX_X, ALU.max))
                V.tensor_scalar(mx[:, b, :], mx[:, b, :], -1.0, None, ALU.mult).then_inc(neg_max, 1)

            def scale(h):
                b = h % 3
                S = Sh[:, b, :]
                dve.wait_ge(exps, h + 1)
                settle(V.reciprocal(sm[:, b, :], sm[:, b, :]))
                g3 = gtok[:, :, 3 * h:3 * h + 3]
                dst = wt[:, b, :].rearrange("p (a t) -> p a t", a=3)
                V.tensor_tensor(dst[:, 0, :], sm[:, b, 4:6], g3[:, :, 0], ALU.mult)
                V.tensor_tensor(dst[:, 1, :], sm[:, b, 0:3:2], g3[:, :, 1], ALU.mult)
                settle(V.tensor_tensor(dst[:, 2, :], sm[:, b, 1:4:2], g3[:, :, 2], ALU.mult))
                cm = const("cmpmask")
                for t in range(2):
                    V.scalar_tensor_tensor(S[:, 384 + 15 * t:399 + 15 * t], S[:, 384 + 15 * t:399 + 15 * t],
                                           wt[:, b, t:t + 1], cm[:, 15 * t:15 * t + 15], ALU.mult, ALU.mult)
                for j, (a, z, w) in enumerate([(0, 128, 2), (128, 384, 3), (414, 542, 4), (542, 798, 5)]):
                    i = V.tensor_scalar(S[:, a:z], S[:, a:z], wt[:, b, w:w + 1], None, ALU.mult)
                i.then_inc(p_ready, 1)

            biased_max(0)
            biased_max(1)
            scale(0)
            for h in range(NH):
                if h + 2 < NH:
                    biased_max(h + 2)
                if h + 1 < NH:
                    scale(h + 1)
            dve.wait_ge(spt_done, 1)
            V.tensor_copy(PTs[:, 0:4, :], T0[:, :].rearrange("p (a n) -> p a n", n=P))
            V.tensor_copy(PTs[0:NS, 4:6, :], T1[0:NS, 0:256].rearrange("p (a n) -> p a n", n=P))
            V.tensor_copy(PTs[0:NS * NCMP, 6, :], T1[0:NS * NCMP, 256:384]).then_inc(spt_ready, 1)
            dve.wait_ge(so_done, 1)
            for g2 in range(2):
                for odd in range(2):
                    src = B[3][64 * g2:64 * g2 + 64, 0:256].rearrange("p (c b h) -> p c b h", c=2, h=NH)
                    dst = hA[64 * odd:64 * odd + 64, :, NP:NT].rearrange("p (c g i) b -> p c g i b", c=2, g=2)
                    for c in range(2):
                        h0 = 8 * c + 4 * g2 + odd
                        i = V.tensor_copy(dst[:, c, g2, :, :], src[:, c, :, h0:h0 + 3:2].rearrange("p b i -> p i b"))
            i.then_inc(so_ready, 1)
            for c in range(KC):
                dve.wait_ge(bo_done, c + 1)
                V.tensor_tensor(x[:, c, :], x[:, c, :], B[c % 4][:, 0:NT], ALU.add).then_inc(x_ready, 1)
            inv_std()
            normed(hB, late("ffn1"))

            dve.wait_ge(kv_stored, 16)
            L = lg
            def col(i, t=None):
                return L[:, :, 8 * i:8 * i + 8] if t is None else L[:, t, 8 * i:8 * i + 8]

            def wide(ap):
                return ap.to_broadcast([P, 3, 8])

            down8 = const("down8").unsqueeze(1).to_broadcast([P, 3, 8])
            V.memset(lg[:], 0.0)
            settle(V.memset(sc[:], 0.0))
            dve.wait_ge(route_done, 1)
            V.tensor_copy(col(0)[:, 0:2, :], MISC[:, 0:16].rearrange("p (t n) -> p t n", n=8))
            settle(V.tensor_copy(col(0, 2)[0:NS, :], MISC[0:NS, 16:24]))

            def best(src, dst, m):
                settle(V.tensor_reduce(sc[:, :, m:m + 1], src, AX_X, ALU.max))
                settle(V.tensor_tensor(col(1), src, wide(sc[:, :, m:m + 1]), ALU.is_equal))
                settle(V.tensor_tensor(col(1), col(1), down8, ALU.mult))
                settle(V.tensor_reduce(sc[:, :, 2:3], col(1), AX_X, ALU.max))
                settle(V.tensor_tensor(dst, col(1), wide(sc[:, :, 2:3]), ALU.is_equal))

            best(col(0), col(2), 0)
            settle(V.scalar_tensor_tensor(col(3), col(2), -3e38, col(0), ALU.mult, ALU.add))
            best(col(3), col(4), 1)
            V.tensor_tensor(col(5), col(2), col(4), ALU.add)
            V.tensor_tensor(sc[:, :, 3:4], sc[:, :, 1:2], sc[:, :, 0:1], ALU.subtract).then_inc(rank_in, 1)
            dve.wait_ge(exp_ready, 1)
            settle(V.tensor_scalar(sc[:, :, 5:6], sc[:, :, 4:5], 1.0, None, ALU.add))
            settle(V.reciprocal(sc[:, :, 6:7], sc[:, :, 5:6]))
            V.tensor_tensor(sc[:, :, 7:8], sc[:, :, 4:5], sc[:, :, 6:7], ALU.mult)
            dve.wait_ge(rank_done, 1)
            counts = MISC[:, 48:56]
            V.tensor_scalar(cnt[:, 0:1], counts[:, 0:1], -1.0, None, ALU.is_gt)
            settle(V.tensor_scalar(cnt[:, 1:8], counts[:, 1:8], 0.0, None, ALU.is_gt))
            settle(V.scalar_tensor_tensor(cnt[:, 0:8], counts, float(ROWS), cnt[:, 0:8], ALU.is_gt, ALU.add))
            settle(V.scalar_tensor_tensor(cnt[:, 0:8], counts, float(2 * ROWS), cnt[:, 0:8], ALU.is_gt, ALU.add))
            settle(V.tensor_copy(cnt[:, 8:16], cnt[:, 0:8]))
            a, z = 8, 16
            for s in (1, 2, 4):
                V.tensor_copy(cnt[:, z:z + s], cnt[:, a:a + s])
                settle(V.tensor_tensor(cnt[:, z + s:z + 8], cnt[:, a + s:a + 8], cnt[:, a:a + 8 - s], ALU.add))
                a, z = z, z + 8
            ends_ = cnt[:, a:a + 8]
            settle(V.tensor_tensor(cnt[:, 48:56], ends_, cnt[:, 0:8], ALU.subtract))
            settle(V.tensor_scalar(cnt[:, 48:56], cnt[:, 48:56], float(ROWS), None, ALU.mult))
            V.tensor_tensor(col(6)[:, 0:2, :], MISC[:, 24:40].rearrange("p (t n) -> p t n", n=8),
                            cnt[:, 48:56].unsqueeze(1).to_broadcast([P, 2, 8]), ALU.add)
            settle(V.tensor_tensor(col(6, 2)[0:NS, :], MISC[0:NS, 40:48], cnt[0:NS, 48:56], ALU.add))
            for m in range(2):
                settle(V.tensor_tensor(col(7), col(2 + 2 * m), col(6), ALU.mult))
                settle(V.tensor_reduce(sc[:, :, 8 + m:9 + m], col(7), AX_X, ALU.add))
            settle(V.tensor_tensor(bcmp[0:1, :].rearrange("p (t e) -> p t e", e=NE),
                                   ends_[0:1, :].unsqueeze(1).to_broadcast([1, MAXB, NE]),
                                   const("blk")[0:1, :].rearrange("p (t e) -> p t e", e=NE), ALU.is_le))
            settle(V.tensor_reduce(bout[0:1, 0:MAXB], bcmp[0:1, :].rearrange("p (t e) -> p t e", e=NE), AX_X, ALU.add))
            settle(V.tensor_scalar(bout[0:1, 0:MAXB], bout[0:1, 0:MAXB], float(NE - 1), None, ALU.min))
            V.tensor_copy(blkinfo[0:1, MAXB:MAXB + 1], ends_[0:1, 7:8])
            V.tensor_copy(blkinfo[0:1, 0:MAXB], bout[0:1, 0:MAXB]).then_inc(blk_ready, 1)

            def selections():
                for t in range(3):
                    r = P if t < 2 else NS
                    iota = const("iota")[0:r, :]
                    d0, d1 = sc[0:r, t, 8:9], sc[0:r, t, 9:10]
                    g0, g1 = sc[0:r, t, 6:7], sc[0:r, t, 7:8]
                    V.tensor_scalar(Gm[0:r, t, :], iota, d0, None, ALU.is_equal).then_inc(dve_sel, 1)
                    V.tensor_scalar(Gw[0:r, t, :], iota, d0, g0, ALU.is_equal, ALU.mult).then_inc(dve_sel, 1)
                    V.tensor_scalar(Gt[0:r, :], iota, d1, g1, ALU.is_equal, ALU.mult).then_inc(dve_sel, 1)
                    dve.wait_ge(dve_sel, selbase[0] + 4 * t + 3)
                    V.scalar_tensor_tensor(Gm[0:r, t, :], iota, d1, Gm[0:r, t, :], ALU.is_equal, ALU.add)
                    V.tensor_tensor(Gw[0:r, t, :], Gw[0:r, t, :], Gt[0:r, :], ALU.add).then_inc(dve_sel, 1)
                    dve.wait_ge(dve_sel, selbase[0] + 4 * t + 4)
                V.tensor_scalar(sc[:, :, 8:10], sc[:, :, 8:10], -float(ROWS), None, ALU.add).then_inc(sel_ready, 1)

            def gathered(t):
                for half, bank in enumerate((STAT, MISC)):
                    dve.wait_ge(xg_hi_ready, 2 * t + half + 1)
                    V.tensor_tensor(xg_lo[:, 4 * half:4 * half + 4, :], bank[:, :].rearrange("p (k n) -> p k n", n=P),
                                    xg_hi[:, 4 * half:4 * half + 4, :].bitcast(F32), ALU.subtract).then_inc(xg_lo_ready, 1)

            def rows_out(t):
                dve.wait_ge(item_used, t * ITEMS + NSPLIT)
                dve.wait_ge(comb_done, t * KC)
                V.tensor_copy(yrow[:, 512:1024], B[3][:, :]).then_inc(yrow_ready, 1)

            def add_combined(t, c):
                dve.wait_ge(comb_done, t * KC + c + 1)
                V.tensor_tensor(x[:, c, :], x[:, c, :], (STAT, MISC)[c % 2][:, 0:NT], ALU.add).then_inc(comb_added, 1)

            V.memset(GwT[:], 0.0).then_inc(gwT_ready, 1)
            selbase = [0]
            selections()
            dve.wait_ge(sel_ready, 1)
            nblk = dve.value_load(blkinfo[0:1, MAXB:MAXB + 1], min_val=1, max_val=MAXB)
            gathered(0)
            with dve.Fori(0, nblk) as t:
                def rest_item(i):
                    dve.wait_ge(hi_ready, t * ITEMS + i + 1)
                    V.tensor_tensor(w_lo[:, i % NSPLIT, :], raw[:, (i // 2) % NRAW, ITEM * (i % 2):ITEM * (i % 2) + ITEM],
                                    w_hi[:, i % NSPLIT, :].bitcast(F32), ALU.subtract).then_inc(lo_ready, 1)

                def rest_hidden(f):
                    dve.wait_ge(hmT_hi, t * FT + f + 1)
                    V.tensor_tensor(hm_lo[:, f % 2, :, :], (T0, T1)[f % 2][:, 0:256].rearrange("p (k n) -> p k n", n=P),
                                    hm_hi[:, f % 2, :, :].bitcast(F32), ALU.subtract).then_inc(hmT_lo, 1)

                n = 0
                for _ in range(4):
                    rest_item(n)
                    n += 1
                rows_out(t)
                for f in range(FT):
                    for _ in range(2 * (f >= 2) + 4 * (f + 1 < FT)):
                        rest_item(n)
                        n += 1
                    dve.wait_ge(sg_ready, t * FT + f + 1)
                    if f >= 2:
                        dve.wait_ge(hmT_done, t * FT + f - 1)
                    V.tensor_tensor(hm[:, f % 2, :], sg[:, f % 2, :], B[f % 2][:, 256:512], ALU.mult).then_inc(hm_ready, 1)
                    if f:
                        rest_hidden(f - 1)
                    if f < 4:
                        for c in (2 * f, 2 * f + 1):
                            add_combined(t, c)
                    if f == 4:
                        dve.wait_ge(gw_done, t + 1)
                        V.tensor_copy(GwT[:, :], MISC[:, 0:NT]).then_inc(gwT_ready, 1)
                    if f == 5:
                        selbase[0] = t * 12 + 12
                        selections()
                        dve.wait_ge(sel_ready, t + 2)
                for _ in range(2):
                    rest_item(n)
                    n += 1
                gathered(t + 1)
                rest_hidden(FT - 1)
                for _ in range(2):
                    rest_item(n)
                    n += 1
            rows_out(nblk)
            for c in range(KC):
                add_combined(nblk, c)
            inv_std()
            normed(hB, late("final"))

        @block.tensor
        def _(pe):
            T = nc.tensor
            mean = const("mean")

            def stat(k, src, bank=STAT):
                return T.matmul(bank[:, 0:NT], mean, src[:, k, :], start=(k == 0), stop=(k == KC - 1))

            def project(bank, w, j, act_in, m=P):
                for k in range(KC):
                    i = T.matmul(bank[0:m, 0:NT], w[:, k, j * P:j * P + m], act_in[:, k, :], start=(k == 0), stop=(k == KC - 1))
                return i

            def stat_after(norm, k):
                pe.wait_ge(sq_ready, 8 * norm + k + 1)
                i = stat(k, sq if norm < 4 else sq_last)
                if k == KC - 1:
                    i.then_inc(stat_ready, 1)

            pe.wait_ge(setup_in, 64)
            for k in range(KC):
                stat_after(0, k)
            for c in range(16):
                t = ("v0", "v1", "u0", "u1")[c // 4]
                if c % 4 == 0:
                    arrived(pe, t)
                if 4 <= c < 12:
                    pe.wait_ge(v_ready, c - 3)
                elif c >= 12:
                    pe.wait_ge(u_ready, c - 11)
                if c == 0:
                    pe.wait_ge(h_ready, 8)
                project(B[c % 4], wtile(t), c % 4, hA).then_inc(acc_done, 1)
                if c == 8:
                    pe.wait_ge(v_ready, 8)
                    for k in range(KC):
                        i = stat(k, vT)
                    i.then_inc(mu_stat, 1)
                if c == 13:
                    pe.wait_ge(csq_ready, 8)
                    for k in range(KC):
                        i = stat(k, sq)
                    i.then_inc(var_stat, 1)
            pe.wait_ge(vn_ready, 8)
            for t, (a, z) in enumerate([(0, P), (P, NP), (NP, NT)]):
                if t:
                    pe.wait_ge(vt_ready, 2 * t)
                for half, bank in ((0, T0), (1, T1)):
                    for k in range(4):
                        i = T.transpose(bank[0:z - a, k * P:(k + 1) * P], vT[:, 4 * half + k, a:z], ident)
                    i.then_inc(vt_done, 1)
            pe.wait_ge(ws_ready, 2)
            pe.wait_ge(vt_ready, 6)
            for g in range(8):
                if g >= 4:
                    pe.wait_ge(gated, g - 3)
                else:
                    pe.wait_ge(u_ready, 4 + g + 1)
                bank, cols = B[g % 4], slice(g * P, (g + 1) * P)
                T.matmul(bank[:, 0:NT], ones_row[:, 0:P], b_s[:, g, :], start=True, stop=False)
                T.matmul(bank[:, 0:P], vtok[:, 0, cols], wsT[:, g, :], start=False, stop=False)
                T.matmul(bank[:, P:NP], vtok[:, 1, cols], wsT[:, g, :], start=False, stop=False)
                T.matmul(bank[:, NP:NT], vtok[0:NS, 2, cols], dg[0:NS, g, :], start=False, stop=True).then_inc(mix_done, 1)
            for c in range(KC):
                if c % 4 == 0:
                    arrived(pe, f"ao{c // 4}")
                if c == 0:
                    pe.wait_ge(gated, 8)
                if c >= 4:
                    pe.wait_ge(x_ready, c - 3)
                project(B[c % 4], wtile(f"ao{c // 4}"), c % 4, hB).then_inc(ao_done, 1)
                if c:
                    stat_after(1, c - 1)
            stat_after(1, 7)
            pe.wait_ge(h_ready, 16)
            for f in range(FC):
                if f % 2 == 0:
                    arrived(pe, f"gu{f // 2}")
                w = tile(f"gu{f // 2}").rearrange("p (k a n) -> p k a n", k=KC, a=2)
                if f >= 2:
                    pe.wait_ge(hF_ready, f - 1)
                project(B[2 * (f % 2)], w[:, :, 0, :], f % 2, hA).then_inc(gate_done, 1)
                project(B[2 * (f % 2) + 1], w[:, :, 1, :], f % 2, hA).then_inc(up_done, 1)
            for half in range(2):
                for part in range(3):
                    t = f"dn{3 * half + part}"
                    arrived(pe, t)
                    if part == 0 and half == 0:
                        pe.wait_ge(hF_ready, FC)
                    for j in range(4):
                        if part == 0 and half:
                            pe.wait_ge(x_ready, 8 + j + 1)
                        for k in range(8 * part, min(8 * part + 8, FC)):
                            i = T.matmul(B[j][:, 0:NT], wtile(t)[:, k - 8 * part, j * P:(j + 1) * P], hF[:, k, :],
                                         start=(k == 0), stop=(k == FC - 1))
                        if part == 2:
                            i.then_inc(down_done, 1)
                    if part < 2:
                        i.then_inc(down_part, 1)
                    if half == 1 and part == 0:
                        for k in range(4):
                            stat_after(2, k)
            for k in range(4, 8):
                stat_after(2, k)
            for c in range(12):
                if c % 4 == 0:
                    arrived(pe, f"kv{c // 4}")
                if c == 0:
                    pe.wait_ge(h_ready, 24)
                if c >= 4:
                    pe.wait_ge(kv_ready, c - 3)
                project(B[c % 4], wtile(f"kv{c // 4}"), c % 4, hA).then_inc(kv_done, 1)
            pe.wait_ge(h_ready, 32)
            for k in range(KC):
                T.matmul(MISC[0:48, 0:NT], w_gate[:, k, :], hB[:, k, :], start=(k == 0), stop=False)
            T.matmul(MISC[0:48, 0:NT], b_gate, ones_row, start=False, stop=True).then_inc(gp_done, 1)
            for c in range(KC):
                if c % 4 == 0:
                    arrived(pe, f"bi{c // 4}")
                if c < 4:
                    pe.wait_ge(kv_ready, 8 + c + 1)
                else:
                    pe.wait_ge(q_even, c - 3)
                    pe.wait_ge(q_odd, c - 3)
                project(B[c % 4], wtile(f"bi{c // 4}"), c % 4, hB).then_inc(q_done, 1)
            pe.wait_ge(sig_ready, 1)
            for t, (a, z) in enumerate([(0, P), (P, NP), (NP, NT)]):
                i = T.transpose(MISC[0:z - a, 48 * t:48 * t + 48], gT[0:48, a:z], ident[0:48, 0:48])
            i.then_inc(gt_done, 1)
            for t, (a, z) in enumerate([(0, P), (P, NP), (NP, NT)]):
                if t == 2:
                    pe.wait_ge(vp_ready, 1)
                for j, c in enumerate((6, 7, 10, 11)):
                    i = T.transpose((T0, T1)[t % 2][0:z - a, j * P:(j + 1) * P], kvT[:, c, a:z], ident)
                i.then_inc(vp_done, 1)
            NSEG = NS * PAGES * NG * 8
            pe.wait_ge(cmp_in, 16 * NS * PAGES)
            pe.wait_ge(q_even, KC)
            pe.wait_ge(q_odd, KC)
            for v in range(2):
                pe.wait_ge(x2_ready, 9 * v + 9)
                if v:
                    pe.wait_ge(pre_ready, 1)
                for m in range(8):
                    T.matmul(B[0][:, :], w1[:, v, m, :], X2[:, v, m:8 * NSEG:8], start=(m == 0), stop=(m == 7))
                    i = T.matmul(B[1][:, 0:66], w1[:, v, m, :], X2[:, v, 8 * NSEG + m:8 * NSEG + 528:8],
                                 start=(m == 0), stop=(m == 7))
                i.then_inc(cmp_done, 1)
                pe.wait_ge(hid_ready, v + 1)
                if v == 0:
                    hid_s = hid[0:64, 0:32, :].rearrange("p (c g b) n -> p c g (b n)", c=2, g=2)
                    for g2 in range(2):
                        T.matmul(B[2][:, 0:240], w2k[0:64, g2, :], hid_s[:, :, g2, :], start=(g2 == 0), stop=(g2 == 1))
                    for g2 in range(2):
                        i = T.matmul(B[2][:, 240:270], w2k[0:64, g2, :], hid[0:64, 32 + g2:36:2, :], start=(g2 == 0),
                                     stop=(g2 == 1))
                else:
                    pe.wait_ge(cmp2_ready, 1)
                    for g in range(NG):
                        cols = slice(64 * g, 64 * g + 64)
                        T.matmul(B[2][0:NS * NCMP, cols], hid[0:64, 8 * g:8 * g + 8, :].rearrange("p b n -> p (b n)"), par("w2v")[0:64, :], start=True, stop=True)
                        i = T.matmul(B[3][0:NCMP, cols], hid[0:64, 32 + g, :], par("w2v")[0:64, :], start=True, stop=True)
                i.then_inc(cmp2_done, 1)
            pe.wait_ge(q_rows, 2)
            pe.wait_ge(pre_ready, 2)
            for n, t in enumerate(("SK", "WK")):
                arrived(pe, t)
                keys = tile(t).rearrange("p (b c k) -> p b c k", b=NS, c=2)
                for j in range(16):
                    i = T.matmul(B[n][:, 0:PAST], Qz[:, j % 2, j // 2, :], keys[:, j // 2, j % 2, :], start=(j == 0), stop=(j == 15))
                i.then_inc(sk_used, 1)
                for c in range(2):
                    T.matmul(B[n][:, PAST:PAST + NS], Qc[:, c, :], kvT[:, 4 + 4 * n + c, NP:NT], start=(c == 0), stop=(c == 1))
            pe.wait_ge(cmp2_ready, 2)
            for c in range(2):
                i = T.matmul(B[2][:, 0:NS * NCMP], Qc[:, c, :], kcT[:, 8 * c:8 * c + 8, :], start=(c == 0), stop=(c == 1))
            i.then_inc(ss_done, 1)

            def scores(h):
                c, b = h // 8, h % 2
                if h == 0:
                    pe.wait_ge(ss_max, 1)
                if h >= 2:
                    pe.wait_ge(s_biased, h - 1)
                q0, q1 = Q[:, h, 0:P], Q[:, h, P:NP]
                slc, win = B[2 * b], B[2 * b + 1]
                T.matmul(slc[:, 0:P], q0, kvT[:, 4 + c, 0:P], start=True, stop=True)
                T.matmul(slc[:, 384:399], q0, kcT[:, 16 + c, :], start=True, stop=True)
                T.matmul(win[:, 0:P], q0, kvT[:, 8 + c, 0:P], start=True, stop=True)
                T.matmul(slc[:, P:384], q1, kvT[:, 4 + c, 0:NP], start=True, stop=True)
                T.matmul(slc[:, 399:414], q1, kcT[:, 16 + c, :], start=True, stop=True)
                T.matmul(win[:, P:384], q1, kvT[:, 8 + c, 0:NP], start=True, stop=True).then_inc(s_done, 1)

            def turn(h):
                S = Sh[:, h % 3, :]
                pe.wait_ge(p_ready, h + 1)
                if h:
                    pe.wait_ge(pt_ready, 2 * h)
                for n, bank in enumerate((T0, T1)):
                    for j in range(3):
                        T.transpose(bank[:, j * P:(j + 1) * P], S[:, 414 * n + j * P:414 * n + (j + 1) * P], ident)
                    T.transpose(bank[0:NCMP, 384:512], S[:, 384 + 15 * n:399 + 15 * n], ident).then_inc(pt_done, 1)

            def weigh(h):
                g, bank = h // 4, (STAT, MISC)[h % 2]
                cols = slice(HD * g, HD * g + HD)
                pe.wait_ge(pt_ready, 2 * h + 2)
                if h >= 2:
                    pe.wait_ge(o_ready, h - 1)
                for n in range(2):
                    T.matmul(bank[0:HD, 0:NP], vtp[:, 0, n, cols], PT[:, h % 2, n, 0:NP], start=(n == 0), stop=False)
                    T.matmul(bank[0:HD, P:NP], vtp[:, 1, n, cols], PT[:, h % 2, n, NP:384], start=False, stop=False)
                T.matmul(bank[0:HD, 0:P], vcp[0:NCMP, cols], PT[0:NCMP, h % 2, 0, 384:512], start=False, stop=False)
                T.matmul(bank[0:HD, P:NP], vcp[0:NCMP, cols], PT[0:NCMP, h % 2, 1, 384:512], start=False, stop=True).then_inc(o_done, 1)

            pe.wait_ge(vp_ready, 3)
            pe.wait_ge(t_zeroed, 2)
            pe.wait_ge(gtok_ready, 2)
            scores(0)
            scores(1)
            for h in range(NH):
                if h + 2 < NH:
                    scores(h + 2)
                turn(h)
                if h:
                    weigh(h - 1)
            weigh(NH - 1)
            W = PAST + NS
            pe.wait_ge(sp_ready, 1)
            pe.wait_ge(s_biased, NH)
            for j in range(4):
                a = W * (j // 2) + P * (j % 2)
                T.transpose(T0[:, j * P:(j + 1) * P], Ss[:, a:a + P], ident)
            T.transpose(T1[0:NS, 0:P], Ss[:, PAST:W], ident)
            T.transpose(T1[0:NS, P:2 * P], Ss[:, W + PAST:2 * W], ident)
            T.transpose(T1[0:NS * NCMP, 2 * P:3 * P], Ss[:, 2 * W:2 * W + NS * NCMP], ident).then_inc(spt_done, 1)
            pe.wait_ge(spt_ready, 1)
            arrived(pe, "SV")
            arrived(pe, "WV")
            vals = [tile(t).rearrange("p (b i v) -> p b i v", b=NS, i=PAGES) for t in ("SV", "WV")]
            for c in range(2):
                rows_, v = B[3][:, c * P:(c + 1) * P], slice(c * P, (c + 1) * P)
                T.matmul(rows_, vnew[0:NS, 0, v], PTs[0:NS, 4, :], start=True, stop=False)
                T.matmul(rows_, vnew[0:NS, 1, v], PTs[0:NS, 5, :], start=False, stop=False)
                for b in range(NS):
                    r = b * NH + 8 * c
                    for n in range(2):
                        for i_ in range(PAGES):
                            T.matmul(rows_[:, r:r + 8], vals[n][:, b, i_, v], PTs[:, 2 * n + i_, r:r + 8], start=False,
                                     stop=False, skip_group_check=True)
                i = T.matmul(rows_, vcs[0:NS * NCMP, v], PTs[0:NS * NCMP, 6, :], start=False, stop=True)
            i.then_inc(so_done, 1)
            for c in range(KC):
                if c % 4 == 0:
                    arrived(pe, f"bo{c // 4}")
                if c == 0:
                    pe.wait_ge(so_ready, 1)
                    pe.wait_ge(o_ready, NH)
                if c >= 4:
                    pe.wait_ge(x_ready, 16 + c - 3)
                project(B[c % 4], wtile(f"bo{c // 4}"), c % 4, hA).then_inc(bo_done, 1)
                if c:
                    stat_after(3, c - 1)
            stat_after(3, 7)
            pe.wait_ge(h_ready, 40)
            for k in range(KC):
                T.matmul(MISC[0:NE, 0:NT], w_router[:, k, :], hB[:, k, :], start=(k == 0), stop=False)
            T.matmul(MISC[0:NE, 0:NT], b_router, ones_row, start=False, stop=True).then_inc(lT_done, 1)
            spans = [(0, P), (P, NP), (NP, NT)]
            for t, (a, z) in enumerate(spans):
                for half in range(2):
                    for k in range(4):
                        i = T.transpose(HT[2 * t + half][0:z - a, k * P:(k + 1) * P], hB[:, 4 * half + k, a:z], ident)
                    i.then_inc(ht_done, 1)
                if t == 0:
                    pe.wait_ge(lT_ready, 1)
                    for u, (a_, z_) in enumerate(spans):
                        i = T.transpose(MISC[0:z_ - a_, 8 * u:8 * u + 8], lgT[:, a_:z_], ident[0:NE, 0:NE])
                    i.then_inc(route_done, 1)
            pe.wait_ge(rank_in, 1)
            both = [lg[0:z - a, t, 40:48] for t, (a, z) in enumerate(spans)]
            before, ones = const("before"), const("ones")
            for t, (a, z) in enumerate(spans):
                r = z - a
                out = MISC[0:r, 24 + 8 * t:32 + 8 * t]
                for u in range(t):
                    T.matmul(out, ones[:, 0:r], both[u], start=(u == 0), stop=False)
                T.matmul(out, before[0:r, 0:r], both[t], start=(t == 0), stop=True)
            for t, (a, z) in enumerate(spans):
                i = T.matmul(MISC[:, 48:56], ones[0:z - a, 0:P], both[t], start=(t == 0), stop=(t == 2))
            i.then_inc(rank_done, 1)
            pe.wait_ge(ht_ready, 6)
            pe.wait_ge(blk_ready, 1)
            nblk = pe.value_load(blkinfo[0:1, MAXB:MAXB + 1], min_val=1, max_val=MAXB)

            def gather(t):
                pe.wait_ge(sel_ready, t + 1)
                for k in range(KC):
                    out = (STAT, MISC)[k // 4][:, (k % 4) * P:(k % 4 + 1) * P]
                    for u, (a, z) in enumerate(spans):
                        i = T.matmul(out, htok[0:z - a, u, k * P:(k + 1) * P], Gm[0:z - a, u, :], start=(u == 0), stop=(u == 2))
                    if k % 4 == 3:
                        i.then_inc(xg_done, 1)

            def combine(t, c):
                if c == 0:
                    pe.wait_ge(yrow_ready, 2 * t + 2)
                    pe.wait_ge(gwT_ready, t + 1)
                if c >= 2:
                    pe.wait_ge(comb_added, t * KC + c - 1)
                T.matmul((STAT, MISC)[c % 2][:, 0:NT], yrow[:, c * P:(c + 1) * P], GwT[:, :], start=True, stop=True)\
                    .then_inc(comb_done, 1)

            gather(0)
            with pe.Fori(0, nblk) as t:

                def turn_hidden(f):
                    pe.wait_ge(hm_ready, t * FT + f + 1)
                    for j in range(2):
                        i = T.transpose((T0, T1)[f % 2][:, j * P:(j + 1) * P], hm[:, f % 2, j * P:(j + 1) * P], ident)
                    i.then_inc(hmT_done, 1)

                n = 0

                def item():
                    nonlocal n
                    pe.wait_ge(lo_ready, t * ITEMS + 2 * NRAW + n + 1)
                    n += 1
                    return (n - 1) % NSPLIT

                def product(out, lhs_hi, lhs_lo, cols, slot, first, last):
                    hi, lo = w_hi[:, slot, cols], w_lo[:, slot, cols]
                    T.matmul(out, lhs_hi, hi, start=first, stop=False)
                    T.matmul(out, lhs_hi, lo, start=False, stop=False)
                    return T.matmul(out, lhs_lo, hi, start=False, stop=last)

                def down(f):
                    pe.wait_ge(hmT_lo, t * FT + f + 1)
                    for j in range(2):
                        slot = item()
                        for half in range(2):
                            i = product(B[2 + half][:, :], hm_hi[:, f % 2, j, :], hm_lo[:, f % 2, j, :],
                                        slice(512 * half, 512 * half + 512), slot, f == 0 and j == 0, f == FT - 1 and j == 1)
                        i.then_inc(item_used, 1)

                for f in range(FT):
                    if f >= 2:
                        pe.wait_ge(hm_ready, t * FT + f - 1)
                    if f == 0:
                        pe.wait_ge(xg_lo_ready, 2 * t + 2)
                    for q in range(4):
                        slot = item()
                        for k in (2 * q, 2 * q + 1):
                            i = product(B[f % 2][:, :], xg_hi[:, k, :], xg_lo[:, k, :],
                                        slice(512 * (k % 2), 512 * (k % 2) + 512), slot, k == 0, k == KC - 1)
                        i.then_inc(item_used, 1)
                    if f < 4:
                        combine(t, 2 * f)
                        combine(t, 2 * f + 1)
                    if f == 4:
                        pe.wait_ge(comb_added, t * KC + KC)
                        for u, (a, z) in enumerate(spans):
                            i = T.transpose(MISC[:, a:z], Gw[0:z - a, u, :], ident[0:z - a, 0:z - a])
                        i.then_inc(gw_done, 1)
                    if f == FT - 1:
                        pe.wait_ge(gwT_ready, t + 2)
                        gather(t + 1)
                    if f >= 1:
                        turn_hidden(f - 1)
                    if f >= 2:
                        down(f - 2)
                turn_hidden(FT - 1)
                down(FT - 2)
                down(FT - 1)
            for c in range(KC):
                combine(nblk, c)
            for k in range(KC):
                stat_after(4, k)


def kernel(**inputs):
    import concourse.bacc as bacc
    from concourse.bass_utils import run_bass_kernel_spmd as run

    a = {k: np.asarray(v) for k, v in inputs.items()}

    def cat(*xs):
        return np.concatenate(xs, axis=-1)

    def chunks(w):
        return w.reshape(-1, P, w.shape[-1]).transpose(1, 0, 2)

    def vec(v):
        return v.reshape(KC, P).T

    def part(rows):
        return np.concatenate([rows, np.zeros((P - rows.shape[0],) + rows.shape[1:], np.float32)], axis=0)

    arrays = {}
    tokens = np.concatenate([a["x_prompt"][0], a["x_sample"][:, 0]], axis=0)
    arrays["x"] = chunks(np.ascontiguousarray(tokens.T))
    ain, aout = chunks(a["a_w_in"][0]), chunks(a["a_w_out"][0])
    fg, fu, fd = chunks(a["f_w_gate"][0]), chunks(a["f_w_up"][0]), chunks(a["f_w_down"][0])
    wkv, bin_, bout = chunks(a["w_kv"]), chunks(a["b_w_in"][0]), chunks(a["b_w_out"][0])
    tiles = [ain[:, :, 1024:1536], ain[:, :, 1536:2048], ain[:, :, 0:512], ain[:, :, 512:1024], aout[:, :, 0:512], aout[:, :, 512:1024]]
    tiles += [cat(fg[:, :, 256 * i:256 * i + 256], fu[:, :, 256 * i:256 * i + 256]) for i in range(FT)]
    for half in range(2):
        for i in range(3):
            d = fd[:, 8 * i:8 * i + 8, 512 * half:512 * half + 512]
            tiles.append(np.concatenate([d, np.zeros((P, 8 - d.shape[1], 512), np.float32)], axis=1))
    tiles += [wkv[:, :, 512 * i:512 * i + 512] for i in range(3)]
    tiles += [bin_[:, :, 0:512], bin_[:, :, 512:1024], bout[:, :, 0:512], bout[:, :, 512:1024]]
    arrays["wd"] = np.stack([t.reshape(P, SLOT) for t in tiles])
    mg, mu, md = a["m_w_gate"][0], a["m_w_up"][0], a["m_w_down"][0]
    moe = np.empty((NE, UNITS, P, UNIT), np.float32)
    for u, (f, kind) in enumerate(USE):
        if kind == "d":
            f -= 2
            moe[:, u] = md[:, 256 * f:256 * f + 256].reshape(NE, 2, P, DM).transpose(0, 2, 1, 3).reshape(NE, P, UNIT)
        else:
            k = 512 * (kind == "b")
            for w, o in ((mg, 0), (mu, 256)):
                moe[:, u].reshape(NE, P, 4, 512)[..., o:o + 256] = \
                    w[:, k:k + 512, 256 * f:256 * f + 256].reshape(NE, 4, P, 256).transpose(0, 2, 1, 3)
    arrays["moe"] = moe
    bw, w1_, w2_ = a["b_w_in"][0], a["cmp_w1"], a["cmp_w2"]
    zero = np.zeros((64, 64), np.float32)
    fields = {
        "mix0": vec(a["norm_mix"][0]), "mix1": vec(a["norm_mix"][1]), "ffn0": vec(a["norm_ffn"][0]),
        "lng": vec(a["a_ln_g"][0]), "lnb": vec(a["a_ln_b"][0]), "kvn": vec(a["kv_norm"]),
        "pe": a["cmp_pe"].reshape(32, P).T, "w00": np.broadcast_to(a["a_w_s"][0, :, 0, 0][None, :], (P, 8)),
        "gate": chunks(bw[:, 1024:]).reshape(P, -1),
        "w1": w1_.reshape(2, 2, 8, P, 64).transpose(3, 0, 2, 1, 4).reshape(P, -1),
        "w2k": part(np.concatenate([w2_[0], zero, zero, w2_[0]], axis=1)), "w2v": part(w2_[1]),
        "wst": a["a_w_s"][0].transpose(2, 0, 1).reshape(P, -1),
    }
    arrays["params"] = cat(*[fields[k] for k in PARAMS])
    arrays["late"] = cat(vec(a["norm_ffn"][1]), vec(a["norm_final"]), chunks(a["m_w_router"][0]).reshape(P, -1),
                         np.broadcast_to(a["m_b_router"], (P, NE)))
    bs = a["a_b_s"][0]
    bsx = cat(bs, bs, np.repeat(bs[:, 0:1], NS, axis=1)).reshape(1, -1)
    arrays["rows"] = cat(bsx, a["b_b_gate"].reshape(1, -1))
    arrays["consts"] = constants()
    cache = a["cache_kv"]
    n_phys = cache.shape[0]
    arrays["cmp_pages"] = cache[:, :, 0:2].reshape(n_phys, 64, 2, 2, NG, HD).transpose(0, 2, 5, 3, 4, 1).reshape(n_phys, P, 2, NG * 64)
    arrays["k_pages"] = cache[:, :, 2].reshape(n_phys, P, 2, P).transpose(0, 3, 2, 1)
    arrays["v_pages"] = cache[:, :, 3].reshape(n_phys, P, NG * HD)
    win = a["state_win_kv"]
    arrays["win_k"] = win[:, :, 0].reshape(NS, PAST, 2, P).transpose(3, 0, 2, 1).reshape(P, SLOT)
    arrays["win_v"] = win[:, :, 1].reshape(NS, PAGES, P, NG * HD).transpose(2, 0, 1, 3).reshape(P, SLOT)
    arrays["state_win"] = win.reshape(P, -1)
    arrays["page_table"] = a["page_table"].reshape(1, -1)

    nc = bacc.Bacc("TRN2", target_bir_lowering=False, num_devices=1)
    args = []
    for name in list(arrays):
        arrays[name] = np.ascontiguousarray(arrays[name])
        args.append(nc.dram_tensor(f"in_{name}", arrays[name].shape, mybir.dt.from_np(arrays[name].dtype), kind="ExternalInput").ap())
    outs = [("y", (P, KC, NT)), ("v", (P, KC, NT)), ("kv", (P, 12, NT)), ("past", (P, NS * PAST * 512 // P))]
    for name, shape in outs:
        args.append(nc.dram_tensor(f"out_{name}", shape, F32, kind="ExternalOutput").ap())
    build(nc, *args)
    r = run(nc, [{f"in_{k}": v for k, v in arrays.items()}], core_ids=[0]).results[0]
    y, v, kv, past = (np.asarray(r[f"out_{name}"]) for name, _ in outs)

    def tokens_of(z):
        return z.transpose(2, 1, 0).reshape(NT, -1)

    y, v, kv = tokens_of(y), tokens_of(v), tokens_of(kv)
    kv_rows, win_rows = kv[:, 0:1024].reshape(NT, 4, NG, HD), kv[:, 1024:1536].reshape(NT, 2, NG, HD)
    win_sample = np.concatenate([past.reshape(NS, PAST, 2, NG, HD), win_rows[NP:][:, None]], axis=1)
    return (y[None, 0:NP], y[NP:][:, None], kv_rows[None, 0:NP], kv_rows[NP:][:, None], win_rows[None, 0:NP], win_sample,
            v[None, None, P:NP], v[NP:][None, :, None])
```

```python
from contextlib import ExitStack

import numpy as np

import concourse.bass as bass
from concourse import mybir

F32 = mybir.dt.float32
I32 = mybir.dt.int32
F32R = mybir.dt.float32r
ALU = mybir.AluOpType
ACT = mybir.ActivationFunctionType
AX_X = mybir.AxisListType.X

P = 128
DM = 1024
KC = DM // P
NP = 256
NS = 8
NT = NP + NS
PAST = 256
HD = 64
NH = 16
NG = 4
FF = 2816
FC = FF // P
FT = FF // 256
NE = 8
ROWS = 128
MAXB = 12
NCMP = 15
CMP_LEN, CMP_STRIDE = 32, 16
RMS_EPS, LN_EPS = 1e-6, 1e-5
BIG = 1e30
SLOT = 4096
UNIT, ITEM = 2048, 1024
USE = [(f, kind) for f in range(FT + 2) for kind in "abd" if (f < FT if kind != "d" else f >= 2)]
UNITS = len(USE)
ITEMS = 2 * UNITS
UP_END = {f: 2 * u + 2 for u, (f, kind) in enumerate(USE) if kind == "b"}
DOWN_END = {f - 2: 2 * u + 2 for u, (f, kind) in enumerate(USE) if kind == "d"}
NRAW = 11
NSPLIT = 6
PAGES = 2
X2W = NS * PAGES * NG * HD + NG * NP // 2 + CMP_LEN // 2

SLOPE = [2.0 ** (-8.0 * (h + 1) / NH) for h in range(NH)]


def layout(widths):
    at, out = 0, {}
    for name, w in widths:
        out[name] = (at, at + w)
        at += w
    return out, at


CONSTS, NC_ = layout([("ident", P), ("mean", P), ("ones", NT), ("before", P), ("upto", P), ("dist", 414),
                      ("cmpmask", 30), ("sdist", PAST + NS), ("scdist", NS * NCMP), ("negslope", 1),
                      ("iota", P), ("down8", NE), ("blk", MAXB * NE), ("eps", 2)])
VECTORS, NVEC = layout([("mix0", 8), ("mix1", 8), ("ffn0", 8), ("lng", 8), ("lnb", 8), ("kvn", 8), ("w00", 8)])
PARAMS, NPAR = layout([("pe", 32), ("gate", 8 * 48), ("w1", 2048),
                       ("w2k", 256), ("w2v", 64), ("bgate", 48)])
LATE, NLATE = layout([("ffn1", 8), ("final", 8), ("router", 64), ("brouter", 8)])


def constants():
    c = np.zeros((P, NC_), np.float32)

    def put(name, v):
        a, b = CONSTS[name]
        c[:, a:b] = v

    p = np.arange(P)[:, None]
    f = np.arange(P)[None, :]
    put("ident", p == f)
    put("mean", 1.0 / DM)
    put("ones", 1.0)
    put("before", p < f)
    put("upto", p <= f)
    ends = np.arange(NCMP) * CMP_STRIDE + CMP_LEN - 1
    d = np.concatenate([p - f, p + P - np.arange(NP)[None, :], p - ends[None, :], p + P - ends[None, :]], axis=1)
    put("dist", np.where(d >= 0, d, BIG))
    put("cmpmask", d[:, 384:414] >= 0)
    own = (p // NH) == np.arange(NS)[None, :]
    put("sdist", np.concatenate([np.broadcast_to(PAST - np.arange(PAST)[None, :], (P, PAST)), np.where(own, 0.0, BIG)], axis=1))
    put("scdist", np.where(np.repeat(own, NCMP, axis=1), np.tile(PAST - ends, NS)[None, :], BIG))
    put("negslope", -np.array(SLOPE, np.float32)[np.arange(P) % NH][:, None])
    put("iota", f)
    put("down8", NE - np.arange(NE)[None, :])
    put("eps", np.array([[RMS_EPS, LN_EPS]]))
    put("blk", np.repeat(np.arange(MAXB), NE)[None, :])
    return c


TILES = (["v0", "v1", "u0", "u1", "ao0", "ao1"] + [f"gu{i}" for i in range(FT)]
         + [f"dn{i}" for i in range(6)] + ["kv0", "kv1", "kv2", "bi0", "bi1", "SK", "WK", "bo0", "bo1"])
WTILES = [t for t in TILES if t[1] not in "KV"]
INDEX = {t: n for n, t in enumerate(TILES)}
NSLOT = 2
DITEM = KC * P
NDS = 3
FIRST, NDENSE = {}, 0
for stage, items in (("vu", 16), ("ao", 8), ("gu", 2 * FC), ("dn", 24), ("kv", 12), ("q", 8)):
    FIRST[stage] = NDENSE
    NDENSE += items


def build(nc, xT, wd, moe, vectors, params, late_in, spatial, spatial_bias, consts, cmp_pages, k_pages, v_pages, win_k, win_v, state_win, page_table,
          y_out, v_out, kv_out, past_out):
    with ExitStack() as ctx:
        def sb(name, shape, dt=F32):
            return ctx.enter_context(nc.sbuf_tensor(name, shape, dt))

        def sem(name):
            return ctx.enter_context(nc.semaphore(name))

        C = sb("consts_sb", [P, NC_])
        LT = sb("late_sb", [P, NLATE])
        VE = sb("vectors_sb", [P, NVEC])
        x = sb("x", [P, KC, NT])
        hB = sb("hB", [P, KC, NT])
        rstd = sb("rstd", [P, NT])
        pages = sb("pages", [1, NS * PAGES], I32)
        blkinfo = sb("blkinfo", [1, 16], I32)

        dense_memory = ctx.enter_context(ExitStack())

        def sbd(name, shape, dt=F32):
            return dense_memory.enter_context(nc.sbuf_tensor(name, shape, dt))

        with ExitStack() as hidden_memory:
            hF_hi = hidden_memory.enter_context(nc.sbuf_tensor("hF_hi", [P, FC, NT], F32R))
            hF_lo = hidden_memory.enter_context(nc.sbuf_tensor("hF_lo", [P, FC, NT], F32R))
            sil = hidden_memory.enter_context(nc.sbuf_tensor("sil", [P, 2, NT], F32))
        ARENA = 19900
        arena = sbd("arena", [P, ARENA])
        PR = sbd("params_sb", [P, NPAR])
        with ExitStack() as normed_memory:
            hA_hi = normed_memory.enter_context(nc.sbuf_tensor("hA_hi", [P, KC, NT], F32R))
            hA_lo = normed_memory.enter_context(nc.sbuf_tensor("hA_lo", [P, KC, NT], F32R))
        X2v = sbd("X2v", [P, X2W])
        with ExitStack() as query_memory:
            hC_hi = query_memory.enter_context(nc.sbuf_tensor("hC_hi", [P, KC, NT], F32R))
            hC_lo = query_memory.enter_context(nc.sbuf_tensor("hC_lo", [P, KC, NT], F32R))
        slc_v = sbd("slc_v", [P, 2 * KC * NT])
        ring = sbd("ring", [P, NSLOT, SLOT])
        with ExitStack() as split_memory:
            d_hi = split_memory.enter_context(nc.sbuf_tensor("d_hi", [P, NDS, DITEM], F32R))
            d_lo = split_memory.enter_context(nc.sbuf_tensor("d_lo", [P, NDS, DITEM], F32R))
        win_v_past = sbd("win_v_past", [P, SLOT])
        sq3 = win_v_past[:, 0:KC * NT].rearrange("p (k t) -> p k t", t=NT)
        top = [0]

        def carve(*shape):
            n = int(np.prod(shape))
            v = arena[:, top[0]:top[0] + n]
            top[0] += n
            assert top[0] <= ARENA, top[0]
            if len(shape) == 2:
                v = v.rearrange("p (a b) -> p a b", b=shape[1])
            if len(shape) == 3:
                v = v.rearrange("p (a b c) -> p a b c", b=shape[1], c=shape[2])
            return v

        uT = carve(KC, NT)
        vT = carve(KC, NT)
        vtok = carve(3, DM)
        wsT = carve(8, P)
        dg = carve(8, NS)
        mu = carve(NT)
        w_s = carve(8, P)
        b_s = carve(8, NT)[0:1]
        top[0] = 0
        kvT = carve(12, NT)
        Q = carve(NH, NT)
        qz_at = top[0]
        Qz = carve(2, NS, P)
        orow = arena[0:NH, qz_at:qz_at + NS * 2 * P]
        Qc = carve(2, P)
        vtp = carve(2, 2, 2 * P)
        vnew = carve(2, 2 * P)
        gT = carve(NT)
        gtok = carve(2, 48)
        gsam = carve(48)
        grow = carve(3)
        hidb = carve(580)
        hid = carve(36, NCMP)
        cbias = carve(1)
        kcT = carve(18, NCMP)
        vcs = carve(2 * P)
        vcp = carve(2 * P)
        x2_at = top[0]
        X2 = [carve(X2W), X2v[:]]
        top[0] = x2_at
        Sh = carve(3, 828)
        mx = carve(3, 6)
        sm = carve(3, 6)
        wt = carve(3, 6)
        PT = carve(2, 2, 512)
        Ss = carve(2 * (PAST + NS) + NS * NCMP)
        smx, ssm, swt = carve(3), carve(3), carve(3)
        PTs = carve(7, P)
        dense_memory.close()
        raw = sb("raw", [P, NRAW, UNIT])
        w_hi = sb("w_hi", [P, NSPLIT, ITEM], F32R)
        w_lo = sb("w_lo", [P, NSPLIT, ITEM], F32R)
        xg_hi = sb("xg_hi", [P, KC, P], F32R)
        xg_lo = sb("xg_lo", [P, KC, P], F32R)
        hm_hi = sb("hm_hi", [P, 2, 2, P], F32R)
        hm_lo = sb("hm_lo", [P, 2, 2, P], F32R)
        htok = sb("htok", [P, 3, DM])
        yrow = sb("yrow", [P, DM])
        Gm = sb("Gm", [P, 3, P])
        Gw = sb("Gw", [P, 3, P])
        Gt = sb("Gt", [P, 3, P])
        GwT = sb("GwT", [P, NT])
        sg = sb("sg", [P, 2, 256])
        hm = sb("hm", [P, 2, 256])
        lgT = sb("lgT", [NE, NT])
        lg = sb("lg", [P, 3, 64])
        sc = sb("sc", [P, 3, 16])
        cnt = sb("cnt", [P, 64])
        bcmp = sb("bcmp", [1, MAXB * NE])
        bout = sb("bout", [1, 16])
        sq_last = htok[:].rearrange("p a b -> p (a b)")[:, 0:KC * NT].rearrange("p (k t) -> p k t", t=NT)

        def const(name):
            a, b = CONSTS[name]
            return C[:, a:b]

        def par(name):
            a, b = PARAMS[name]
            return PR[:, a:b]

        def vector(name):
            a, b = VECTORS[name]
            return VE[:, a:b]

        def late(name):
            a, b = LATE[name]
            return LT[:, a:b]

        ident = const("ident")
        w1 = par("w1").rearrange("p (v m e) -> p v m e", v=2, e=P)
        w_gate = par("gate").rearrange("p (k n) -> p k n", k=KC)
        w_router = late("router").rearrange("p (k n) -> p k n", k=KC)
        w2k = par("w2k").rearrange("p (a n) -> p a n", a=2)
        b_gate = par("bgate")[0:1, :]
        b_router = late("brouter")[0:1, :]
        ones_row = C[0:1, CONSTS["ones"][0]:CONSTS["ones"][1]]

        B = [ctx.enter_context(nc.psum_tensor(f"bank{i}", [P, 512], F32)) for i in range(8)]
        STAT, T0, T1, MISC = B[4], B[5], B[6], B[7]
        HT = [B[0], B[1], B[2], B[3], T0, T1]

        slot_in = [sem(f"slot_in{i}") for i in range(NSLOT)]
        setup_in = sem("setup_in")
        spatial_in, params_in = sem("spatial_in"), sem("params_in")
        x_in = sem("x_in")
        pages_in = sem("pages_in")
        past_v_in = sem("past_v_in")
        cmp_in = [sem("cmp_k_in"), sem("cmp_v_in")]
        x_ready = sem("x_ready")
        sq_ready = sem("sq_ready")
        std_ready = sem("std_ready")
        stat_ready = sem("stat_ready")
        norm_ready = sem("norm_ready")
        h_hi_ready = sem("h_hi_ready")
        h_ready = sem("h_ready")
        d_hi_ready = sem("d_hi_ready")
        d_lo_ready = sem("d_lo_ready")
        dense_done = sem("dense_done")
        dve_step = sem("dve_step")
        act_step = sem("act_step")
        v_ready, u_ready = sem("v_ready"), sem("u_ready")
        mu_stat, ctr_ready, csq_ready, var_stat, vn_ready = (sem("mu_stat"), sem("ctr_ready"), sem("csq_ready"),
                                                            sem("var_stat"), sem("vn_ready"))
        vt_done, vt_ready, ws_ready = sem("vt_done"), sem("vt_ready"), sem("ws_ready")
        mix_done, gated = sem("mix_done"), sem("gated")
        gated_hi, gated_lo = sem("gated_hi"), sem("gated_lo")
        sil_ready, hF_ready, hF_hi_ready, hF_lo_ready = sem("sil_ready"), sem("hF_ready"), sem("hF_hi_ready"), sem("hF_lo_ready")
        kv_ready = sem("kv_ready")
        q_even, q_odd = sem("q_even"), sem("q_odd")
        gp_done, sig_ready, gt_done, gtok_ready, grow_in = (sem("gp_done"), sem("sig_ready"), sem("gt_done"),
                                                            sem("gtok_ready"), sem("grow_in"))
        vp_done, vp_ready = sem("vp_done"), sem("vp_ready")
        q_zero, q_rows = sem("q_zero"), sem("q_rows")
        x2_ready = sem("x2_ready")
        cmp_done, bhalf_ready, pre_ready, hid_ready, cmp2_done, cmp2_ready = (
            sem("cmp_done"), sem("bhalf_ready"), sem("pre_ready"), sem("hid_ready"), sem("cmp2_done"), sem("cmp2_ready"))
        s_done, s_biased, neg_max, exps, p_ready, pt_done, pt_ready, o_done, o_ready = (
            sem("s_done"), sem("s_biased"), sem("neg_max"), sem("exps"), sem("p_ready"), sem("pt_done"),
            sem("pt_ready"), sem("o_done"), sem("o_ready"))
        ss_done, ss_max, ss_exp, sp_ready, spt_done, spt_ready, so_done, so_ready, orow_done, orow_ready = (
            sem("ss_done"), sem("ss_max"), sem("ss_exp"), sem("sp_ready"), sem("spt_done"), sem("spt_ready"),
            sem("so_done"), sem("so_ready"), sem("orow_done"), sem("orow_ready"))
        bo_done = sem("bo_done")
        sk_used, t_zeroed, lT_done, lT_ready = sem("sk_used"), sem("t_zeroed"), sem("lT_done"), sem("lT_ready")
        route_done, ht_done, ht_ready, rank_in, rank_done, blk_ready, exp_ready = (
            sem("route_done"), sem("ht_done"), sem("ht_ready"), sem("rank_in"), sem("rank_done"), sem("blk_ready"), sem("exp_ready"))
        raw_in = [sem(f"raw_in{i}") for i in range(NRAW)]
        hi_ready, lo_ready, item_used = sem("hi_ready"), sem("lo_ready"), sem("item_used")
        dve_sel, gw_sel = sem("dve_sel"), sem("gw_sel")
        sel_ready, gw_done, gwT_ready, xg_done, xg_hi_ready, xg_lo_ready = (sem("sel_ready"), sem("gw_done"), sem("gwT_ready"),
                                                            sem("xg_done"), sem("xg_hi_ready"), sem("xg_lo_ready"))
        sg_ready, hm_ready, hmT_done, hmT_hi, hmT_lo, yrow_ready = (
            sem("sg_ready"), sem("hm_ready"), sem("hmT_done"), sem("hmT_hi"), sem("hmT_lo"),
            sem("yrow_ready"))
        comb_done, comb_added = sem("comb_done"), sem("comb_added")
        v_stored, kv_stored, past_stored, y_stored = sem("v_stored"), sem("kv_stored"), sem("past_stored"), sem("y_stored")

        used = {t: (d_lo_ready, 4 * n + 4) for n, t in enumerate(TILES[:NDENSE // 4])}
        used |= {"SK": (sk_used, 1), "WK": (sk_used, 2)}

        landed, filled = {}, [0] * NSLOT
        for n, t in enumerate(TILES):
            filled[n % NSLOT] += 16 * (NS * PAGES if t == "SK" else 1)
            landed[t] = filled[n % NSLOT]

        def arrived(eng, t):
            eng.wait_ge(slot_in[INDEX[t] % NSLOT], landed[t])

        def tile(t):
            return ring[:, INDEX[t] % NSLOT, :]

        def items(t):
            return tile(t).rearrange("p (j k n) -> p j k n", j=4, k=KC)

        def raw_item(n):
            return ring[:, (n // 4) % NSLOT, DITEM * (n % 4):DITEM * (n % 4 + 1)]

        def projected(eng, stage, c):
            eng.wait_ge(dense_done, FIRST[stage] + c + 1)

        block = ctx.enter_context(nc.Block())

        @block.sync
        def _(sp):
            sp.dma_start(x[:], xT).then_inc(x_in, 16)
            sp.dma_start(VE[:], vectors).then_inc(setup_in, 16)
            sp.dma_start(C[:], consts).then_inc(setup_in, 16)
            wn = 0

            def page(b, i):
                return sp.value_load(pages[0:1, b * PAGES + i:b * PAGES + i + 1], min_val=0, max_val=k_pages.shape[0] - 1)

            for n, t in enumerate(TILES):
                if n >= NSLOT:
                    sp.wait_ge(*used[TILES[n - NSLOT]])
                done = slot_in[n % NSLOT]
                if t == "SK":
                    sp.wait_ge(pages_in, 16)
                    for b in range(NS):
                        for i in range(PAGES):
                            pg = page(b, i)
                            dst = tile(t).rearrange("p (b c i k) -> p b c i k", b=NS, c=2, i=PAGES)[:, b, :, i, :]
                            sp.dma_start(dst, k_pages[bass.ds(pg, 1)].rearrange("o p c k -> p (o c) k")).then_inc(done, 16)
                elif t == "WK":
                    sp.dma_start(tile(t), win_k).then_inc(done, 16)
                    projected(sp, "q", 7)
                    for b in range(NS):
                        for i in range(PAGES):
                            pg = page(b, i)
                            c = (b * PAGES + i) * 2 * P
                            sp.dma_start(slc_v[:, c:c + 2 * P], v_pages[bass.ds(pg, 1)].rearrange("o p v -> (o p) v"))\
                              .then_inc(past_v_in, 16)
                    sp.dma_start(win_v_past[:], win_v).then_inc(past_v_in, 16)
                else:
                    sp.dma_start(ring[:, n % NSLOT, :], wd[wn]).then_inc(done, 16)
                    wn += 1
                if n == NSLOT - 1:
                    sp.dma_start(w_s, spatial).then_inc(spatial_in, 16)
                    sp.dma_start(b_s, spatial_bias).then_inc(spatial_in, 16)
                    sp.dma_start(pages[:], page_table).then_inc(pages_in, 16)
                    sp.dma_start(PR[:], params).then_inc(params_in, 16)
                    sp.dma_start(LT[:], late_in).then_inc(params_in, 16)
            sp.sem_inc(lo_ready, 2 * NRAW)
            sp.sem_inc(item_used, NSPLIT)
            sp.wait_ge(o_done, NH)
            sp.wait_ge(so_ready, 1)
            sp.wait_ge(kv_stored, 16)
            for u in range(UNITS):
                if u >= NRAW:
                    sp.wait_ge(lo_ready, 2 * u + 2)
                sp.dma_start(raw[:, u % NRAW, :], moe[0, u]).then_inc(raw_in[u % NRAW], 16)
            sp.wait_ge(blk_ready, 1)
            nblk = sp.value_load(blkinfo[0:1, MAXB:MAXB + 1], min_val=2, max_val=MAXB)
            with sp.Fori(1, nblk) as t:
                e = sp.value_load(blkinfo[0:1, bass.ds(t, 1)], min_val=0, max_val=NE - 1)
                for u in range(UNITS):
                    sp.wait_ge(lo_ready, t * ITEMS + 2 * u + 2)
                    sp.dma_start(raw[:, u % NRAW, :], moe[bass.ds(e, 1), u].rearrange("o p n -> (o p) n"))\
                      .then_inc(raw_in[u % NRAW], 16)
            sp.wait_ge(h_ready, 48)
            sp.dma_start(y_out, hB[:]).then_inc(y_stored, 16)
            for stored in (y_stored, v_stored, kv_stored, past_stored):
                sp.wait_ge(stored, 16)

        @block.gpsimd
        def _(pool):
            pool.wait_ge(vn_ready, 8)
            pool.dma_start(v_out, vT).then_inc(v_stored, 16)
            pool.dma_start(past_out, state_win).then_inc(past_stored, 16)
            pool.wait_ge(pages_in, 16)
            for v in range(2):
                if v == 0:
                    projected(pool, "dn", 23)
                else:
                    nc.gpsimd.memset(Q[:], 0.0).then_inc(q_zero, 1)
                    nc.gpsimd.memset(Qz[:], 0.0).then_inc(q_zero, 1)
                    nc.gpsimd.memset(Qc[:], 0.0).then_inc(q_zero, 1)
                    projected(pool, "kv", 11)
                for b in range(NS):
                    for i in range(PAGES):
                        pg = pool.value_load(pages[0:1, b * PAGES + i:b * PAGES + i + 1], min_val=0,
                                             max_val=cmp_pages.shape[0] - 1)
                        c = (b * PAGES + i) * NG * HD
                        pool.dma_start(X2[v][:, c:c + NG * HD],
                                       cmp_pages[bass.ds(pg, 1), :, v].rearrange("o p n -> (o p) n")).then_inc(cmp_in[v], 16)
            pool.wait_ge(kv_ready, 12)
            pool.dma_start(kv_out, kvT).then_inc(kv_stored, 16)
            pool.wait_ge(gtok_ready, 2)
            pool.dma_start(grow[:], gsam[0:NS, :]).then_inc(grow_in, 16)

        @block.scalar
        def _(act):
            nstep = [0]

            def settle(ins):
                nstep[0] += 1
                ins.then_inc(act_step, 1)
                act.wait_ge(act_step, nstep[0])

            def std(ready, n, eps):
                act.wait_ge(ready, n)
                nc.scalar.activation(rstd[:, :], STAT[:, 0:NT], ACT.Sqrt, bias=const("eps")[:, eps:eps + 1]).then_inc(std_ready, 1)

            def squares(norm, k, dst=hB):
                act.wait_ge(x_ready, 8 * norm + k - 7)
                nc.scalar.activation(dst[:, k, :], x[:, k, :], ACT.Square).then_inc(sq_ready, 1)

            rounded = [0]

            def round_to(stage, c):
                while rounded[0] < min(FIRST[stage] + c + 3, NDENSE):
                    n = rounded[0]
                    if n % 4 == 0:
                        arrived(act, TILES[n // 4])
                    if n >= NDS:
                        act.wait_ge(dense_done, n - NDS + 1)
                    nc.scalar.copy(d_hi[:, n % NDS, :], raw_item(n)).then_inc(d_hi_ready, 1)
                    rounded[0] += 1

            def round_normed(norm, dst):
                for k in range(KC):
                    act.wait_ge(norm_ready, 8 * norm + k + 1)
                    nc.scalar.copy(dst[:, k, :], hB[:, k, :]).then_inc(h_hi_ready, 1)

            act.wait_ge(setup_in, 32)
            act.wait_ge(x_in, 16)
            for k in range(KC):
                nc.scalar.activation(hB[:, k, :], x[:, k, :], ACT.Square).then_inc(sq_ready, 1)
            std(stat_ready, 1, 0)
            round_to("vu", -1)
            round_normed(0, hA_hi)
            for c in range(KC):
                round_to("vu", c)
                projected(act, "vu", c)
                nc.scalar.activation(vT[:, c, :], B[c % 4][:, 0:NT], ACT.Gelu_apprx_tanh).then_inc(v_ready, 1)
            for c in range(KC):
                round_to("vu", KC + c)
                projected(act, "vu", KC + c)
                nc.scalar.activation(uT[:, c, :], B[c % 4][:, 0:NT], ACT.Gelu_apprx_tanh).then_inc(u_ready, 1)
                if c < 4:
                    for k in (2 * c, 2 * c + 1):
                        act.wait_ge(ctr_ready, k + 1)
                        nc.scalar.activation(hB[:, k, :], vT[:, k, :], ACT.Square).then_inc(csq_ready, 1)
                if c == 5:
                    std(var_stat, 1, 1)
            for i in range(6):
                if i % 2:
                    r = P if i < 4 else NS
                    act.wait_ge(vt_done, i + 1)
                    nc.scalar.copy(vtok[0:r, i // 2, 512:1024], T1[0:r, :]).then_inc(vt_ready, 1)
            for g in range(8):
                act.wait_ge(gated, g + 1)
                nc.scalar.copy(hC_hi[:, g, :], hB[:, g, :]).then_inc(gated_hi, 1)
            for c in range(KC):
                round_to("ao", c)
                squares(1, c)
            std(stat_ready, 2, 0)
            round_normed(1, hA_hi)

            def round_hidden(f):
                act.wait_ge(hF_ready, f + 1)
                nc.scalar.copy(hF_hi[:, f, :], hB[:, f % 4, :]).then_inc(hF_hi_ready, 1)

            for f in range(FC):
                round_to("gu", 2 * f)
                projected(act, "gu", 2 * f)
                if f >= 2:
                    act.wait_ge(hF_ready, f - 1)
                nc.scalar.activation(sil[:, f % 2, :], B[2 * (f % 2)][:, 0:NT], ACT.Silu).then_inc(sil_ready, 1)
                if f:
                    round_hidden(f - 1)
            round_to("gu", 2 * FC - 1)
            round_hidden(FC - 1)
            for c in range(KC):
                round_to("dn", 12 * (c // 4) + 8 + c % 4)
                squares(2, c)
            std(stat_ready, 3, 0)
            round_normed(2, hA_hi)
            round_normed(3, hC_hi)
            for c in range(12):
                round_to("kv", c)
                projected(act, "kv", c)
                nc.scalar.copy(kvT[:, c, :], B[c % 4][:, 0:NT]).then_inc(kv_ready, 1)
            act.wait_ge(q_zero, 1)
            for c in range(KC):
                half = 64 * ((c // 2) % 2)
                round_to("q", c)
                projected(act, "q", c)
                nc.scalar.mul(Q[half:half + 64, 2 * c + 1, :], B[c % 4][64:128, 0:NT], HD ** -0.5).then_inc(q_odd, 1)
            act.wait_ge(gp_done, 1)
            nc.scalar.activation(gT[0:48, :], MISC[0:48, 0:NT], ACT.Sigmoid).then_inc(sig_ready, 1)
            for v in range(2):
                act.wait_ge(cmp_done, v + 1)
                if v:
                    act.wait_ge(pre_ready, 1)
                nc.scalar.copy(hidb[0:64, 0:512], B[2 * v][64:128, :]).then_inc(bhalf_ready, 1)
                nc.scalar.copy(hidb[0:64, 512:578], B[2 * v + 1][64:128, 0:66]).then_inc(bhalf_ready, 1)
                act.wait_ge(pre_ready, v + 1)
                nc.scalar.activation(hid[0:64], hid[0:64], ACT.Gelu_apprx_tanh, bias=cbias[0:64, :]).then_inc(hid_ready, 1)
            act.wait_ge(ss_max, 1)
            W = PAST + NS
            for j, (a, z) in enumerate([(0, W), (W, 2 * W), (2 * W, 2 * W + NS * NCMP)]):
                i = nc.scalar.activation(Ss[:, a:z], Ss[:, a:z], ACT.Exp, bias=smx[:, j:j + 1], accum_out=ssm[:, j:j + 1])
            i.then_inc(ss_exp, 1)

            def exp_head(h):
                b = h % 3
                act.wait_ge(neg_max, h + 1)
                S = Sh[:, b, :]
                for j, (a, z) in enumerate([(0, 128), (414, 542), (128, 384), (542, 798), (384, 399), (399, 414)]):
                    i = nc.scalar.activation(S[:, a:z], S[:, a:z], ACT.Exp, bias=mx[:, b, j:j + 1],
                                             accum_out=sm[:, b, j:j + 1])
                i.then_inc(exps, 1)

            def head_out(h):
                act.wait_ge(o_done, h + 1)
                half = 64 * (h % 2)
                nc.scalar.copy(hB[half:half + 64, h // 2, 0:NP], (STAT, MISC)[h % 2][0:64, 0:NP]).then_inc(o_ready, 1)

            exp_head(0)
            exp_head(1)
            for j in (0, 2):
                act.wait_ge(orow_done, j + 1)
                nc.scalar.copy(orow[:, 512 * j:512 * j + 512], B[j][0:NH, :]).then_inc(orow_ready, 1)
            for h in range(NH):
                act.wait_ge(pt_done, 2 * h + 2)
                if h >= 2:
                    act.wait_ge(o_done, h - 1)
                nc.scalar.copy(PT[:, h % 2, 0, :], T0[:, :]).then_inc(pt_ready, 1)
                nc.scalar.copy(PT[:, h % 2, 1, :], T1[:, :]).then_inc(pt_ready, 1)
                if h + 2 < NH:
                    exp_head(h + 2)
                if h >= 1:
                    head_out(h - 1)
            head_out(NH - 1)
            for c in range(KC):
                squares(3, c, sq3)
            std(stat_ready, 4, 0)
            act.wait_ge(lT_done, 1)
            nc.scalar.copy(lgT[:, :], MISC[0:NE, 0:NT]).then_inc(lT_ready, 1)
            act.wait_ge(kv_stored, 16)
            for t in range(3):
                r = P if t < 2 else NS
                for half in range(2):
                    act.wait_ge(ht_done, 2 * t + half + 1)
                    nc.scalar.copy(htok[0:r, t, 512 * half:512 * half + 512], HT[2 * t + half][0:r, :]).then_inc(ht_ready, 1)
            act.wait_ge(rank_in, 1)
            nc.scalar.activation(sc[:, :, 4:5], sc[:, :, 3:4], ACT.Exp).then_inc(exp_ready, 1)
            act.wait_ge(blk_ready, 1)
            nblk = act.value_load(blkinfo[0:1, MAXB:MAXB + 1], min_val=1, max_val=MAXB)

            def gathered(t):
                for half, bank in enumerate((STAT, MISC)):
                    act.wait_ge(xg_done, 2 * t + half + 1)
                    nc.scalar.copy(xg_hi[:, 4 * half:4 * half + 4, :], bank[:, :].rearrange("p (k n) -> p k n", n=P))\
                        .then_inc(xg_hi_ready, 1)

            def rows_out(t):
                act.wait_ge(item_used, t * ITEMS + NSPLIT)
                act.wait_ge(comb_done, t * KC)
                nc.scalar.copy(yrow[:, 0:512], B[2][:, :]).then_inc(yrow_ready, 1)

            gathered(0)
            with act.Fori(0, nblk) as t:
                def round_item(i):
                    u = i // 2
                    if i % 2 == 0:
                        act.wait_ge(raw_in[u % NRAW], t * (16 * UNITS // NRAW) + 16 * (u // NRAW + 1))
                    act.wait_ge(item_used, t * ITEMS + i + 1)
                    nc.scalar.copy(w_hi[:, i % NSPLIT, :], raw[:, u % NRAW, ITEM * (i % 2):ITEM * (i % 2) + ITEM])\
                        .then_inc(hi_ready, 1)

                def transposed(f):
                    act.wait_ge(hmT_done, t * FT + f + 1)
                    if f >= 2:
                        act.wait_ge(item_used, t * ITEMS + NSPLIT + DOWN_END[f - 2])
                    nc.scalar.copy(hm_hi[:, f % 2, :, :], (T0, T1)[f % 2][:, 0:256].rearrange("p (k n) -> p k n", n=P))\
                        .then_inc(hmT_hi, 1)

                n = 0
                for _ in range(4):
                    round_item(n)
                    n += 1
                rows_out(t)
                for f in range(FT):
                    for _ in range(2 * (f >= 2) + 4 * (f + 1 < FT)):
                        round_item(n)
                        n += 1
                    act.wait_ge(item_used, t * ITEMS + NSPLIT + UP_END[f])
                    nc.scalar.activation(sg[:, f % 2, :], B[f % 2][:, 0:256], ACT.Silu).then_inc(sg_ready, 1)
                    if f:
                        transposed(f - 1)
                for _ in range(2):
                    round_item(n)
                    n += 1
                gathered(t + 1)
                transposed(FT - 1)
                for _ in range(2):
                    round_item(n)
                    n += 1
            rows_out(nblk)
            act.wait_ge(comb_added, nblk * KC + KC)
            for k in range(KC):
                nc.scalar.activation(sq_last[:, k, :], x[:, k, :], ACT.Square).then_inc(sq_ready, 1)
            std(stat_ready, 5, 0)

        @block.vector
        def _(dve):
            V = nc.vector
            nstep = [0]

            def settle(ins):
                nstep[0] += 1
                ins.then_inc(dve_step, 1)
                dve.wait_ge(dve_step, nstep[0])

            nstd = [0]

            def inv_std():
                nstd[0] += 1
                dve.wait_ge(std_ready, nstd[0])
                settle(V.reciprocal(rstd[:, :], rstd[:, :]))

            def normed(weight):
                for k in range(KC):
                    V.scalar_tensor_tensor(hB[:, k, :], x[:, k, :], weight[:, k:k + 1], rstd[:, :], ALU.mult, ALU.mult)\
                        .then_inc(h_ready, 1)

            def split_normed(norm, weight, hi, lo):
                for k in range(KC + 2):
                    if k < KC:
                        if norm:
                            dve.wait_ge(h_ready, 8 * norm - KC + k + 1)
                        V.scalar_tensor_tensor(hB[:, k, :], x[:, k, :], weight[:, k:k + 1], rstd[:, :], ALU.mult, ALU.mult)\
                            .then_inc(norm_ready, 1)
                    if k >= 2:
                        dve.wait_ge(h_hi_ready, 8 * norm + k - 1)
                        V.tensor_tensor(lo[:, k - 2, :], hB[:, k - 2, :], hi[:, k - 2, :].bitcast(F32), ALU.subtract)\
                            .then_inc(h_ready, 1)

            rested = [0]

            def rest_to(stage, c):
                while rested[0] < min(FIRST[stage] + c + 3, NDENSE):
                    n = rested[0]
                    dve.wait_ge(d_hi_ready, n + 1)
                    V.tensor_tensor(d_lo[:, n % NDS, :], raw_item(n), d_hi[:, n % NDS, :].bitcast(F32), ALU.subtract)\
                        .then_inc(d_lo_ready, 1)
                    rested[0] += 1

            dve.wait_ge(setup_in, 32)
            dve.wait_ge(x_in, 16)
            inv_std()
            rest_to("vu", -1)
            split_normed(0, vector("mix0"), hA_hi, hA_lo)
            dve.wait_ge(spatial_in, 32)
            upto = const("upto").unsqueeze(1).to_broadcast([P, 8, P])
            V.tensor_tensor(wsT[:], w_s, upto, ALU.mult).then_inc(ws_ready, 1)
            V.tensor_tensor(dg[0:NS], ident[0:NS, 0:NS].unsqueeze(1).to_broadcast([NS, 8, NS]),
                            vector("w00")[0:NS, :].unsqueeze(2).to_broadcast([NS, 8, NS]), ALU.mult).then_inc(ws_ready, 1)
            rest_to("vu", 8)
            dve.wait_ge(mu_stat, 1)
            settle(V.tensor_copy(mu[:, :], STAT[:, 0:NT]))
            for k in range(KC):
                V.tensor_tensor(vT[:, k, :], vT[:, k, :], mu[:, :], ALU.subtract).then_inc(ctr_ready, 1)
                if k % 2:
                    rest_to("vu", 8 + k // 2)
            rest_to("vu", 13)
            inv_std()
            for k in range(KC):
                if k % 3 == 2:
                    rest_to("vu", 13 + k // 3)
                V.scalar_tensor_tensor(vT[:, k, :], vT[:, k, :], vector("lng")[:, k:k + 1], rstd[:, :], ALU.mult, ALU.mult)\
                    .then_inc(dve_step, 1)
                nstep[0] += 1
            dve.wait_ge(dve_step, nstep[0])
            for k in range(KC):
                V.tensor_scalar(vT[:, k, :], vT[:, k, :], vector("lnb")[:, k:k + 1], None, ALU.add).then_inc(vn_ready, 1)
            for i in range(0, 6, 2):
                r = P if i < 4 else NS
                dve.wait_ge(vt_done, i + 1)
                V.tensor_copy(vtok[0:r, i // 2, 0:512], T0[0:r, :]).then_inc(vt_ready, 1)
            rest_to("vu", 15)
            for g in range(10):
                if g < 8:
                    dve.wait_ge(mix_done, g + 1)
                    dve.wait_ge(u_ready, g + 1)
                    V.tensor_tensor(hB[:, g, :], uT[:, g, :], B[g % 4][:, 0:NT], ALU.mult).then_inc(gated, 1)
                if g >= 2:
                    dve.wait_ge(gated_hi, g - 1)
                    V.tensor_tensor(hC_lo[:, g - 2, :], hB[:, g - 2, :], hC_hi[:, g - 2, :].bitcast(F32), ALU.subtract)\
                        .then_inc(gated_lo, 1)
            for c in range(KC):
                rest_to("ao", c)
                projected(dve, "ao", c)
                V.tensor_tensor(x[:, c, :], x[:, c, :], B[c % 4][:, 0:NT], ALU.add).then_inc(x_ready, 1)
            inv_std()
            split_normed(1, vector("ffn0"), hA_hi, hA_lo)
            dve.wait_ge(v_stored, 16)

            def rest_hidden_row(f):
                dve.wait_ge(hF_hi_ready, f + 1)
                V.tensor_tensor(hF_lo[:, f, :], hB[:, f % 4, :], hF_hi[:, f, :].bitcast(F32), ALU.subtract).then_inc(hF_lo_ready, 1)

            for f in range(FC):
                rest_to("gu", 2 * f + 1)
                projected(dve, "gu", 2 * f + 1)
                dve.wait_ge(sil_ready, f + 1)
                if f >= 2:
                    rest_hidden_row(f - 2)
                if f >= 4:
                    dve.wait_ge(hF_lo_ready, f - 3)
                V.tensor_tensor(hB[:, f % 4, :], sil[:, f % 2, :], B[2 * (f % 2) + 1][:, 0:NT], ALU.mult).then_inc(hF_ready, 1)
            rest_hidden_row(FC - 2)
            rest_hidden_row(FC - 1)
            for c in range(KC):
                rest_to("dn", 12 * (c // 4) + 8 + c % 4)
                projected(dve, "dn", 12 * (c // 4) + 8 + c % 4)
                V.tensor_tensor(x[:, c, :], x[:, c, :], B[c % 4][:, 0:NT], ALU.add).then_inc(x_ready, 1)
            inv_std()
            split_normed(2, vector("kvn"), hA_hi, hA_lo)
            split_normed(3, vector("mix1"), hC_hi, hC_lo)
            for v in range(2):
                o = NS * PAGES * NG * HD
                for g in range(NG):
                    c = 2 * v + g // 2
                    rest_to("kv", 11 if v else 1 + g)
                    if v:
                        projected(dve, "kv", 11)
                    dve.wait_ge(kv_ready, c + 1)
                    for r in range(2):
                        src = kvT[64 * (g % 2):64 * (g % 2) + 64, c, r:NP:2]
                        V.tensor_copy(X2[v][64 * r:64 * r + 64, o + g * P:o + g * P + P], src).then_inc(x2_ready, 1)
                o += NG * P
                dve.wait_ge(params_in, 32)
                V.tensor_copy(X2[v][:, o:o + 16], par("pe")[:, 16 * v:16 * v + 16]).then_inc(x2_ready, 1)
            dve.wait_ge(q_zero, 1)
            for c in range(KC):
                half = 64 * ((c // 2) % 2)
                rest_to("q", c)
                projected(dve, "q", c)
                V.tensor_scalar(Q[half:half + 64, 2 * c, :], B[c % 4][0:64, 0:NT], HD ** -0.5, None, ALU.mult).then_inc(q_even, 1)
            dve.wait_ge(q_zero, 3)
            dve.wait_ge(q_even, KC)
            dve.wait_ge(q_odd, KC)
            for gp in range(2):
                src = Q[:, 8 * gp:8 * gp + 8, NP:NT].rearrange("p h b -> p b h")
                qz = Qz[:, gp, :, :].rearrange("p b n -> p (b n)")
                for b in range(NS):
                    V.tensor_copy(Qz[:, gp, b, b * NH + 8 * gp:b * NH + 8 * gp + 8], src[:, b, :])
                V.tensor_copy(Qc[:, gp, :].rearrange("p (b h) -> p b h", h=NH)[:, :, 8 * gp:8 * gp + 8], src).then_inc(q_rows, 1)
            dve.wait_ge(gt_done, 1)
            V.tensor_copy(gtok[:, :, :], MISC[:, 0:96].rearrange("p (t n) -> p t n", n=48)).then_inc(gtok_ready, 1)
            V.tensor_copy(gsam[0:NS, :], MISC[0:NS, 96:144]).then_inc(gtok_ready, 1)
            for t in range(3):
                r = P if t < 2 else NS
                dve.wait_ge(vp_done, t + 1)
                dst = vtp[:, t, :, :] if t < 2 else vnew[0:NS]
                V.tensor_copy(dst, (T0, T1)[t % 2][0:r, :].rearrange("p (a n) -> p a n", a=2)).then_inc(vp_ready, 1)
            for v in range(2):
                dve.wait_ge(bhalf_ready, 2 * v + 2)
                if v:
                    dve.wait_ge(cmp2_done, 1)
                A0 = B[2 * v][0:64, :].rearrange("p (b i g s) -> p b i g s", b=NS, i=PAGES, g=NG)
                H0 = hidb[0:64, 0:512].rearrange("p (b i g s) -> p b i g s", b=NS, i=PAGES, g=NG)
                out = hid[0:64, 0:32, :].rearrange("p (g b) n -> p b g n", g=NG)
                V.tensor_tensor(out[:, :, :, 0:7], A0[:, :, 0, :, 0:7], H0[:, :, 0, :, 1:8], ALU.add)
                V.tensor_tensor(out[:, :, :, 7:8], A0[:, :, 0, :, 7:8], H0[:, :, 1, :, 0:1], ALU.add)
                V.tensor_tensor(out[:, :, :, 8:15], A0[:, :, 1, :, 0:7], H0[:, :, 1, :, 1:8], ALU.add)
                A1 = B[2 * v + 1][0:64, 0:64].rearrange("p (g s) -> p g s", g=NG)
                H1 = hidb[0:64, 512:576].rearrange("p (g s) -> p g s", g=NG)
                V.tensor_tensor(hid[0:64, 32:36, :], A1[:, :, 0:15], H1[:, :, 1:16], ALU.add)
                V.tensor_tensor(cbias[0:64, :], B[2 * v + 1][0:64, 64:65], hidb[0:64, 577:578], ALU.add).then_inc(pre_ready, 1)
                dve.wait_ge(cmp2_done, v + 1)
                if v == 0:
                    V.tensor_copy(kcT[:], T0[:, 0:270].rearrange("p (a n) -> p a n", n=NCMP)).then_inc(cmp2_ready, 1)
                else:
                    V.tensor_copy(vcs[0:NS * NCMP, :], T1[0:NS * NCMP, 0:256])
                    V.tensor_copy(vcp[0:NCMP, :], T1[0:NCMP, 256:512]).then_inc(cmp2_ready, 1)
            dve.wait_ge(cmp2_ready, 2)
            V.memset(T0[:, 384:512], 0.0).then_inc(t_zeroed, 1)
            V.memset(T1[:, 384:512], 0.0).then_inc(t_zeroed, 1)
            dist = const("dist")
            W = PAST + NS
            slope = const("negslope")
            dve.wait_ge(ss_done, 1)
            V.scalar_tensor_tensor(Ss[:, 0:W], const("sdist"), slope, B[0][:, 0:W], ALU.mult, ALU.add)
            V.scalar_tensor_tensor(Ss[:, W:2 * W], const("sdist"), slope, B[1][:, 0:W], ALU.mult, ALU.add)
            settle(V.scalar_tensor_tensor(Ss[:, 2 * W:2 * W + 120], const("scdist"), slope, B[2][:, 0:120], ALU.mult, ALU.add))
            parts = [(0, W), (W, 2 * W), (2 * W, 2 * W + NS * NCMP)]
            for j, (a, z) in enumerate(parts):
                i = V.tensor_reduce(smx[:, j:j + 1], Ss[:, a:z], AX_X, ALU.max)
            settle(i)
            V.tensor_scalar(smx[:, :], smx[:, :], -1.0, None, ALU.mult).then_inc(ss_max, 1)
            dve.wait_ge(ss_exp, 1)
            settle(V.reciprocal(ssm[:, :], ssm[:, :]))
            dve.wait_ge(grow_in, 16)
            V.tensor_tensor(swt[:, 0:2], ssm[:, 0:2], grow[:, 1:3], ALU.mult)
            settle(V.tensor_tensor(swt[:, 2:3], ssm[:, 2:3], grow[:, 0:1], ALU.mult))
            for j, (a, z) in enumerate(parts):
                i = V.tensor_scalar(Ss[:, a:z], Ss[:, a:z], swt[:, j:j + 1], None, ALU.mult)
            i.then_inc(sp_ready, 1)

            def by_two(h, a, w):
                return Sh[:, h % 3, 0:828].rearrange("p (n c) -> p n c", n=2)[:, :, a:a + w]

            def biased_max(h):
                b = h % 3
                S = Sh[:, b, :]
                dve.wait_ge(s_done, h + 1)
                if h >= 3:
                    dve.wait_ge(pt_done, 2 * h - 4)
                V.scalar_tensor_tensor(S[:, 0:414], dist, -SLOPE[h], B[2 * (h % 2)][:, 0:414], ALU.mult, ALU.add)
                V.scalar_tensor_tensor(S[:, 414:798], dist[:, 0:384], -SLOPE[h], B[2 * (h % 2) + 1][:, 0:384], ALU.mult, ALU.add)\
                    .then_inc(s_biased, 1)
                dve.wait_ge(s_biased, h + 1)
                V.tensor_reduce(mx[:, b, 0:2], by_two(h, 0, P), AX_X, ALU.max)
                V.tensor_reduce(mx[:, b, 2:4], by_two(h, P, NP), AX_X, ALU.max)
                settle(V.tensor_reduce(mx[:, b, 4:6], S[:, 384:414].rearrange("p (t n) -> p t n", n=NCMP), AX_X, ALU.max))
                V.tensor_scalar(mx[:, b, :], mx[:, b, :], -1.0, None, ALU.mult).then_inc(neg_max, 1)

            def scale(h):
                b = h % 3
                S = Sh[:, b, :]
                dve.wait_ge(exps, h + 1)
                settle(V.reciprocal(sm[:, b, :], sm[:, b, :]))
                g3 = gtok[:, :, 3 * h:3 * h + 3]
                dst = wt[:, b, :].rearrange("p (a t) -> p a t", a=3)
                V.tensor_tensor(dst[:, 0, :], sm[:, b, 4:6], g3[:, :, 0], ALU.mult)
                V.tensor_tensor(dst[:, 1, :], sm[:, b, 0:3:2], g3[:, :, 1], ALU.mult)
                settle(V.tensor_tensor(dst[:, 2, :], sm[:, b, 1:4:2], g3[:, :, 2], ALU.mult))
                cm = const("cmpmask")
                for t in range(2):
                    V.scalar_tensor_tensor(S[:, 384 + 15 * t:399 + 15 * t], S[:, 384 + 15 * t:399 + 15 * t],
                                           wt[:, b, t:t + 1], cm[:, 15 * t:15 * t + 15], ALU.mult, ALU.mult)
                for j, (a, z, w) in enumerate([(0, 128, 2), (128, 384, 3), (414, 542, 4), (542, 798, 5)]):
                    i = V.tensor_scalar(S[:, a:z], S[:, a:z], wt[:, b, w:w + 1], None, ALU.mult)
                i.then_inc(p_ready, 1)

            biased_max(0)
            biased_max(1)
            dve.wait_ge(spt_done, 1)
            V.tensor_copy(PTs[:, 0:4, :], T0[:, :].rearrange("p (a n) -> p a n", n=P))
            V.tensor_copy(PTs[0:NS, 4:6, :], T1[0:NS, 0:256].rearrange("p (a n) -> p a n", n=P))
            V.tensor_copy(PTs[0:NS * NCMP, 6, :], T1[0:NS * NCMP, 256:384]).then_inc(spt_ready, 1)
            for j in (1, 3):
                dve.wait_ge(orow_done, j + 1)
                V.tensor_copy(orow[:, 512 * j:512 * j + 512], B[j][0:NH, :]).then_inc(orow_ready, 1)
            dve.wait_ge(so_done, 1)
            for g2 in range(2):
                for odd in range(2):
                    src = STAT[64 * g2:64 * g2 + 64, 0:256].rearrange("p (c b h) -> p c b h", c=2, h=NH)
                    dst = hB[64 * odd:64 * odd + 64, :, NP:NT].rearrange("p (c g i) b -> p c g i b", c=2, g=2)
                    for c in range(2):
                        h0 = 8 * c + 4 * g2 + odd
                        i = V.tensor_copy(dst[:, c, g2, :, :], src[:, c, :, h0:h0 + 3:2].rearrange("p b i -> p i b"))
            i.then_inc(so_ready, 1)
            scale(0)
            for h in range(NH):
                if h + 2 < NH:
                    biased_max(h + 2)
                if h + 1 < NH:
                    scale(h + 1)
            for c in range(KC):
                dve.wait_ge(bo_done, c + 1)
                V.tensor_tensor(x[:, c, :], x[:, c, :], B[c % 4][:, 0:NT], ALU.add).then_inc(x_ready, 1)
            inv_std()
            normed(late("ffn1"))

            dve.wait_ge(kv_stored, 16)
            L = lg
            def col(i, t=None):
                return L[:, :, 8 * i:8 * i + 8] if t is None else L[:, t, 8 * i:8 * i + 8]

            def wide(ap):
                return ap.to_broadcast([P, 3, 8])

            down8 = const("down8").unsqueeze(1).to_broadcast([P, 3, 8])
            V.memset(lg[:], 0.0)
            settle(V.memset(sc[:], 0.0))
            dve.wait_ge(route_done, 1)
            V.tensor_copy(col(0)[:, 0:2, :], MISC[:, 0:16].rearrange("p (t n) -> p t n", n=8))
            settle(V.tensor_copy(col(0, 2)[0:NS, :], MISC[0:NS, 16:24]))

            def best(src, dst, m):
                settle(V.tensor_reduce(sc[:, :, m:m + 1], src, AX_X, ALU.max))
                settle(V.tensor_tensor(col(1), src, wide(sc[:, :, m:m + 1]), ALU.is_equal))
                settle(V.tensor_tensor(col(1), col(1), down8, ALU.mult))
                settle(V.tensor_reduce(sc[:, :, 2:3], col(1), AX_X, ALU.max))
                settle(V.tensor_tensor(dst, col(1), wide(sc[:, :, 2:3]), ALU.is_equal))

            best(col(0), col(2), 0)
            settle(V.scalar_tensor_tensor(col(3), col(2), -3e38, col(0), ALU.mult, ALU.add))
            best(col(3), col(4), 1)
            V.tensor_tensor(col(5), col(2), col(4), ALU.add)
            V.tensor_tensor(sc[:, :, 3:4], sc[:, :, 1:2], sc[:, :, 0:1], ALU.subtract).then_inc(rank_in, 1)
            dve.wait_ge(exp_ready, 1)
            settle(V.tensor_scalar(sc[:, :, 5:6], sc[:, :, 4:5], 1.0, None, ALU.add))
            settle(V.reciprocal(sc[:, :, 6:7], sc[:, :, 5:6]))
            V.tensor_tensor(sc[:, :, 7:8], sc[:, :, 4:5], sc[:, :, 6:7], ALU.mult)
            dve.wait_ge(rank_done, 1)
            counts = MISC[:, 48:56]
            V.tensor_scalar(cnt[:, 0:1], counts[:, 0:1], -1.0, None, ALU.is_gt)
            settle(V.tensor_scalar(cnt[:, 1:8], counts[:, 1:8], 0.0, None, ALU.is_gt))
            settle(V.scalar_tensor_tensor(cnt[:, 0:8], counts, float(ROWS), cnt[:, 0:8], ALU.is_gt, ALU.add))
            settle(V.scalar_tensor_tensor(cnt[:, 0:8], counts, float(2 * ROWS), cnt[:, 0:8], ALU.is_gt, ALU.add))
            settle(V.tensor_copy(cnt[:, 8:16], cnt[:, 0:8]))
            a, z = 8, 16
            for s in (1, 2, 4):
                V.tensor_copy(cnt[:, z:z + s], cnt[:, a:a + s])
                settle(V.tensor_tensor(cnt[:, z + s:z + 8], cnt[:, a + s:a + 8], cnt[:, a:a + 8 - s], ALU.add))
                a, z = z, z + 8
            ends_ = cnt[:, a:a + 8]
            settle(V.tensor_tensor(cnt[:, 48:56], ends_, cnt[:, 0:8], ALU.subtract))
            settle(V.tensor_scalar(cnt[:, 48:56], cnt[:, 48:56], float(ROWS), None, ALU.mult))
            V.tensor_tensor(col(6)[:, 0:2, :], MISC[:, 24:40].rearrange("p (t n) -> p t n", n=8),
                            cnt[:, 48:56].unsqueeze(1).to_broadcast([P, 2, 8]), ALU.add)
            settle(V.tensor_tensor(col(6, 2)[0:NS, :], MISC[0:NS, 40:48], cnt[0:NS, 48:56], ALU.add))
            for m in range(2):
                settle(V.tensor_tensor(col(7), col(2 + 2 * m), col(6), ALU.mult))
                settle(V.tensor_reduce(sc[:, :, 8 + m:9 + m], col(7), AX_X, ALU.add))
            settle(V.tensor_tensor(bcmp[0:1, :].rearrange("p (t e) -> p t e", e=NE),
                                   ends_[0:1, :].unsqueeze(1).to_broadcast([1, MAXB, NE]),
                                   const("blk")[0:1, :].rearrange("p (t e) -> p t e", e=NE), ALU.is_le))
            settle(V.tensor_reduce(bout[0:1, 0:MAXB], bcmp[0:1, :].rearrange("p (t e) -> p t e", e=NE), AX_X, ALU.add))
            settle(V.tensor_scalar(bout[0:1, 0:MAXB], bout[0:1, 0:MAXB], float(NE - 1), None, ALU.min))
            V.tensor_copy(blkinfo[0:1, MAXB:MAXB + 1], ends_[0:1, 7:8])
            V.tensor_copy(blkinfo[0:1, 0:MAXB], bout[0:1, 0:MAXB]).then_inc(blk_ready, 1)

            def selections():
                tiles = [(t, P if t < 2 else NS) for t in range(3)]
                iota = const("iota")
                for t, r in tiles:
                    V.tensor_scalar(Gm[0:r, t, :], iota[0:r, :], sc[0:r, t, 8:9], None, ALU.is_equal).then_inc(dve_sel, 1)
                for t, r in tiles:
                    dve.wait_ge(dve_sel, selbase[0] + t + 1)
                    V.scalar_tensor_tensor(Gm[0:r, t, :], iota[0:r, :], sc[0:r, t, 9:10], Gm[0:r, t, :], ALU.is_equal, ALU.add)\
                        .then_inc(sel_ready, 1)
                for t, r in tiles:
                    V.tensor_scalar(Gw[0:r, t, :], iota[0:r, :], sc[0:r, t, 8:9], sc[0:r, t, 6:7], ALU.is_equal, ALU.mult)
                    V.tensor_scalar(Gt[0:r, t, :], iota[0:r, :], sc[0:r, t, 9:10], sc[0:r, t, 7:8], ALU.is_equal, ALU.mult)\
                        .then_inc(dve_sel, 1)
                for t, r in tiles:
                    dve.wait_ge(dve_sel, selbase[0] + t + 4)
                    V.tensor_tensor(Gw[0:r, t, :], Gw[0:r, t, :], Gt[0:r, t, :], ALU.add).then_inc(gw_sel, 1)
                V.tensor_scalar(sc[:, :, 8:10], sc[:, :, 8:10], -float(ROWS), None, ALU.add).then_inc(gw_sel, 1)

            def gathered(t):
                for half, bank in enumerate((STAT, MISC)):
                    dve.wait_ge(xg_hi_ready, 2 * t + half + 1)
                    V.tensor_tensor(xg_lo[:, 4 * half:4 * half + 4, :], bank[:, :].rearrange("p (k n) -> p k n", n=P),
                                    xg_hi[:, 4 * half:4 * half + 4, :].bitcast(F32), ALU.subtract).then_inc(xg_lo_ready, 1)

            def rows_out(t):
                dve.wait_ge(item_used, t * ITEMS + NSPLIT)
                dve.wait_ge(comb_done, t * KC)
                V.tensor_copy(yrow[:, 512:1024], B[3][:, :]).then_inc(yrow_ready, 1)

            def add_combined(t, c):
                dve.wait_ge(comb_done, t * KC + c + 1)
                V.tensor_tensor(x[:, c, :], x[:, c, :], (STAT, MISC)[c % 2][:, 0:NT], ALU.add).then_inc(comb_added, 1)

            V.memset(GwT[:], 0.0).then_inc(gwT_ready, 1)
            selbase = [0]
            selections()
            nblk = dve.value_load(blkinfo[0:1, MAXB:MAXB + 1], min_val=1, max_val=MAXB)
            gathered(0)
            with dve.Fori(0, nblk) as t:
                def rest_item(i):
                    dve.wait_ge(hi_ready, t * ITEMS + i + 1)
                    V.tensor_tensor(w_lo[:, i % NSPLIT, :], raw[:, (i // 2) % NRAW, ITEM * (i % 2):ITEM * (i % 2) + ITEM],
                                    w_hi[:, i % NSPLIT, :].bitcast(F32), ALU.subtract).then_inc(lo_ready, 1)

                def rest_hidden(f):
                    dve.wait_ge(hmT_hi, t * FT + f + 1)
                    V.tensor_tensor(hm_lo[:, f % 2, :, :], (T0, T1)[f % 2][:, 0:256].rearrange("p (k n) -> p k n", n=P),
                                    hm_hi[:, f % 2, :, :].bitcast(F32), ALU.subtract).then_inc(hmT_lo, 1)

                n = 0
                for _ in range(4):
                    rest_item(n)
                    n += 1
                rows_out(t)
                for f in range(FT):
                    for _ in range(2 * (f >= 2) + 4 * (f + 1 < FT)):
                        rest_item(n)
                        n += 1
                    dve.wait_ge(sg_ready, t * FT + f + 1)
                    if f >= 2:
                        dve.wait_ge(hmT_done, t * FT + f - 1)
                    V.tensor_tensor(hm[:, f % 2, :], sg[:, f % 2, :], B[f % 2][:, 256:512], ALU.mult).then_inc(hm_ready, 1)
                    if f:
                        rest_hidden(f - 1)
                    if f < 4:
                        for c in (2 * f, 2 * f + 1):
                            add_combined(t, c)
                    if f == 4:
                        dve.wait_ge(gw_done, t + 1)
                        V.tensor_copy(GwT[:, :], MISC[:, 0:NT]).then_inc(gwT_ready, 1)
                    if f == 5:
                        dve.wait_ge(gw_sel, 4 * t + 4)
                        selbase[0] = t * 6 + 6
                        selections()
                for _ in range(2):
                    rest_item(n)
                    n += 1
                gathered(t + 1)
                rest_hidden(FT - 1)
                for _ in range(2):
                    rest_item(n)
                    n += 1
            rows_out(nblk)
            for c in range(KC):
                add_combined(nblk, c)
            inv_std()
            normed(late("final"))

        @block.tensor
        def _(pe):
            T = nc.tensor
            mean = const("mean")

            def stat(k, src, bank=STAT):
                return T.matmul(bank[:, 0:NT], mean, src[:, k, :], start=(k == 0), stop=(k == KC - 1))

            taken = [0]

            def product(bank, hi, lo, ks=range(KC), first=True, last=True, each=None):
                n = taken[0]
                taken[0] += 1
                pe.wait_ge(d_lo_ready, n + 1)
                w_hi_, w_lo_ = (d[:, n % NDS, :].rearrange("p (k m) -> p k m", m=P) for d in (d_hi, d_lo))
                out = bank[:, 0:NT]
                for j, k in enumerate(ks):
                    if each:
                        each(k)
                    T.matmul(out, w_hi_[:, j, :], hi[:, k, :], start=(first and j == 0), stop=False)
                    T.matmul(out, w_hi_[:, j, :], lo[:, k, :], start=False, stop=False)
                    i = T.matmul(out, w_lo_[:, j, :], hi[:, k, :], start=False, stop=(last and k == ks[-1]))
                i.then_inc(dense_done, 1)

            def chunks_of(count, base):
                return lambda k: pe.wait_ge(count, base + k + 1)

            def stat_after(norm, k):
                pe.wait_ge(sq_ready, 8 * norm + k + 1)
                i = stat(k, {3: sq3, 4: sq_last}.get(norm, hB))
                if k == KC - 1:
                    i.then_inc(stat_ready, 1)

            pe.wait_ge(setup_in, 32)
            for k in range(KC):
                stat_after(0, k)
            for c in range(16):
                if 4 <= c < 12:
                    pe.wait_ge(v_ready, c - 3)
                elif c >= 12:
                    pe.wait_ge(u_ready, c - 11)
                product(B[c % 4], hA_hi, hA_lo, each=chunks_of(h_ready, 0) if c == 0 else None)
                if c == 8:
                    pe.wait_ge(v_ready, 8)
                    for k in range(KC):
                        i = stat(k, vT)
                    i.then_inc(mu_stat, 1)
                if c == 13:
                    pe.wait_ge(csq_ready, 8)
                    for k in range(KC):
                        i = stat(k, hB)
                    i.then_inc(var_stat, 1)
            pe.wait_ge(vn_ready, 8)
            for t, (a, z) in enumerate([(0, P), (P, NP), (NP, NT)]):
                if t:
                    pe.wait_ge(vt_ready, 2 * t)
                for half, bank in ((0, T0), (1, T1)):
                    for k in range(4):
                        i = T.transpose(bank[0:z - a, k * P:(k + 1) * P], vT[:, 4 * half + k, a:z], ident)
                    i.then_inc(vt_done, 1)
            pe.wait_ge(ws_ready, 2)
            pe.wait_ge(spatial_in, 32)
            pe.wait_ge(vt_ready, 6)
            for g in range(8):
                if g >= 4:
                    pe.wait_ge(gated, g - 3)
                else:
                    pe.wait_ge(u_ready, 4 + g + 1)
                bank, cols = B[g % 4], slice(g * P, (g + 1) * P)
                T.matmul(bank[:, 0:NT], ones_row[:, 0:P], b_s[:, g, :], start=True, stop=False)
                T.matmul(bank[:, 0:P], vtok[:, 0, cols], wsT[:, g, :], start=False, stop=False)
                T.matmul(bank[:, P:NP], vtok[:, 1, cols], wsT[:, g, :], start=False, stop=False)
                T.matmul(bank[:, NP:NT], vtok[0:NS, 2, cols], dg[0:NS, g, :], start=False, stop=True).then_inc(mix_done, 1)
            for c in range(KC):
                if c < 4:
                    pe.wait_ge(gated, c + 5)
                else:
                    pe.wait_ge(x_ready, c - 3)
                product(B[c % 4], hC_hi, hC_lo, each=chunks_of(gated_lo, 0) if c == 0 else None)
                if c:
                    stat_after(1, c - 1)
            stat_after(1, 7)
            for f in range(FC):
                if f >= 2:
                    pe.wait_ge(hF_ready, f - 1)
                product(B[2 * (f % 2)], hA_hi, hA_lo, each=chunks_of(h_ready, 8) if f == 0 else None)
                product(B[2 * (f % 2) + 1], hA_hi, hA_lo)
            for half in range(2):
                for part in range(3):
                    ks = range(8 * part, min(8 * part + 8, FC))
                    for j in range(4):
                        if part == 0 and half:
                            pe.wait_ge(x_ready, 8 + j + 1)
                        if half == 0 and j == 0:
                            pe.wait_ge(hF_lo_ready, ks[-1] + 1)
                        if part == 0 and half == 0 and j < 2:
                            pe.wait_ge(hF_ready, FC)
                        product(B[j], hF_hi, hF_lo, ks, part == 0, part == 2)
                    if half == 1 and part == 0:
                        for k in range(4):
                            stat_after(2, k)
            for k in range(4, 8):
                stat_after(2, k)
            for c in range(12):
                if c < 4:
                    pe.wait_ge(x_ready, 16)
                if c >= 4:
                    pe.wait_ge(kv_ready, c - 3)
                product(B[c % 4], hA_hi, hA_lo, each=chunks_of(h_ready, 16) if c == 0 else None)
            pe.wait_ge(h_ready, 32)
            pe.wait_ge(params_in, 32)
            for k in range(KC):
                T.matmul(MISC[0:48, 0:NT], w_gate[:, k, :], hB[:, k, :], start=(k == 0), stop=False)
            T.matmul(MISC[0:48, 0:NT], b_gate, ones_row, start=False, stop=True).then_inc(gp_done, 1)
            for c in range(KC):
                if c < 4:
                    pe.wait_ge(kv_ready, 8 + c + 1)
                else:
                    pe.wait_ge(q_even, c - 3)
                    pe.wait_ge(q_odd, c - 3)
                product(B[c % 4], hC_hi, hC_lo)
            pe.wait_ge(sig_ready, 1)
            for t, (a, z) in enumerate([(0, P), (P, NP), (NP, NT)]):
                i = T.transpose(MISC[0:z - a, 48 * t:48 * t + 48], gT[0:48, a:z], ident[0:48, 0:48])
            i.then_inc(gt_done, 1)
            for t, (a, z) in enumerate([(0, P), (P, NP), (NP, NT)]):
                if t == 2:
                    pe.wait_ge(vp_ready, 1)
                for j, c in enumerate((6, 7, 10, 11)):
                    i = T.transpose((T0, T1)[t % 2][0:z - a, j * P:(j + 1) * P], kvT[:, c, a:z], ident)
                i.then_inc(vp_done, 1)
            NSEG = NS * PAGES * NG * 8
            pe.wait_ge(q_even, KC)
            pe.wait_ge(q_odd, KC)
            for v in range(2):
                pe.wait_ge(cmp_in[v], 16 * NS * PAGES)
                pe.wait_ge(x2_ready, 9 * v + 9)
                for m in range(8):
                    T.matmul(B[2 * v][:, :], w1[:, v, m, :], X2[v][:, m:8 * NSEG:8], start=(m == 0), stop=(m == 7))
                    i = T.matmul(B[2 * v + 1][:, 0:66], w1[:, v, m, :], X2[v][:, 8 * NSEG + m:8 * NSEG + 528:8],
                                 start=(m == 0), stop=(m == 7))
                i.then_inc(cmp_done, 1)
            pe.wait_ge(vp_ready, 3)
            pe.wait_ge(hid_ready, 1)
            hid_s = hid[0:64, 0:32, :].rearrange("p (c g b) n -> p c g (b n)", c=2, g=2)
            for g2 in range(2):
                T.matmul(T0[:, 0:240], w2k[0:64, g2, :], hid_s[:, :, g2, :], start=(g2 == 0), stop=(g2 == 1))
            for g2 in range(2):
                i = T.matmul(T0[:, 240:270], w2k[0:64, g2, :], hid[0:64, 32 + g2:36:2, :], start=(g2 == 0), stop=(g2 == 1))
            i.then_inc(cmp2_done, 1)

            def sample_scores(n, t):
                arrived(pe, t)
                keys = tile(t).rearrange("p (b c k) -> p b c k", b=NS, c=2)
                for j in range(16):
                    i = T.matmul(B[n][:, 0:PAST], Qz[:, j % 2, j // 2, :], keys[:, j // 2, j % 2, :], start=(j == 0), stop=(j == 15))
                i.then_inc(sk_used, 1)
                for c in range(2):
                    T.matmul(B[n][:, PAST:PAST + NS], Qc[:, c, :], kvT[:, 4 + 4 * n + c, NP:NT], start=(c == 0), stop=(c == 1))

            pe.wait_ge(q_rows, 2)
            pe.wait_ge(pre_ready, 1)
            sample_scores(0, "SK")
            pe.wait_ge(hid_ready, 2)
            for g in range(NG):
                cols = slice(64 * g, 64 * g + 64)
                T.matmul(T1[0:NS * NCMP, cols], hid[0:64, 8 * g:8 * g + 8, :].rearrange("p b n -> p (b n)"), par("w2v")[0:64, :],
                         start=True, stop=True)
                i = T.matmul(T1[0:NCMP, 256 + 64 * g:320 + 64 * g], hid[0:64, 32 + g, :], par("w2v")[0:64, :], start=True, stop=True)
            i.then_inc(cmp2_done, 1)
            sample_scores(1, "WK")
            pe.wait_ge(pre_ready, 2)
            pe.wait_ge(cmp2_ready, 1)
            for c in range(2):
                i = T.matmul(B[2][:, 0:NS * NCMP], Qc[:, c, :], kcT[:, 8 * c:8 * c + 8, :], start=(c == 0), stop=(c == 1))
            i.then_inc(ss_done, 1)

            def scores(h):
                c, b = h // 8, h % 2
                if h == 0:
                    pe.wait_ge(ss_max, 1)
                if h >= 2:
                    pe.wait_ge(s_biased, h - 1)
                q0, q1 = Q[:, h, 0:P], Q[:, h, P:NP]
                slc, win = B[2 * b], B[2 * b + 1]
                T.matmul(slc[:, 0:P], q0, kvT[:, 4 + c, 0:P], start=True, stop=True)
                T.matmul(slc[:, 384:399], q0, kcT[:, 16 + c, :], start=True, stop=True)
                T.matmul(win[:, 0:P], q0, kvT[:, 8 + c, 0:P], start=True, stop=True)
                T.matmul(slc[:, P:384], q1, kvT[:, 4 + c, 0:NP], start=True, stop=True)
                T.matmul(slc[:, 399:414], q1, kcT[:, 16 + c, :], start=True, stop=True)
                T.matmul(win[:, P:384], q1, kvT[:, 8 + c, 0:NP], start=True, stop=True).then_inc(s_done, 1)

            def turn(h):
                S = Sh[:, h % 3, :]
                pe.wait_ge(p_ready, h + 1)
                if h:
                    pe.wait_ge(pt_ready, 2 * h)
                for n, bank in enumerate((T0, T1)):
                    for j in range(3):
                        T.transpose(bank[:, j * P:(j + 1) * P], S[:, 414 * n + j * P:414 * n + (j + 1) * P], ident)
                    T.transpose(bank[0:NCMP, 384:512], S[:, 384 + 15 * n:399 + 15 * n], ident).then_inc(pt_done, 1)

            def weigh(h):
                g, bank = h // 4, (STAT, MISC)[h % 2]
                cols = slice(HD * g, HD * g + HD)
                pe.wait_ge(pt_ready, 2 * h + 2)
                if h == 0:
                    pe.wait_ge(so_ready, 1)
                if h >= 2:
                    pe.wait_ge(o_ready, h - 1)
                for n in range(2):
                    T.matmul(bank[0:HD, 0:NP], vtp[:, 0, n, cols], PT[:, h % 2, n, 0:NP], start=(n == 0), stop=False)
                    T.matmul(bank[0:HD, P:NP], vtp[:, 1, n, cols], PT[:, h % 2, n, NP:384], start=False, stop=False)
                T.matmul(bank[0:HD, 0:P], vcp[0:NCMP, cols], PT[0:NCMP, h % 2, 0, 384:512], start=False, stop=False)
                T.matmul(bank[0:HD, P:NP], vcp[0:NCMP, cols], PT[0:NCMP, h % 2, 1, 384:512], start=False, stop=True).then_inc(o_done, 1)

            pe.wait_ge(vp_ready, 3)
            pe.wait_ge(t_zeroed, 2)
            pe.wait_ge(gtok_ready, 2)
            scores(0)
            scores(1)
            W = PAST + NS
            pe.wait_ge(sp_ready, 1)
            for j in range(4):
                a = W * (j // 2) + P * (j % 2)
                T.transpose(T0[:, j * P:(j + 1) * P], Ss[:, a:a + P], ident)
            T.transpose(T1[0:NS, 0:P], Ss[:, PAST:W], ident)
            T.transpose(T1[0:NS, P:2 * P], Ss[:, W + PAST:2 * W], ident)
            T.transpose(T1[0:NS * NCMP, 2 * P:3 * P], Ss[:, 2 * W:2 * W + NS * NCMP], ident).then_inc(spt_done, 1)
            pe.wait_ge(spt_ready, 1)
            pe.wait_ge(past_v_in, 16 * (NS * PAGES + 1))
            pe.wait_ge(s_biased, 2)
            vals = [v[:, 0:SLOT].rearrange("p (b i v) -> p b i v", b=NS, i=PAGES) for v in (slc_v, win_v_past)]
            for b in range(NS):
                out = B[b // 2][0:NH, 256 * (b % 2):256 * (b % 2) + 256]
                for j in range(4):
                    i = T.matmul(out, PTs[:, j, b * NH:(b + 1) * NH], vals[j // 2][:, b, j % 2, :], start=(j == 0), stop=(j == 3))
                if b % 2:
                    i.then_inc(orow_done, 1)
            for c in range(2):
                rows_, v = STAT[:, c * P:(c + 1) * P], slice(c * P, (c + 1) * P)
                T.matmul(rows_, vcs[0:NS * NCMP, v], PTs[0:NS * NCMP, 6, :], start=True, stop=False)
                T.matmul(rows_, vnew[0:NS, 0, v], PTs[0:NS, 4, :], start=False, stop=False)
                if c == 0:
                    pe.wait_ge(orow_ready, 4)
                for b in range(NS):
                    T.matmul(rows_[:, b * NH:(b + 1) * NH], orow[:, 256 * b + c * P:256 * b + c * P + P], ident[0:NH, 0:NH],
                             start=False, stop=False, skip_group_check=True)
                i = T.matmul(rows_, vnew[0:NS, 1, v], PTs[0:NS, 5, :], start=False, stop=True)
            i.then_inc(so_done, 1)
            for h in range(NH):
                if h + 2 < NH:
                    scores(h + 2)
                turn(h)
                if h:
                    weigh(h - 1)
            weigh(NH - 1)
            for c in range(KC):
                if c % 4 == 0:
                    arrived(pe, f"bo{c // 4}")
                if c == 0:
                    pe.wait_ge(o_ready, NH)
                if c >= 4:
                    pe.wait_ge(x_ready, 16 + c - 3)
                for k in range(KC):
                    i = T.matmul(B[c % 4][:, 0:NT], items(f"bo{c // 4}")[:, c % 4, k, :], hB[:, k, :], start=(k == 0), stop=(k == KC - 1))
                i.then_inc(bo_done, 1)
                if c:
                    stat_after(3, c - 1)
            stat_after(3, 7)
            for k in range(KC):
                pe.wait_ge(h_ready, 32 + k + 1)
                T.matmul(MISC[0:NE, 0:NT], w_router[:, k, :], hB[:, k, :], start=(k == 0), stop=False)
            T.matmul(MISC[0:NE, 0:NT], b_router, ones_row, start=False, stop=True).then_inc(lT_done, 1)
            spans = [(0, P), (P, NP), (NP, NT)]
            for t, (a, z) in enumerate(spans):
                for half in range(2):
                    for k in range(4):
                        i = T.transpose(HT[2 * t + half][0:z - a, k * P:(k + 1) * P], hB[:, 4 * half + k, a:z], ident)
                    i.then_inc(ht_done, 1)
                if t == 0:
                    pe.wait_ge(lT_ready, 1)
                    for u, (a_, z_) in enumerate(spans):
                        i = T.transpose(MISC[0:z_ - a_, 8 * u:8 * u + 8], lgT[:, a_:z_], ident[0:NE, 0:NE])
                    i.then_inc(route_done, 1)
            pe.wait_ge(rank_in, 1)
            both = [lg[0:z - a, t, 40:48] for t, (a, z) in enumerate(spans)]
            before, ones = const("before"), const("ones")
            for t, (a, z) in enumerate(spans):
                r = z - a
                out = MISC[0:r, 24 + 8 * t:32 + 8 * t]
                for u in range(t):
                    T.matmul(out, ones[:, 0:r], both[u], start=(u == 0), stop=False)
                T.matmul(out, before[0:r, 0:r], both[t], start=(t == 0), stop=True)
            for t, (a, z) in enumerate(spans):
                i = T.matmul(MISC[:, 48:56], ones[0:z - a, 0:P], both[t], start=(t == 0), stop=(t == 2))
            i.then_inc(rank_done, 1)
            pe.wait_ge(ht_ready, 6)
            pe.wait_ge(blk_ready, 1)
            nblk = pe.value_load(blkinfo[0:1, MAXB:MAXB + 1], min_val=1, max_val=MAXB)

            def gather(t):
                pe.wait_ge(sel_ready, 3 * t + 3)
                for k in range(KC):
                    out = (STAT, MISC)[k // 4][:, (k % 4) * P:(k % 4 + 1) * P]
                    for u, (a, z) in enumerate(spans):
                        i = T.matmul(out, htok[0:z - a, u, k * P:(k + 1) * P], Gm[0:z - a, u, :], start=(u == 0), stop=(u == 2))
                    if k % 4 == 3:
                        i.then_inc(xg_done, 1)

            def combine(t, c):
                if c == 0:
                    pe.wait_ge(yrow_ready, 2 * t + 2)
                    pe.wait_ge(gwT_ready, t + 1)
                if c >= 2:
                    pe.wait_ge(comb_added, t * KC + c - 1)
                T.matmul((STAT, MISC)[c % 2][:, 0:NT], yrow[:, c * P:(c + 1) * P], GwT[:, :], start=True, stop=True)\
                    .then_inc(comb_done, 1)

            gather(0)
            with pe.Fori(0, nblk) as t:

                def turn_hidden(f):
                    pe.wait_ge(hm_ready, t * FT + f + 1)
                    for j in range(2):
                        i = T.transpose((T0, T1)[f % 2][:, j * P:(j + 1) * P], hm[:, f % 2, j * P:(j + 1) * P], ident)
                    i.then_inc(hmT_done, 1)

                n = 0

                def item():
                    nonlocal n
                    pe.wait_ge(lo_ready, t * ITEMS + 2 * NRAW + n + 1)
                    n += 1
                    return (n - 1) % NSPLIT

                def expert_product(out, lhs_hi, lhs_lo, cols, slot, first, last):
                    hi, lo = w_hi[:, slot, cols], w_lo[:, slot, cols]
                    T.matmul(out, lhs_hi, hi, start=first, stop=False)
                    T.matmul(out, lhs_hi, lo, start=False, stop=False)
                    return T.matmul(out, lhs_lo, hi, start=False, stop=last)

                def down(f):
                    pe.wait_ge(hmT_lo, t * FT + f + 1)
                    for j in range(2):
                        slot = item()
                        for half in range(2):
                            i = expert_product(B[2 + half][:, :], hm_hi[:, f % 2, j, :], hm_lo[:, f % 2, j, :],
                                        slice(512 * half, 512 * half + 512), slot, f == 0 and j == 0, f == FT - 1 and j == 1)
                        i.then_inc(item_used, 1)

                for f in range(FT):
                    if f >= 2:
                        pe.wait_ge(hm_ready, t * FT + f - 1)
                    if f == 0:
                        pe.wait_ge(xg_lo_ready, 2 * t + 2)
                    for q in range(4):
                        slot = item()
                        for k in (2 * q, 2 * q + 1):
                            i = expert_product(B[f % 2][:, :], xg_hi[:, k, :], xg_lo[:, k, :],
                                        slice(512 * (k % 2), 512 * (k % 2) + 512), slot, k == 0, k == KC - 1)
                        i.then_inc(item_used, 1)
                    if f < 4:
                        combine(t, 2 * f)
                        combine(t, 2 * f + 1)
                    if f == 4:
                        pe.wait_ge(comb_added, t * KC + KC)
                        pe.wait_ge(gw_sel, 4 * t + 3)
                        for u, (a, z) in enumerate(spans):
                            i = T.transpose(MISC[:, a:z], Gw[0:z - a, u, :], ident[0:z - a, 0:z - a])
                        i.then_inc(gw_done, 1)
                    if f == FT - 1:
                        pe.wait_ge(gwT_ready, t + 2)
                        gather(t + 1)
                    if f >= 1:
                        turn_hidden(f - 1)
                    if f >= 2:
                        down(f - 2)
                turn_hidden(FT - 1)
                down(FT - 2)
                down(FT - 1)
            for c in range(KC):
                combine(nblk, c)
            for k in range(KC):
                stat_after(4, k)


def kernel(**inputs):
    import concourse.bacc as bacc
    from concourse.bass_utils import run_bass_kernel_spmd as run

    a = {k: np.asarray(v) for k, v in inputs.items()}

    def cat(*xs):
        return np.concatenate(xs, axis=-1)

    def chunks(w):
        return w.reshape(-1, P, w.shape[-1]).transpose(1, 0, 2)

    def vec(v):
        return v.reshape(KC, P).T

    def part(rows):
        return np.concatenate([rows, np.zeros((P - rows.shape[0],) + rows.shape[1:], np.float32)], axis=0)

    arrays = {}
    tokens = np.concatenate([a["x_prompt"][0], a["x_sample"][:, 0]], axis=0)
    arrays["x"] = chunks(np.ascontiguousarray(tokens.T))
    ain, aout = chunks(a["a_w_in"][0]), chunks(a["a_w_out"][0])
    fg, fu, fd = chunks(a["f_w_gate"][0]), chunks(a["f_w_up"][0]), chunks(a["f_w_down"][0])
    wkv, bin_, bout = chunks(a["w_kv"]), chunks(a["b_w_in"][0]), chunks(a["b_w_out"][0])

    def columns(w, *firsts):
        w = np.concatenate([w[:, :, c:c + P] for c in firsts], axis=1)
        return w.reshape(P, SLOT)

    def four(w, c):
        return columns(w, c, c + P, c + 2 * P, c + 3 * P)

    tiles = [four(ain, c) for c in (1024, 1536, 0, 512)] + [four(aout, c) for c in (0, 512)]
    gate_up = np.concatenate([fg, fu], axis=2)
    tiles += [columns(gate_up, c, FF + c, c + P, FF + c + P) for c in range(0, FF, 256)]
    down = np.concatenate([fd, np.zeros((P, 24 - FC, DM), np.float32)], axis=1)
    tiles += [four(down[:, 8 * i:8 * i + 8], c) for c in (0, 512) for i in range(3)]
    tiles += [four(wkv, c) for c in (0, 512, 1024)] + [four(bin_, c) for c in (0, 512)] + [four(bout, c) for c in (0, 512)]
    arrays["wd"] = np.stack(tiles)
    mg, mu, md = a["m_w_gate"][0], a["m_w_up"][0], a["m_w_down"][0]
    moe = np.empty((NE, UNITS, P, UNIT), np.float32)
    for u, (f, kind) in enumerate(USE):
        if kind == "d":
            f -= 2
            moe[:, u] = md[:, 256 * f:256 * f + 256].reshape(NE, 2, P, DM).transpose(0, 2, 1, 3).reshape(NE, P, UNIT)
        else:
            k = 512 * (kind == "b")
            for w, o in ((mg, 0), (mu, 256)):
                moe[:, u].reshape(NE, P, 4, 512)[..., o:o + 256] = \
                    w[:, k:k + 512, 256 * f:256 * f + 256].reshape(NE, 4, P, 256).transpose(0, 2, 1, 3)
    arrays["moe"] = moe
    bw, w1_, w2_ = a["b_w_in"][0], a["cmp_w1"], a["cmp_w2"]
    zero = np.zeros((64, 64), np.float32)
    fields = {
        "mix0": vec(a["norm_mix"][0]), "mix1": vec(a["norm_mix"][1]), "ffn0": vec(a["norm_ffn"][0]),
        "lng": vec(a["a_ln_g"][0]), "lnb": vec(a["a_ln_b"][0]), "kvn": vec(a["kv_norm"]),
        "pe": a["cmp_pe"].reshape(32, P).T, "w00": np.broadcast_to(a["a_w_s"][0, :, 0, 0][None, :], (P, 8)),
        "gate": chunks(bw[:, 1024:]).reshape(P, -1),
        "w1": w1_.reshape(2, 2, 8, P, 64).transpose(3, 0, 2, 1, 4).reshape(P, -1),
        "w2k": part(np.concatenate([w2_[0], zero, zero, w2_[0]], axis=1)), "w2v": part(w2_[1]),
        "bgate": np.broadcast_to(a["b_b_gate"], (P, 48)),
    }
    arrays["vectors"] = cat(*[fields[k] for k in VECTORS])
    arrays["params"] = cat(*[fields[k] for k in PARAMS])
    arrays["late"] = cat(vec(a["norm_ffn"][1]), vec(a["norm_final"]), chunks(a["m_w_router"][0]).reshape(P, -1),
                         np.broadcast_to(a["m_b_router"], (P, NE)))
    bs = a["a_b_s"][0]
    arrays["spatial"] = a["a_w_s"][0].transpose(2, 0, 1)
    arrays["spatial_bias"] = cat(bs, bs, np.repeat(bs[:, 0:1], NS, axis=1))[None]
    arrays["consts"] = constants()
    cache = a["cache_kv"]
    n_phys = cache.shape[0]
    arrays["cmp_pages"] = cache[:, :, 0:2].reshape(n_phys, 64, 2, 2, NG, HD).transpose(0, 2, 5, 3, 4, 1).reshape(n_phys, P, 2, NG * 64)
    arrays["k_pages"] = cache[:, :, 2].reshape(n_phys, P, 2, P).transpose(0, 3, 2, 1)
    arrays["v_pages"] = cache[:, :, 3].reshape(n_phys, P, NG * HD)
    win = a["state_win_kv"]
    arrays["win_k"] = win[:, :, 0].reshape(NS, PAST, 2, P).transpose(3, 0, 2, 1).reshape(P, SLOT)
    arrays["win_v"] = win[:, :, 1].reshape(NS, PAGES, P, NG * HD).transpose(2, 0, 1, 3).reshape(P, SLOT)
    arrays["state_win"] = win.reshape(P, -1)
    arrays["page_table"] = a["page_table"].reshape(1, -1)

    nc = bacc.Bacc("TRN2", target_bir_lowering=False, num_devices=1)
    args = []
    for name in list(arrays):
        arrays[name] = np.ascontiguousarray(arrays[name])
        args.append(nc.dram_tensor(f"in_{name}", arrays[name].shape, mybir.dt.from_np(arrays[name].dtype), kind="ExternalInput").ap())
    outs = [("y", (P, KC, NT)), ("v", (P, KC, NT)), ("kv", (P, 12, NT)), ("past", (P, NS * PAST * 512 // P))]
    for name, shape in outs:
        args.append(nc.dram_tensor(f"out_{name}", shape, F32, kind="ExternalOutput").ap())
    build(nc, *args)
    r = run(nc, [{f"in_{k}": v for k, v in arrays.items()}], core_ids=[0]).results[0]
    y, v, kv, past = (np.asarray(r[f"out_{name}"]) for name, _ in outs)

    def tokens_of(z):
        return z.transpose(2, 1, 0).reshape(NT, -1)

    y, v, kv = tokens_of(y), tokens_of(v), tokens_of(kv)
    kv_rows, win_rows = kv[:, 0:1024].reshape(NT, 4, NG, HD), kv[:, 1024:1536].reshape(NT, 2, NG, HD)
    win_sample = np.concatenate([past.reshape(NS, PAST, 2, NG, HD), win_rows[NP:][:, None]], axis=1)
    return (y[None, 0:NP], y[NP:][:, None], kv_rows[None, 0:NP], kv_rows[NP:][:, None], win_rows[None, 0:NP], win_sample,
            v[None, None, P:NP], v[NP:][None, :, None])
```

```python
from contextlib import ExitStack

import numpy as np

import concourse.bass as bass
from concourse import mybir

F32 = mybir.dt.float32
I32 = mybir.dt.int32
F32R = mybir.dt.float32r
ALU = mybir.AluOpType
ACT = mybir.ActivationFunctionType
AX_X = mybir.AxisListType.X

P = 128
DM = 1024
KC = DM // P
NP = 256
NS = 8
NT = NP + NS
PAST = 256
HD = 64
NH = 16
NG = 4
FF = 2816
FC = FF // P
FT = FF // 256
NE = 8
ROWS = 128
MAXB = 12
NCMP = 15
CMP_LEN, CMP_STRIDE = 32, 16
RMS_EPS, LN_EPS = 1e-6, 1e-5
BIG = 1e30
SLOT = 4096
UNIT, ITEM = 2048, 1024
USE = [(f, kind) for f in range(FT + 2) for kind in "abd" if (f < FT if kind != "d" else f >= 2)]
UNITS = len(USE)
ITEMS = 2 * UNITS
UP_END = {f: 2 * u + 2 for u, (f, kind) in enumerate(USE) if kind == "b"}
DOWN_END = {f - 2: 2 * u + 2 for u, (f, kind) in enumerate(USE) if kind == "d"}
NRAW = 11
NSPLIT = 6
AHEAD = 2
PAGES = 2
X2W = NS * PAGES * NG * HD + NG * NP // 2 + CMP_LEN // 2

SLOPE = [2.0 ** (-8.0 * (h + 1) / NH) for h in range(NH)]


def layout(widths):
    at, out = 0, {}
    for name, w in widths:
        out[name] = (at, at + w)
        at += w
    return out, at


CONSTS, NC_ = layout([("ident", P), ("ones", P), ("before", P), ("upto", P), ("dist", 414),
                      ("cmpmask", 30), ("sdist", PAST + NS), ("scdist", NS * NCMP), ("negslope", 1),
                      ("iota", P), ("down8", NE), ("blk", MAXB * NE)])
VECTORS, NVEC = layout([("mean", P), ("eps", 2), ("mix0", 8), ("mix1", 8), ("ffn0", 8), ("lng", 8), ("lnb", 8), ("kvn", 8), ("w00", 8)])
PARAMS, NPAR = layout([("pe", 32), ("gate", 8 * 48), ("w1", 2048),
                       ("w2k", 256), ("w2v", 64), ("bgate", 1)])
LATE, NLATE = layout([("ffn1", 8), ("final", 8), ("router", 64), ("brouter", 8)])


def constants():
    c = np.zeros((P, NC_), np.float32)

    def put(name, v):
        a, b = CONSTS[name]
        c[:, a:b] = v

    p = np.arange(P)[:, None]
    f = np.arange(P)[None, :]
    put("ident", p == f)
    put("ones", 1.0)
    put("before", p < f)
    put("upto", p <= f)
    ends = np.arange(NCMP) * CMP_STRIDE + CMP_LEN - 1
    d = np.concatenate([p - f, p + P - np.arange(NP)[None, :], p - ends[None, :], p + P - ends[None, :]], axis=1)
    put("dist", np.where(d >= 0, d, BIG))
    put("cmpmask", d[:, 384:414] >= 0)
    own = (p // NH) == np.arange(NS)[None, :]
    put("sdist", np.concatenate([np.broadcast_to(PAST - np.arange(PAST)[None, :], (P, PAST)), np.where(own, 0.0, BIG)], axis=1))
    put("scdist", np.where(np.repeat(own, NCMP, axis=1), np.tile(PAST - ends, NS)[None, :], BIG))
    put("negslope", -np.array(SLOPE, np.float32)[np.arange(P) % NH][:, None])
    put("iota", f)
    put("down8", NE - np.arange(NE)[None, :])
    put("blk", np.repeat(np.arange(MAXB), NE)[None, :])
    return c


TILES = (["v0", "v1", "u0", "u1", "ao0", "ao1"] + [f"gu{i}" for i in range(FT)]
         + [f"dn{i}" for i in range(6)] + ["kv0", "kv1", "kv2", "bi0", "bi1", "SK", "WK", "bo0", "bo1"])
WTILES = [t for t in TILES if t[1] not in "KV"]
INDEX = {t: n for n, t in enumerate(TILES)}
NSLOT = 2
DITEM = KC * P
NDS = 3
FIRST, NDENSE = {}, 0
for stage, items in (("vu", 16), ("ao", 8), ("gu", 2 * FC), ("dn", 24), ("kv", 12), ("q", 8), ("bo", 8)):
    FIRST[stage] = NDENSE
    NDENSE += items


def build(nc, xT, wd, moe, vectors, params, late_in, spatial, spatial_bias, consts, cmp_pages, k_pages, v_pages,
          win_k, win_v, state_win, page_table, y_out, v_out, kv_out, past_out):
    with ExitStack() as ctx:
        def sb(name, shape, dt=F32):
            return ctx.enter_context(nc.sbuf_tensor(name, shape, dt))

        def sem(name):
            return ctx.enter_context(nc.semaphore(name))

        C = sb("consts_sb", [P, NC_])
        LT = sb("late_sb", [P, NLATE])
        VE = sb("vectors_sb", [P, NVEC])
        x = sb("x", [P, KC, NT])
        hB = sb("hB", [P, KC, NT])
        rstd = sb("rstd", [P, NT])
        total = sb("total", [P, NT])
        pages = sb("pages", [1, NS * PAGES], I32)
        blkinfo = sb("blkinfo", [1, 16], I32)

        dense_memory = ctx.enter_context(ExitStack())

        def sbd(name, shape, dt=F32):
            return dense_memory.enter_context(nc.sbuf_tensor(name, shape, dt))

        with ExitStack() as hidden_memory:
            hF_hi = hidden_memory.enter_context(nc.sbuf_tensor("hF_hi", [P, FC, NT], F32R))
            hF_lo = hidden_memory.enter_context(nc.sbuf_tensor("hF_lo", [P, FC, NT], F32R))
            sil = hidden_memory.enter_context(nc.sbuf_tensor("sil", [P, 2, NT], F32))
        ARENA = 19900
        arena = sbd("arena", [P, ARENA])
        PR = sbd("params_sb", [P, NPAR])
        with ExitStack() as normed_memory:
            hA_hi = normed_memory.enter_context(nc.sbuf_tensor("hA_hi", [P, KC, NT], F32R))
            hA_lo = normed_memory.enter_context(nc.sbuf_tensor("hA_lo", [P, KC, NT], F32R))
        X2v = sbd("X2v", [P, X2W])
        with ExitStack() as query_memory:
            hC_hi = query_memory.enter_context(nc.sbuf_tensor("hC_hi", [P, KC, NT], F32R))
            hC_lo = query_memory.enter_context(nc.sbuf_tensor("hC_lo", [P, KC, NT], F32R))
        slc_v = sbd("slc_v", [P, 2 * KC * NT])
        ring = sbd("ring", [P, NSLOT, SLOT])
        with ExitStack() as split_memory:
            d_hi = split_memory.enter_context(nc.sbuf_tensor("d_hi", [P, NDS, DITEM], F32R))
            d_lo = split_memory.enter_context(nc.sbuf_tensor("d_lo", [P, NDS, DITEM], F32R))
        win_v_past = sbd("win_v_past", [P, SLOT])
        sq3 = slc_v[:, 0:KC * NT].rearrange("p (k t) -> p k t", t=NT)
        top = [0]

        def carve(*shape):
            n = int(np.prod(shape))
            v = arena[:, top[0]:top[0] + n]
            top[0] += n
            assert top[0] <= ARENA, top[0]
            if len(shape) == 2:
                v = v.rearrange("p (a b) -> p a b", b=shape[1])
            if len(shape) == 3:
                v = v.rearrange("p (a b c) -> p a b c", b=shape[1], c=shape[2])
            return v

        uT = carve(KC, NT)
        vT = carve(KC, NT)
        vtok = carve(3, DM)
        wsT = carve(8, P)
        dg = carve(8, NS)
        mu = carve(NT)
        w_s = carve(8, P)
        b_s = carve(8, NT)
        top[0] = 0
        kvT = carve(12, NT)
        Q = carve(NH, NT)
        qz_at = top[0]
        Qz = carve(2, NS, P)
        orow = arena[0:NH, qz_at:qz_at + NS * 2 * P]
        Qc = carve(2, P)
        vtp = carve(2, 2, 2 * P)
        vnew = carve(2, 2 * P)
        gT = carve(NT)
        gtok = carve(2, 48)
        gsam = carve(48)
        grow = carve(3)
        hidb = carve(580)
        hid = carve(36, NCMP)
        cbias = carve(1)
        kcT = carve(18, NCMP)
        vcs = carve(2 * P)
        vcp = carve(2 * P)
        x2_at = top[0]
        X2 = [carve(X2W), X2v[:]]
        top[0] = x2_at
        Sh = carve(3, 828)
        mx = carve(3, 6)
        sm = carve(3, 6)
        wt = carve(3, 6)
        PT = carve(2, 2, 512)
        Ss = carve(2 * (PAST + NS) + NS * NCMP)
        smx, ssm, swt = carve(3), carve(3), carve(3)
        PTs = carve(7, P)
        dense_memory.close()
        raw = sb("raw", [P, NRAW, UNIT])
        w_hi = sb("w_hi", [P, NSPLIT, ITEM], F32R)
        w_lo = sb("w_lo", [P, NSPLIT, ITEM], F32R)
        xg_hi = sb("xg_hi", [P, KC, P], F32R)
        xg_lo = sb("xg_lo", [P, KC, P], F32R)
        hm_hi = sb("hm_hi", [P, 2, 2, P], F32R)
        hm_lo = sb("hm_lo", [P, 2, 2, P], F32R)
        htok = sb("htok", [P, 3, DM])
        yrow = sb("yrow", [P, DM])
        Gm = sb("Gm", [P, 3, P])
        Gw = sb("Gw", [P, 3, P])
        Gt = sb("Gt", [P, 3, P])
        GwT = sb("GwT", [P, NT])
        sg = sb("sg", [P, 2, 256])
        hm = sb("hm", [P, 2, 256])
        lgT = sb("lgT", [NE, NT])
        lg = sb("lg", [P, 3, 64])
        sc = sb("sc", [P, 3, 16])
        cnt = sb("cnt", [P, 64])
        bcmp = sb("bcmp", [1, MAXB * NE])
        bout = sb("bout", [1, 16])
        sq_last = htok[:].rearrange("p a b -> p (a b)")[:, 0:KC * NT].rearrange("p (k t) -> p k t", t=NT)

        def const(name):
            a, b = CONSTS[name]
            return C[:, a:b]

        def par(name):
            a, b = PARAMS[name]
            return PR[:, a:b]

        def vector(name):
            a, b = VECTORS[name]
            return VE[:, a:b]

        def late(name):
            a, b = LATE[name]
            return LT[:, a:b]

        ident = const("ident")
        w1 = par("w1").rearrange("p (v m e) -> p v m e", v=2, e=P)
        w_gate = par("gate").rearrange("p (k n) -> p k n", k=KC)
        w_router = late("router").rearrange("p (k n) -> p k n", k=KC)
        w2k = par("w2k").rearrange("p (a n) -> p a n", a=2)
        b_router = late("brouter")

        B = [ctx.enter_context(nc.psum_tensor(f"bank{i}", [P, 512], F32)) for i in range(8)]
        STAT, T0, T1, MISC = B[4], B[5], B[6], B[7]
        HT = [B[0], B[1], B[2], B[3], T0, T1]

        slot_in = [sem(f"slot_in{i}") for i in range(NSLOT)]
        setup_in = sem("setup_in")
        spatial_in, params_in = sem("spatial_in"), sem("params_in")
        x_in = sem("x_in")
        pages_in = sem("pages_in")
        past_v_in = sem("past_v_in")
        cmp_in = [sem("cmp_k_in"), sem("cmp_v_in")]
        x_ready = sem("x_ready")
        sq_ready = sem("sq_ready")
        sum_step = sem("sum_step")
        std_ready = sem("std_ready")
        mean_done = sem("mean_done")
        norm_ready = sem("norm_ready")
        h_hi_ready = sem("h_hi_ready")
        h_ready = sem("h_ready")
        d_hi_ready = sem("d_hi_ready")
        d_lo_ready = sem("d_lo_ready")
        dense_done = sem("dense_done")
        dve_step = sem("dve_step")
        v_ready, u_ready = sem("v_ready"), sem("u_ready")
        ctr_ready, csq_ready, vn_ready = sem("ctr_ready"), sem("csq_ready"), sem("vn_ready")
        vt_done, vt_ready, ws_ready = sem("vt_done"), sem("vt_ready"), sem("ws_ready")
        mix_done, gated = sem("mix_done"), sem("gated")
        mixed = sem("mixed")
        gated_hi, gated_lo = sem("gated_hi"), sem("gated_lo")
        sil_ready, hF_ready, hF_hi_ready, hF_lo_ready = sem("sil_ready"), sem("hF_ready"), sem("hF_hi_ready"), sem("hF_lo_ready")
        kv_ready = sem("kv_ready")
        q_even, q_odd = sem("q_even"), sem("q_odd")
        gp_done, sig_ready, gt_done, gtok_ready, grow_in = (sem("gp_done"), sem("sig_ready"), sem("gt_done"),
                                                            sem("gtok_ready"), sem("grow_in"))
        vp_done, vp_ready = sem("vp_done"), sem("vp_ready")
        q_zero, q_rows = sem("q_zero"), sem("q_rows")
        x2_ready = sem("x2_ready")
        cmp_done, bhalf_ready, pre_ready, hid_ready, cmp2_done, cmp2_ready = (
            sem("cmp_done"), sem("bhalf_ready"), sem("pre_ready"), sem("hid_ready"), sem("cmp2_done"), sem("cmp2_ready"))
        s_done, s_biased, neg_max, exps, p_ready, pt_done, pt_ready, o_done, o_ready = (
            sem("s_done"), sem("s_biased"), sem("neg_max"), sem("exps"), sem("p_ready"), sem("pt_done"),
            sem("pt_ready"), sem("o_done"), sem("o_ready"))
        ss_done, ss_max, ss_exp, sp_ready, spt_done, spt_ready, so_done, so_ready, orow_done, orow_ready = (
            sem("ss_done"), sem("ss_max"), sem("ss_exp"), sem("sp_ready"), sem("spt_done"), sem("spt_ready"),
            sem("so_done"), sem("so_ready"), sem("orow_done"), sem("orow_ready"))
        out_hi, out_lo = sem("out_hi"), sem("out_lo")
        sk_used, t_zeroed, lT_done, lT_ready = sem("sk_used"), sem("t_zeroed"), sem("lT_done"), sem("lT_ready")
        route_done, ht_done, ht_ready, rank_in, rank_done, blk_ready, exp_ready = (
            sem("route_done"), sem("ht_done"), sem("ht_ready"), sem("rank_in"), sem("rank_done"), sem("blk_ready"), sem("exp_ready"))
        raw_in = [sem(f"raw_in{i}") for i in range(NRAW)]
        hi_ready, lo_ready, item_used = sem("hi_ready"), sem("lo_ready"), sem("item_used")
        dve_sel, gw_sel = sem("dve_sel"), sem("gw_sel")
        sel_ready, gw_done, gwT_ready, xg_done, xg_hi_ready, xg_lo_ready = (sem("sel_ready"), sem("gw_done"), sem("gwT_ready"),
                                                            sem("xg_done"), sem("xg_hi_ready"), sem("xg_lo_ready"))
        sg_ready, hm_ready, hmT_done, hmT_hi, hmT_lo, yrow_ready = (
            sem("sg_ready"), sem("hm_ready"), sem("hmT_done"), sem("hmT_hi"), sem("hmT_lo"),
            sem("yrow_ready"))
        comb_done, comb_added = sem("comb_done"), sem("comb_added")
        v_stored, kv_stored, past_stored, y_stored = sem("v_stored"), sem("kv_stored"), sem("past_stored"), sem("y_stored")

        used = {t: (d_lo_ready, 4 * n + 4) for n, t in enumerate(WTILES)}
        used |= {"SK": (sk_used, 1), "WK": (sk_used, 2)}

        landed, filled = {}, [0] * NSLOT
        for n, t in enumerate(TILES):
            filled[n % NSLOT] += 16 * (NS * PAGES if t == "SK" else 1)
            landed[t] = filled[n % NSLOT]

        def arrived(eng, t):
            eng.wait_ge(slot_in[INDEX[t] % NSLOT], landed[t])

        def tile(t):
            return ring[:, INDEX[t] % NSLOT, :]

        def items(t):
            return tile(t).rearrange("p (j k n) -> p j k n", j=4, k=KC)

        def raw_item(n):
            return ring[:, INDEX[WTILES[n // 4]] % NSLOT, DITEM * (n % 4):DITEM * (n % 4 + 1)]

        def ahead_of(stage, c):
            return min(FIRST[stage] + c + 3, FIRST["bo"] if stage != "bo" else NDENSE)

        def projected(eng, stage, c):
            eng.wait_ge(dense_done, FIRST[stage] + c + 1)

        block = ctx.enter_context(nc.Block())

        @block.sync
        def _(sp):
            sp.dma_start(x[:], xT).then_inc(x_in, 16)
            sp.dma_start(VE[:], vectors).then_inc(setup_in, 16)
            wn = 0

            def page(b, i):
                return sp.value_load(pages[0:1, b * PAGES + i:b * PAGES + i + 1], min_val=0, max_val=k_pages.shape[0] - 1)

            for n, t in enumerate(TILES):
                if n >= NSLOT:
                    sp.wait_ge(*used[TILES[n - NSLOT]])
                done = slot_in[n % NSLOT]
                if t == "SK":
                    sp.wait_ge(pages_in, 16)
                    for b in range(NS):
                        for i in range(PAGES):
                            pg = page(b, i)
                            dst = tile(t).rearrange("p (b c i k) -> p b c i k", b=NS, c=2, i=PAGES)[:, b, :, i, :]
                            sp.dma_start(dst, k_pages[bass.ds(pg, 1)].rearrange("o p c k -> p (o c) k")).then_inc(done, 16)
                elif t == "WK":
                    sp.dma_start(tile(t), win_k).then_inc(done, 16)
                    projected(sp, "q", 7)
                    for b in range(NS):
                        for i in range(PAGES):
                            pg = page(b, i)
                            c = (b * PAGES + i) * 2 * P
                            sp.dma_start(slc_v[:, c:c + 2 * P], v_pages[bass.ds(pg, 1)].rearrange("o p v -> (o p) v"))\
                              .then_inc(past_v_in, 16)
                    sp.dma_start(win_v_past[:], win_v).then_inc(past_v_in, 16)
                else:
                    sp.dma_start(ring[:, n % NSLOT, :], wd[wn]).then_inc(done, 16)
                    wn += 1
                if n == NSLOT - 1:
                    sp.dma_start(C[:], consts).then_inc(spatial_in, 16)
                    sp.dma_start(w_s, spatial).then_inc(spatial_in, 16)
                    sp.dma_start(b_s, spatial_bias).then_inc(spatial_in, 16)
                    sp.dma_start(pages[:], page_table).then_inc(pages_in, 16)
                    sp.dma_start(PR[:], params).then_inc(params_in, 16)
                    sp.dma_start(LT[:], late_in).then_inc(params_in, 16)
            sp.sem_inc(lo_ready, 2 * NRAW)
            sp.sem_inc(item_used, NSPLIT)
            sp.wait_ge(o_done, NH)
            sp.wait_ge(so_ready, 1)
            sp.wait_ge(kv_stored, 16)
            for u in range(UNITS):
                if u >= NRAW:
                    sp.wait_ge(lo_ready, 2 * u + 2)
                sp.dma_start(raw[:, u % NRAW, :], moe[0, u]).then_inc(raw_in[u % NRAW], 16)
            sp.wait_ge(blk_ready, 1)
            nblk = sp.value_load(blkinfo[0:1, MAXB:MAXB + 1], min_val=2, max_val=MAXB)
            with sp.Fori(1, nblk) as t:
                e = sp.value_load(blkinfo[0:1, bass.ds(t, 1)], min_val=0, max_val=NE - 1)
                for u in range(UNITS):
                    sp.wait_ge(lo_ready, t * ITEMS + 2 * u + 2)
                    sp.dma_start(raw[:, u % NRAW, :], moe[bass.ds(e, 1), u].rearrange("o p n -> (o p) n"))\
                      .then_inc(raw_in[u % NRAW], 16)
            sp.wait_ge(lo_ready, nblk * ITEMS + 2 * NRAW)
            for u in range(AHEAD // 2):
                sp.sem_inc(raw_in[u], 16)
            for half in range(2):
                sp.wait_ge(h_ready, 44 + 4 * half)
                sp.dma_start(y_out[:, 4 * half:4 * half + 4, :], hB[:, 4 * half:4 * half + 4, :]).then_inc(y_stored, 16)
            sp.wait_ge(y_stored, 32)
            for stored in (v_stored, kv_stored, past_stored):
                sp.wait_ge(stored, 16)

        @block.gpsimd
        def _(pool):
            pool.wait_ge(vn_ready, 8)
            pool.dma_start(v_out, vT).then_inc(v_stored, 16)
            pool.dma_start(past_out, state_win).then_inc(past_stored, 16)
            pool.wait_ge(pages_in, 16)
            for v in range(2):
                if v == 0:
                    projected(pool, "dn", 23)
                else:
                    nc.gpsimd.memset(Q[:], 0.0).then_inc(q_zero, 1)
                    nc.gpsimd.memset(Qz[:], 0.0).then_inc(q_zero, 1)
                    nc.gpsimd.memset(Qc[:], 0.0).then_inc(q_zero, 1)
                    projected(pool, "kv", 11)
                for b in range(NS):
                    for i in range(PAGES):
                        pg = pool.value_load(pages[0:1, b * PAGES + i:b * PAGES + i + 1], min_val=0,
                                             max_val=cmp_pages.shape[0] - 1)
                        c = (b * PAGES + i) * NG * HD
                        pool.dma_start(X2[v][:, c:c + NG * HD],
                                       cmp_pages[bass.ds(pg, 1), :, v].rearrange("o p n -> (o p) n")).then_inc(cmp_in[v], 16)
            pool.wait_ge(kv_ready, 12)
            pool.dma_start(kv_out, kvT).then_inc(kv_stored, 16)
            pool.wait_ge(gtok_ready, 2)
            pool.dma_start(grow[:], gsam[0:NS, :]).then_inc(grow_in, 16)

        @block.scalar
        def _(act):
            def std(n, eps):
                act.wait_ge(mean_done, n)
                nc.scalar.activation(rstd[:, :], STAT[:, 0:NT], ACT.Sqrt, bias=vector("eps")[:, eps:eps + 1]).then_inc(std_ready, 1)

            def squares(norm, k, dst=hB):
                act.wait_ge(x_ready, 8 * norm + k - 7)
                nc.scalar.activation(dst[:, k, :], x[:, k, :], ACT.Square).then_inc(sq_ready, 1)

            rounded = [0]

            def round_to(stage, c):
                while rounded[0] < ahead_of(stage, c):
                    n = rounded[0]
                    if n % 4 == 0:
                        arrived(act, WTILES[n // 4])
                    if n >= NDS:
                        act.wait_ge(dense_done, n - NDS + 1)
                    nc.scalar.copy(d_hi[:, n % NDS, :], raw_item(n)).then_inc(d_hi_ready, 1)
                    rounded[0] += 1

            def round_normed(norm, dst):
                for k in range(KC):
                    act.wait_ge(norm_ready, 8 * norm + k + 1)
                    nc.scalar.copy(dst[:, k, :], hB[:, k, :]).then_inc(h_hi_ready, 1)

            act.wait_ge(x_in, 16)
            for k in range(KC):
                nc.scalar.activation(hB[:, k, :], x[:, k, :], ACT.Square).then_inc(sq_ready, 1)
            act.wait_ge(setup_in, 16)
            std(1, 0)
            round_to("vu", -1)
            round_normed(0, hA_hi)
            for c in range(KC):
                round_to("vu", c)
                projected(act, "vu", c)
                nc.scalar.activation(vT[:, c, :], B[c % 4][:, 0:NT], ACT.Gelu_apprx_tanh).then_inc(v_ready, 1)
            for c in range(KC):
                round_to("vu", KC + c)
                projected(act, "vu", KC + c)
                nc.scalar.activation(uT[:, c, :], B[c % 4][:, 0:NT], ACT.Gelu_apprx_tanh).then_inc(u_ready, 1)
                if c in (1, 2):
                    for k in range(4 * c - 4, 4 * c):
                        act.wait_ge(ctr_ready, k + 1)
                        nc.scalar.activation(hB[:, k, :], vT[:, k, :], ACT.Square).then_inc(csq_ready, 1)
                if c == 4:
                    std(3, 1)
            for i in range(6):
                if i % 2:
                    r = P if i < 4 else NS
                    act.wait_ge(vt_done, i + 1)
                    nc.scalar.copy(vtok[0:r, i // 2, 512:1024], T1[0:r, :]).then_inc(vt_ready, 1)
            for g in range(8):
                act.wait_ge(gated, g + 1)
                nc.scalar.copy(hC_hi[:, g, :], hB[:, g, :]).then_inc(gated_hi, 1)
            for c in range(KC):
                round_to("ao", c)
                squares(1, c)
            std(4, 0)
            round_normed(1, hA_hi)

            def round_hidden(f):
                act.wait_ge(hF_ready, f + 1)
                nc.scalar.copy(hF_hi[:, f, :], hB[:, f % 4, :]).then_inc(hF_hi_ready, 1)

            for f in range(FC):
                round_to("gu", 2 * f)
                projected(act, "gu", 2 * f)
                if f >= 2:
                    act.wait_ge(hF_ready, f - 1)
                nc.scalar.activation(sil[:, f % 2, :], B[2 * (f % 2)][:, 0:NT], ACT.Silu).then_inc(sil_ready, 1)
                if f:
                    round_hidden(f - 1)
            round_to("gu", 2 * FC - 1)
            round_hidden(FC - 1)
            for c in range(KC):
                round_to("dn", 12 * (c // 4) + 8 + c % 4)
                squares(2, c)
            std(5, 0)
            round_normed(2, hA_hi)
            round_normed(3, hC_hi)
            for c in range(12):
                round_to("kv", c)
                projected(act, "kv", c)
                nc.scalar.copy(kvT[:, c, :], B[c % 4][:, 0:NT]).then_inc(kv_ready, 1)
            act.wait_ge(q_zero, 1)
            for c in range(KC):
                half = 64 * ((c // 2) % 2)
                round_to("q", c)
                projected(act, "q", c)
                nc.scalar.mul(Q[half:half + 64, 2 * c + 1, :], B[c % 4][64:128, 0:NT], HD ** -0.5).then_inc(q_odd, 1)
            act.wait_ge(gp_done, 1)
            nc.scalar.activation(gT[0:48, :], MISC[0:48, 0:NT], ACT.Sigmoid, bias=par("bgate")[0:48, :]).then_inc(sig_ready, 1)
            for v in range(2):
                act.wait_ge(cmp_done, v + 1)
                if v:
                    act.wait_ge(pre_ready, 1)
                nc.scalar.copy(hidb[0:64, 0:512], B[2 * v][64:128, :]).then_inc(bhalf_ready, 1)
                nc.scalar.copy(hidb[0:64, 512:578], B[2 * v + 1][64:128, 0:66]).then_inc(bhalf_ready, 1)
                act.wait_ge(pre_ready, v + 1)
                nc.scalar.activation(hid[0:64], hid[0:64], ACT.Gelu_apprx_tanh, bias=cbias[0:64, :]).then_inc(hid_ready, 1)
            act.wait_ge(ss_max, 1)
            W = PAST + NS
            for j, (a, z) in enumerate([(0, W), (W, 2 * W), (2 * W, 2 * W + NS * NCMP)]):
                i = nc.scalar.activation(Ss[:, a:z], Ss[:, a:z], ACT.Exp, bias=smx[:, j:j + 1], accum_out=ssm[:, j:j + 1])
            i.then_inc(ss_exp, 1)

            def exp_head(h):
                b = h % 3
                act.wait_ge(neg_max, h + 1)
                S = Sh[:, b, :]
                for j, (a, z) in enumerate([(0, 128), (414, 542), (128, 384), (542, 798), (384, 399), (399, 414)]):
                    i = nc.scalar.activation(S[:, a:z], S[:, a:z], ACT.Exp, bias=mx[:, b, j:j + 1],
                                             accum_out=sm[:, b, j:j + 1])
                i.then_inc(exps, 1)

            def head_out(h):
                act.wait_ge(o_done, h + 1)
                half = 64 * (h % 2)
                nc.scalar.copy(hB[half:half + 64, h // 2, 0:NP], (STAT, MISC)[h % 2][0:64, 0:NP]).then_inc(o_ready, 1)

            def round_out(c):
                act.wait_ge(so_ready, 1)
                act.wait_ge(o_ready, 2 * c + 2)
                nc.scalar.copy(hA_hi[:, c, :], hB[:, c, :]).then_inc(out_hi, 1)

            exp_head(0)
            exp_head(1)
            for j in (0, 2):
                act.wait_ge(orow_done, j + 1)
                nc.scalar.copy(orow[:, 512 * j:512 * j + 512], B[j][0:NH, :]).then_inc(orow_ready, 1)
            for h in range(NH):
                act.wait_ge(pt_done, 2 * h + 2)
                if h >= 2:
                    act.wait_ge(o_done, h - 1)
                nc.scalar.copy(PT[:, h % 2, 0, :], T0[:, :]).then_inc(pt_ready, 1)
                nc.scalar.copy(PT[:, h % 2, 1, :], T1[:, :]).then_inc(pt_ready, 1)
                if h + 2 < NH:
                    exp_head(h + 2)
                if h >= 1:
                    head_out(h - 1)
                if h and h % 2 == 0:
                    round_out(h // 2 - 1)
                if h >= NH - 2:
                    round_to("bo", h - NH)
            head_out(NH - 1)
            round_out(KC - 1)
            for c in range(KC):
                round_to("bo", c)
                squares(3, c, sq3)
            std(6, 0)
            act.wait_ge(lT_done, 1)
            nc.scalar.copy(lgT[:, :], MISC[0:NE, 0:NT]).then_inc(lT_ready, 1)
            act.wait_ge(kv_stored, 16)
            for t in range(3):
                r = P if t < 2 else NS
                for half in range(2):
                    act.wait_ge(ht_done, 2 * t + half + 1)
                    nc.scalar.copy(htok[0:r, t, 512 * half:512 * half + 512], HT[2 * t + half][0:r, :]).then_inc(ht_ready, 1)
            act.wait_ge(rank_in, 1)
            nc.scalar.activation(sc[:, :, 4:5], sc[:, :, 3:4], ACT.Exp).then_inc(exp_ready, 1)
            def round_item(t, i):
                u = i // 2
                if i % 2 == 0:
                    act.wait_ge(raw_in[u % NRAW], t * (16 * UNITS // NRAW) + 16 * (u // NRAW + 1))
                act.wait_ge(item_used, t * ITEMS + i + 1)
                nc.scalar.copy(w_hi[:, i % NSPLIT, :], raw[:, u % NRAW, ITEM * (i % 2):ITEM * (i % 2) + ITEM])\
                    .then_inc(hi_ready, 1)

            for i in range(AHEAD):
                round_item(0, i)
            act.wait_ge(blk_ready, 1)
            nblk = act.value_load(blkinfo[0:1, MAXB:MAXB + 1], min_val=1, max_val=MAXB)

            def gathered(t, half):
                act.wait_ge(xg_done, 2 * t + half + 1)
                nc.scalar.copy(xg_hi[:, 4 * half:4 * half + 4, :], (STAT, MISC)[half][:, :].rearrange("p (k n) -> p k n", n=P))\
                    .then_inc(xg_hi_ready, 1)

            def rows_out(t):
                act.wait_ge(item_used, t * ITEMS + NSPLIT)
                act.wait_ge(comb_done, t * KC)
                nc.scalar.copy(yrow[:, 0:512], B[2][:, :]).then_inc(yrow_ready, 1)
                nc.scalar.copy(yrow[:, 512:1024], B[3][:, :]).then_inc(yrow_ready, 1)

            gathered(0, 0)
            gathered(0, 1)
            with act.Fori(0, nblk) as t:
                def transposed(f):
                    act.wait_ge(hmT_done, t * FT + f + 1)
                    if f >= 2:
                        act.wait_ge(item_used, t * ITEMS + NSPLIT + DOWN_END[f - 2])
                    nc.scalar.copy(hm_hi[:, f % 2, :, :], (T0, T1)[f % 2][:, 0:256].rearrange("p (k n) -> p k n", n=P))\
                        .then_inc(hmT_hi, 1)

                n = AHEAD
                for _ in range(2):
                    round_item(t, n)
                    n += 1
                rows_out(t)
                for f in range(FT):
                    for _ in range(2 * (f >= 2) + 4 * (f + 1 < FT)):
                        round_item(t, n)
                        n += 1
                    act.wait_ge(item_used, t * ITEMS + NSPLIT + UP_END[f])
                    nc.scalar.activation(sg[:, f % 2, :], B[f % 2][:, 0:256], ACT.Silu).then_inc(sg_ready, 1)
                    if f:
                        transposed(f - 1)
                for _ in range(2):
                    round_item(t, n)
                    n += 1
                gathered(t + 1, 0)
                transposed(FT - 1)
                round_item(t, n)
                n += 1
                gathered(t + 1, 1)
                round_item(t, n)
                n += 1
                for i in range(AHEAD):
                    round_item(t + 1, i)
            rows_out(nblk)
            for k in range(KC):
                act.wait_ge(comb_added, nblk * KC + k + 1)
                nc.scalar.activation(sq_last[:, k, :], x[:, k, :], ACT.Square).then_inc(sq_ready, 1)
            std(7, 0)

        @block.vector
        def _(dve):
            V = nc.vector
            nstep = [0]

            def settle(ins):
                nstep[0] += 1
                ins.then_inc(dve_step, 1)
                dve.wait_ge(dve_step, nstep[0])

            nstd, nsum = [0], [0]

            def inv_std():
                nstd[0] += 1
                dve.wait_ge(std_ready, nstd[0])
                settle(V.reciprocal(rstd[:, :], rstd[:, :]))

            def add_up(src, k, ready, n):
                dve.wait_ge(ready, n)
                if k == 0:
                    return
                if k == 1:
                    if nsum[0]:
                        dve.wait_ge(mean_done, nsum[0] // 7)
                    V.tensor_tensor(total[:, :], src[:, 0, :], src[:, 1, :], ALU.add).then_inc(sum_step, 1)
                else:
                    dve.wait_ge(sum_step, nsum[0])
                    V.tensor_tensor(total[:, :], total[:, :], src[:, k, :], ALU.add).then_inc(sum_step, 1)
                nsum[0] += 1

            def normed(weight):
                for k in range(KC):
                    V.scalar_tensor_tensor(hB[:, k, :], x[:, k, :], weight[:, k:k + 1], rstd[:, :], ALU.mult, ALU.mult)\
                        .then_inc(h_ready, 1)

            def split_normed(norm, weight, hi, lo):
                for k in range(KC + 2):
                    if k < KC:
                        if norm:
                            dve.wait_ge(h_ready, 8 * norm - KC + k + 1)
                        V.scalar_tensor_tensor(hB[:, k, :], x[:, k, :], weight[:, k:k + 1], rstd[:, :], ALU.mult, ALU.mult)\
                            .then_inc(norm_ready, 1)
                    if k >= 2:
                        dve.wait_ge(h_hi_ready, 8 * norm + k - 1)
                        V.tensor_tensor(lo[:, k - 2, :], hB[:, k - 2, :], hi[:, k - 2, :].bitcast(F32), ALU.subtract)\
                            .then_inc(h_ready, 1)

            rested = [0]

            def rest_to(stage, c):
                while rested[0] < ahead_of(stage, c):
                    n = rested[0]
                    dve.wait_ge(d_hi_ready, n + 1)
                    V.tensor_tensor(d_lo[:, n % NDS, :], raw_item(n), d_hi[:, n % NDS, :].bitcast(F32), ALU.subtract)\
                        .then_inc(d_lo_ready, 1)
                    rested[0] += 1

            for k in range(KC):
                add_up(hB, k, sq_ready, k + 1)
            dve.wait_ge(setup_in, 16)
            inv_std()
            rest_to("vu", -2)
            split_normed(0, vector("mix0"), hA_hi, hA_lo)
            rest_to("vu", -1)
            dve.wait_ge(spatial_in, 48)
            upto = const("upto").unsqueeze(1).to_broadcast([P, 8, P])
            V.tensor_tensor(wsT[:], w_s, upto, ALU.mult).then_inc(ws_ready, 1)
            V.tensor_tensor(dg[0:NS], ident[0:NS, 0:NS].unsqueeze(1).to_broadcast([NS, 8, NS]),
                            vector("w00")[0:NS, :].unsqueeze(2).to_broadcast([NS, 8, NS]), ALU.mult).then_inc(ws_ready, 1)
            for k in range(KC):
                rest_to("vu", k)
                add_up(vT, k, v_ready, k + 1)
            rest_to("vu", 8)
            dve.wait_ge(mean_done, 2)
            settle(V.tensor_copy(mu[:, :], STAT[:, 0:NT]))
            for k in range(KC):
                V.tensor_tensor(vT[:, k, :], vT[:, k, :], mu[:, :], ALU.subtract).then_inc(ctr_ready, 1)
            for k in range(KC):
                rest_to("vu", 9 + k // 4)
                add_up(hB, k, csq_ready, k + 1)
            rest_to("vu", 12)
            inv_std()
            for k in range(KC):
                if k == 5:
                    rest_to("vu", 13)
                V.scalar_tensor_tensor(vT[:, k, :], vT[:, k, :], vector("lng")[:, k:k + 1], rstd[:, :], ALU.mult, ALU.mult)\
                    .then_inc(dve_step, 1)
                nstep[0] += 1
            dve.wait_ge(dve_step, nstep[0])
            for k in range(KC):
                V.tensor_scalar(vT[:, k, :], vT[:, k, :], vector("lnb")[:, k:k + 1], None, ALU.add).then_inc(vn_ready, 1)
            for i in range(0, 6, 2):
                r = P if i < 4 else NS
                dve.wait_ge(vt_done, i + 1)
                V.tensor_copy(vtok[0:r, i // 2, 0:512], T0[0:r, :]).then_inc(vt_ready, 1)
            rest_to("vu", 15)
            for g in range(10):
                if g < 8:
                    dve.wait_ge(mix_done, g + 1)
                    dve.wait_ge(u_ready, g + 1)
                    V.tensor_tensor(hB[:, g, :], b_s[:, g, :], B[g % 4][:, 0:NT], ALU.add).then_inc(mixed, 1)
                    dve.wait_ge(mixed, g + 1)
                    V.tensor_tensor(hB[:, g, :], uT[:, g, :], hB[:, g, :], ALU.mult).then_inc(gated, 1)
                if g >= 2:
                    dve.wait_ge(gated_hi, g - 1)
                    V.tensor_tensor(hC_lo[:, g - 2, :], hB[:, g - 2, :], hC_hi[:, g - 2, :].bitcast(F32), ALU.subtract)\
                        .then_inc(gated_lo, 1)
            def add_chunk(c, norm, stage, item, squared=hB):
                rest_to(stage, item - 1)
                projected(dve, stage, item)
                V.tensor_tensor(x[:, c, :], x[:, c, :], B[c % 4][:, 0:NT], ALU.add).then_inc(x_ready, 1)
                if c < KC - 1:
                    rest_to(stage, item)
                add_up(squared, c, sq_ready, 8 * norm + c + 1)
                rest_to(stage, item)

            for c in range(KC):
                add_chunk(c, 1, "ao", c)
            inv_std()
            split_normed(1, vector("ffn0"), hA_hi, hA_lo)
            dve.wait_ge(v_stored, 16)

            def rest_hidden_row(f):
                dve.wait_ge(hF_hi_ready, f + 1)
                V.tensor_tensor(hF_lo[:, f, :], hB[:, f % 4, :], hF_hi[:, f, :].bitcast(F32), ALU.subtract).then_inc(hF_lo_ready, 1)

            for f in range(FC):
                rest_to("gu", 2 * f + 1)
                projected(dve, "gu", 2 * f + 1)
                dve.wait_ge(sil_ready, f + 1)
                if f >= 2:
                    rest_hidden_row(f - 2)
                if f >= 4:
                    dve.wait_ge(hF_lo_ready, f - 3)
                V.tensor_tensor(hB[:, f % 4, :], sil[:, f % 2, :], B[2 * (f % 2) + 1][:, 0:NT], ALU.mult).then_inc(hF_ready, 1)
            rest_hidden_row(FC - 2)
            rest_hidden_row(FC - 1)
            for c in range(KC):
                add_chunk(c, 2, "dn", 12 * (c // 4) + 8 + c % 4)
            inv_std()
            split_normed(2, vector("kvn"), hA_hi, hA_lo)
            split_normed(3, vector("mix1"), hC_hi, hC_lo)
            for v in range(2):
                o = NS * PAGES * NG * HD
                for g in range(NG):
                    c = 2 * v + g // 2
                    rest_to("kv", 11 if v else 1 + g)
                    if v:
                        projected(dve, "kv", 11)
                    dve.wait_ge(kv_ready, c + 1)
                    for r in range(2):
                        src = kvT[64 * (g % 2):64 * (g % 2) + 64, c, r:NP:2]
                        V.tensor_copy(X2[v][64 * r:64 * r + 64, o + g * P:o + g * P + P], src).then_inc(x2_ready, 1)
                o += NG * P
                dve.wait_ge(params_in, 32)
                V.tensor_copy(X2[v][:, o:o + 16], par("pe")[:, 16 * v:16 * v + 16]).then_inc(x2_ready, 1)
            dve.wait_ge(q_zero, 1)
            for c in range(KC):
                half = 64 * ((c // 2) % 2)
                rest_to("q", c)
                projected(dve, "q", c)
                V.tensor_scalar(Q[half:half + 64, 2 * c, :], B[c % 4][0:64, 0:NT], HD ** -0.5, None, ALU.mult).then_inc(q_even, 1)
            dve.wait_ge(q_zero, 3)
            dve.wait_ge(q_even, KC)
            dve.wait_ge(q_odd, KC)
            for gp in range(2):
                src = Q[:, 8 * gp:8 * gp + 8, NP:NT].rearrange("p h b -> p b h")
                qz = Qz[:, gp, :, :].rearrange("p b n -> p (b n)")
                for b in range(NS):
                    V.tensor_copy(Qz[:, gp, b, b * NH + 8 * gp:b * NH + 8 * gp + 8], src[:, b, :])
                V.tensor_copy(Qc[:, gp, :].rearrange("p (b h) -> p b h", h=NH)[:, :, 8 * gp:8 * gp + 8], src).then_inc(q_rows, 1)
            dve.wait_ge(gt_done, 1)
            V.tensor_copy(gtok[:, :, :], MISC[:, 0:96].rearrange("p (t n) -> p t n", n=48)).then_inc(gtok_ready, 1)
            V.tensor_copy(gsam[0:NS, :], MISC[0:NS, 96:144]).then_inc(gtok_ready, 1)
            for t in range(3):
                r = P if t < 2 else NS
                dve.wait_ge(vp_done, t + 1)
                dst = vtp[:, t, :, :] if t < 2 else vnew[0:NS]
                V.tensor_copy(dst, (T0, T1)[t % 2][0:r, :].rearrange("p (a n) -> p a n", a=2)).then_inc(vp_ready, 1)
            for v in range(2):
                dve.wait_ge(bhalf_ready, 2 * v + 2)
                if v:
                    dve.wait_ge(cmp2_done, 1)
                A0 = B[2 * v][0:64, :].rearrange("p (b i g s) -> p b i g s", b=NS, i=PAGES, g=NG)
                H0 = hidb[0:64, 0:512].rearrange("p (b i g s) -> p b i g s", b=NS, i=PAGES, g=NG)
                out = hid[0:64, 0:32, :].rearrange("p (g b) n -> p b g n", g=NG)
                V.tensor_tensor(out[:, :, :, 0:7], A0[:, :, 0, :, 0:7], H0[:, :, 0, :, 1:8], ALU.add)
                V.tensor_tensor(out[:, :, :, 7:8], A0[:, :, 0, :, 7:8], H0[:, :, 1, :, 0:1], ALU.add)
                V.tensor_tensor(out[:, :, :, 8:15], A0[:, :, 1, :, 0:7], H0[:, :, 1, :, 1:8], ALU.add)
                A1 = B[2 * v + 1][0:64, 0:64].rearrange("p (g s) -> p g s", g=NG)
                H1 = hidb[0:64, 512:576].rearrange("p (g s) -> p g s", g=NG)
                V.tensor_tensor(hid[0:64, 32:36, :], A1[:, :, 0:15], H1[:, :, 1:16], ALU.add)
                V.tensor_tensor(cbias[0:64, :], B[2 * v + 1][0:64, 64:65], hidb[0:64, 577:578], ALU.add).then_inc(pre_ready, 1)
                dve.wait_ge(cmp2_done, v + 1)
                if v == 0:
                    V.tensor_copy(kcT[:], T0[:, 0:270].rearrange("p (a n) -> p a n", n=NCMP)).then_inc(cmp2_ready, 1)
                else:
                    V.tensor_copy(vcs[0:NS * NCMP, :], T1[0:NS * NCMP, 0:256])
                    V.tensor_copy(vcp[0:NCMP, :], T1[0:NCMP, 256:512]).then_inc(cmp2_ready, 1)
            dve.wait_ge(cmp2_ready, 2)
            V.memset(T0[:, 384:512], 0.0).then_inc(t_zeroed, 1)
            V.memset(T1[:, 384:512], 0.0).then_inc(t_zeroed, 1)
            dist = const("dist")
            W = PAST + NS
            slope = const("negslope")
            dve.wait_ge(ss_done, 1)
            V.scalar_tensor_tensor(Ss[:, 0:W], const("sdist"), slope, B[0][:, 0:W], ALU.mult, ALU.add)
            V.scalar_tensor_tensor(Ss[:, W:2 * W], const("sdist"), slope, B[1][:, 0:W], ALU.mult, ALU.add)
            settle(V.scalar_tensor_tensor(Ss[:, 2 * W:2 * W + 120], const("scdist"), slope, B[2][:, 0:120], ALU.mult, ALU.add))
            parts = [(0, W), (W, 2 * W), (2 * W, 2 * W + NS * NCMP)]
            for j, (a, z) in enumerate(parts):
                i = V.tensor_reduce(smx[:, j:j + 1], Ss[:, a:z], AX_X, ALU.max)
            settle(i)
            V.tensor_scalar(smx[:, :], smx[:, :], -1.0, None, ALU.mult).then_inc(ss_max, 1)
            dve.wait_ge(ss_exp, 1)
            settle(V.reciprocal(ssm[:, :], ssm[:, :]))
            dve.wait_ge(grow_in, 16)
            V.tensor_tensor(swt[:, 0:2], ssm[:, 0:2], grow[:, 1:3], ALU.mult)
            settle(V.tensor_tensor(swt[:, 2:3], ssm[:, 2:3], grow[:, 0:1], ALU.mult))
            for j, (a, z) in enumerate(parts):
                i = V.tensor_scalar(Ss[:, a:z], Ss[:, a:z], swt[:, j:j + 1], None, ALU.mult)
            i.then_inc(sp_ready, 1)

            def by_two(h, a, w):
                return Sh[:, h % 3, 0:828].rearrange("p (n c) -> p n c", n=2)[:, :, a:a + w]

            def biased_max(h):
                b = h % 3
                S = Sh[:, b, :]
                dve.wait_ge(s_done, h + 1)
                if h >= 3:
                    dve.wait_ge(pt_done, 2 * h - 4)
                V.scalar_tensor_tensor(S[:, 0:414], dist, -SLOPE[h], B[2 * (h % 2)][:, 0:414], ALU.mult, ALU.add)
                V.scalar_tensor_tensor(S[:, 414:798], dist[:, 0:384], -SLOPE[h], B[2 * (h % 2) + 1][:, 0:384], ALU.mult, ALU.add)\
                    .then_inc(s_biased, 1)
                dve.wait_ge(s_biased, h + 1)
                V.tensor_reduce(mx[:, b, 0:2], by_two(h, 0, P), AX_X, ALU.max)
                V.tensor_reduce(mx[:, b, 2:4], by_two(h, P, NP), AX_X, ALU.max)
                settle(V.tensor_reduce(mx[:, b, 4:6], S[:, 384:414].rearrange("p (t n) -> p t n", n=NCMP), AX_X, ALU.max))
                V.tensor_scalar(mx[:, b, :], mx[:, b, :], -1.0, None, ALU.mult).then_inc(neg_max, 1)

            def scale(h):
                b = h % 3
                S = Sh[:, b, :]
                dve.wait_ge(exps, h + 1)
                settle(V.reciprocal(sm[:, b, :], sm[:, b, :]))
                g3 = gtok[:, :, 3 * h:3 * h + 3]
                dst = wt[:, b, :].rearrange("p (a t) -> p a t", a=3)
                V.tensor_tensor(dst[:, 0, :], sm[:, b, 4:6], g3[:, :, 0], ALU.mult)
                V.tensor_tensor(dst[:, 1, :], sm[:, b, 0:3:2], g3[:, :, 1], ALU.mult)
                settle(V.tensor_tensor(dst[:, 2, :], sm[:, b, 1:4:2], g3[:, :, 2], ALU.mult))
                cm = const("cmpmask")
                for t in range(2):
                    V.scalar_tensor_tensor(S[:, 384 + 15 * t:399 + 15 * t], S[:, 384 + 15 * t:399 + 15 * t],
                                           wt[:, b, t:t + 1], cm[:, 15 * t:15 * t + 15], ALU.mult, ALU.mult)
                for j, (a, z, w) in enumerate([(0, 128, 2), (128, 384, 3), (414, 542, 4), (542, 798, 5)]):
                    i = V.tensor_scalar(S[:, a:z], S[:, a:z], wt[:, b, w:w + 1], None, ALU.mult)
                i.then_inc(p_ready, 1)

            def rest_out(c):
                dve.wait_ge(out_hi, c + 1)
                V.tensor_tensor(hA_lo[:, c, :], hB[:, c, :], hA_hi[:, c, :].bitcast(F32), ALU.subtract).then_inc(out_lo, 1)

            biased_max(0)
            biased_max(1)
            dve.wait_ge(spt_done, 1)
            V.tensor_copy(PTs[:, 0:4, :], T0[:, :].rearrange("p (a n) -> p a n", n=P))
            V.tensor_copy(PTs[0:NS, 4:6, :], T1[0:NS, 0:256].rearrange("p (a n) -> p a n", n=P))
            V.tensor_copy(PTs[0:NS * NCMP, 6, :], T1[0:NS * NCMP, 256:384]).then_inc(spt_ready, 1)
            for j in (1, 3):
                dve.wait_ge(orow_done, j + 1)
                V.tensor_copy(orow[:, 512 * j:512 * j + 512], B[j][0:NH, :]).then_inc(orow_ready, 1)
            dve.wait_ge(so_done, 1)
            for g2 in range(2):
                for odd in range(2):
                    src = STAT[64 * g2:64 * g2 + 64, 0:256].rearrange("p (c b h) -> p c b h", c=2, h=NH)
                    dst = hB[64 * odd:64 * odd + 64, :, NP:NT].rearrange("p (c g i) b -> p c g i b", c=2, g=2)
                    for c in range(2):
                        h0 = 8 * c + 4 * g2 + odd
                        i = V.tensor_copy(dst[:, c, g2, :, :], src[:, c, :, h0:h0 + 3:2].rearrange("p b i -> p i b"))
            i.then_inc(so_ready, 1)
            scale(0)
            for h in range(NH):
                if h + 2 < NH:
                    biased_max(h + 2)
                if h + 1 < NH:
                    scale(h + 1)
                if h >= 4 and h % 2 == 0:
                    rest_out(h // 2 - 2)
                if h == NH - 1:
                    rest_to("bo", -2)
            rest_out(KC - 2)
            rest_to("bo", -1)
            rest_out(KC - 1)
            for c in range(KC):
                add_chunk(c, 3, "bo", c, sq3)
            inv_std()
            normed(late("ffn1"))

            dve.wait_ge(kv_stored, 16)
            L = lg
            def col(i, t=None):
                return L[:, :, 8 * i:8 * i + 8] if t is None else L[:, t, 8 * i:8 * i + 8]

            def wide(ap):
                return ap.to_broadcast([P, 3, 8])

            down8 = const("down8").unsqueeze(1).to_broadcast([P, 3, 8])
            V.memset(GwT[:], 0.0).then_inc(gwT_ready, 1)
            V.memset(lg[:], 0.0)
            settle(V.memset(sc[:], 0.0))
            dve.wait_ge(route_done, 1)
            V.tensor_tensor(col(0)[:, 0:2, :], MISC[:, 0:16].rearrange("p (t n) -> p t n", n=8),
                            b_router.unsqueeze(1).to_broadcast([P, 2, 8]), ALU.add)
            settle(V.tensor_tensor(col(0, 2)[0:NS, :], MISC[0:NS, 16:24], b_router[0:NS, :], ALU.add))

            def best(src, dst, m):
                settle(V.tensor_reduce(sc[:, :, m:m + 1], src, AX_X, ALU.max))
                settle(V.tensor_tensor(col(1), src, wide(sc[:, :, m:m + 1]), ALU.is_equal))
                settle(V.tensor_tensor(col(1), col(1), down8, ALU.mult))
                settle(V.tensor_reduce(sc[:, :, 2:3], col(1), AX_X, ALU.max))
                settle(V.tensor_tensor(dst, col(1), wide(sc[:, :, 2:3]), ALU.is_equal))

            best(col(0), col(2), 0)
            settle(V.scalar_tensor_tensor(col(3), col(2), -3e38, col(0), ALU.mult, ALU.add))
            best(col(3), col(4), 1)
            V.tensor_tensor(col(5), col(2), col(4), ALU.add)
            V.tensor_tensor(sc[:, :, 3:4], sc[:, :, 1:2], sc[:, :, 0:1], ALU.subtract).then_inc(rank_in, 1)
            dve.wait_ge(exp_ready, 1)
            settle(V.tensor_scalar(sc[:, :, 5:6], sc[:, :, 4:5], 1.0, None, ALU.add))
            settle(V.reciprocal(sc[:, :, 6:7], sc[:, :, 5:6]))
            V.tensor_tensor(sc[:, :, 7:8], sc[:, :, 4:5], sc[:, :, 6:7], ALU.mult)
            dve.wait_ge(rank_done, 1)
            counts = MISC[:, 48:56]
            V.tensor_scalar(cnt[:, 0:1], counts[:, 0:1], -1.0, None, ALU.is_gt)
            settle(V.tensor_scalar(cnt[:, 1:8], counts[:, 1:8], 0.0, None, ALU.is_gt))
            settle(V.scalar_tensor_tensor(cnt[:, 0:8], counts, float(ROWS), cnt[:, 0:8], ALU.is_gt, ALU.add))
            settle(V.scalar_tensor_tensor(cnt[:, 0:8], counts, float(2 * ROWS), cnt[:, 0:8], ALU.is_gt, ALU.add))
            settle(V.tensor_copy(cnt[:, 8:16], cnt[:, 0:8]))
            a, z = 8, 16
            for s in (1, 2, 4):
                V.tensor_copy(cnt[:, z:z + s], cnt[:, a:a + s])
                settle(V.tensor_tensor(cnt[:, z + s:z + 8], cnt[:, a + s:a + 8], cnt[:, a:a + 8 - s], ALU.add))
                a, z = z, z + 8
            ends_ = cnt[:, a:a + 8]
            settle(V.tensor_tensor(cnt[:, 48:56], ends_, cnt[:, 0:8], ALU.subtract))
            settle(V.tensor_scalar(cnt[:, 48:56], cnt[:, 48:56], float(ROWS), None, ALU.mult))
            V.tensor_tensor(col(6)[:, 0:2, :], MISC[:, 24:40].rearrange("p (t n) -> p t n", n=8),
                            cnt[:, 48:56].unsqueeze(1).to_broadcast([P, 2, 8]), ALU.add)
            settle(V.tensor_tensor(col(6, 2)[0:NS, :], MISC[0:NS, 40:48], cnt[0:NS, 48:56], ALU.add))
            for m in range(2):
                settle(V.tensor_tensor(col(7), col(2 + 2 * m), col(6), ALU.mult))
                settle(V.tensor_reduce(sc[:, :, 8 + m:9 + m], col(7), AX_X, ALU.add))
            def block_info():
                settle(V.tensor_tensor(bcmp[0:1, :].rearrange("p (t e) -> p t e", e=NE),
                                       ends_[0:1, :].unsqueeze(1).to_broadcast([1, MAXB, NE]),
                                       const("blk")[0:1, :].rearrange("p (t e) -> p t e", e=NE), ALU.is_le))
                settle(V.tensor_reduce(bout[0:1, 0:MAXB], bcmp[0:1, :].rearrange("p (t e) -> p t e", e=NE), AX_X, ALU.add))
                settle(V.tensor_scalar(bout[0:1, 0:MAXB], bout[0:1, 0:MAXB], float(NE - 1), None, ALU.min))
                V.tensor_copy(blkinfo[0:1, MAXB:MAXB + 1], ends_[0:1, 7:8])
                V.tensor_copy(blkinfo[0:1, 0:MAXB], bout[0:1, 0:MAXB]).then_inc(blk_ready, 1)

            def selections(between=None):
                tiles = [(t, P if t < 2 else NS) for t in range(3)]
                iota = const("iota")
                for t, r in tiles:
                    V.tensor_scalar(Gm[0:r, t, :], iota[0:r, :], sc[0:r, t, 8:9], None, ALU.is_equal).then_inc(dve_sel, 1)
                for t, r in tiles:
                    dve.wait_ge(dve_sel, selbase[0] + t + 1)
                    V.scalar_tensor_tensor(Gm[0:r, t, :], iota[0:r, :], sc[0:r, t, 9:10], Gm[0:r, t, :], ALU.is_equal, ALU.add)\
                        .then_inc(sel_ready, 1)
                if between:
                    between()
                for t, r in tiles:
                    V.tensor_scalar(Gw[0:r, t, :], iota[0:r, :], sc[0:r, t, 8:9], sc[0:r, t, 6:7], ALU.is_equal, ALU.mult)
                    V.tensor_scalar(Gt[0:r, t, :], iota[0:r, :], sc[0:r, t, 9:10], sc[0:r, t, 7:8], ALU.is_equal, ALU.mult)\
                        .then_inc(dve_sel, 1)
                for t, r in tiles:
                    dve.wait_ge(dve_sel, selbase[0] + t + 4)
                    V.tensor_tensor(Gw[0:r, t, :], Gw[0:r, t, :], Gt[0:r, t, :], ALU.add).then_inc(gw_sel, 1)
                V.tensor_scalar(sc[:, :, 8:10], sc[:, :, 8:10], -float(ROWS), None, ALU.add).then_inc(gw_sel, 1)

            def rest_item(t, i):
                dve.wait_ge(hi_ready, t * ITEMS + i + 1)
                V.tensor_tensor(w_lo[:, i % NSPLIT, :], raw[:, (i // 2) % NRAW, ITEM * (i % 2):ITEM * (i % 2) + ITEM],
                                w_hi[:, i % NSPLIT, :].bitcast(F32), ALU.subtract).then_inc(lo_ready, 1)

            def gathered(t, half):
                dve.wait_ge(xg_hi_ready, 2 * t + half + 1)
                V.tensor_tensor(xg_lo[:, 4 * half:4 * half + 4, :], (STAT, MISC)[half][:, :].rearrange("p (k n) -> p k n", n=P),
                                xg_hi[:, 4 * half:4 * half + 4, :].bitcast(F32), ALU.subtract).then_inc(xg_lo_ready, 1)

            def add_combined(t, c):
                dve.wait_ge(comb_done, t * KC + c + 1)
                V.tensor_tensor(x[:, c, :], x[:, c, :], (STAT, MISC)[c % 2][:, 0:NT], ALU.add).then_inc(comb_added, 1)

            selbase = [0]
            selections(block_info)
            for i in range(AHEAD):
                rest_item(0, i)
            nblk = dve.value_load(blkinfo[0:1, MAXB:MAXB + 1], min_val=1, max_val=MAXB)
            gathered(0, 0)
            gathered(0, 1)
            with dve.Fori(0, nblk) as t:
                def rest_hidden(f):
                    dve.wait_ge(hmT_hi, t * FT + f + 1)
                    V.tensor_tensor(hm_lo[:, f % 2, :, :], (T0, T1)[f % 2][:, 0:256].rearrange("p (k n) -> p k n", n=P),
                                    hm_hi[:, f % 2, :, :].bitcast(F32), ALU.subtract).then_inc(hmT_lo, 1)

                n = AHEAD
                for _ in range(2):
                    rest_item(t, n)
                    n += 1
                for f in range(FT):
                    for _ in range(2 * (f >= 2) + 4 * (f + 1 < FT)):
                        rest_item(t, n)
                        n += 1
                    dve.wait_ge(sg_ready, t * FT + f + 1)
                    if f >= 2:
                        dve.wait_ge(hmT_done, t * FT + f - 1)
                    V.tensor_tensor(hm[:, f % 2, :], sg[:, f % 2, :], B[f % 2][:, 256:512], ALU.mult).then_inc(hm_ready, 1)
                    if f:
                        rest_hidden(f - 1)
                    if f < 4:
                        for c in (2 * f, 2 * f + 1):
                            add_combined(t, c)
                    if f == 4:
                        dve.wait_ge(gw_done, t + 1)
                        V.tensor_copy(GwT[:, :], MISC[:, 0:NT]).then_inc(gwT_ready, 1)
                    if f == 5:
                        dve.wait_ge(gw_sel, 4 * t + 4)
                        selbase[0] = t * 6 + 6
                        selections()
                for _ in range(2):
                    rest_item(t, n)
                    n += 1
                gathered(t + 1, 0)
                rest_hidden(FT - 1)
                rest_item(t, n)
                n += 1
                gathered(t + 1, 1)
                rest_item(t, n)
                n += 1
                for i in range(AHEAD):
                    rest_item(t + 1, i)
            for c in range(KC + 1):
                if c < KC:
                    add_combined(nblk, c)
                if c:
                    add_up(sq_last, c - 1, sq_ready, 32 + c)
            inv_std()
            normed(late("final"))

        @block.tensor
        def _(pe):
            T = nc.tensor
            mean = vector("mean")

            nmean = [0]

            def mean_of():
                nmean[0] += 1
                pe.wait_ge(sum_step, 7 * nmean[0])
                T.matmul(STAT[:, 0:NT], mean, total[:, :], start=True, stop=True).then_inc(mean_done, 1)

            taken = [0]

            def product(bank, hi, lo, ks=range(KC), first=True, last=True, each=None):
                n = taken[0]
                taken[0] += 1
                pe.wait_ge(d_lo_ready, n + 1)
                w_hi_, w_lo_ = (d[:, n % NDS, :].rearrange("p (k m) -> p k m", m=P) for d in (d_hi, d_lo))
                out = bank[:, 0:NT]
                for j, k in enumerate(ks):
                    if each:
                        each(k)
                    T.matmul(out, w_hi_[:, j, :], hi[:, k, :], start=(first and j == 0), stop=False)
                    T.matmul(out, w_hi_[:, j, :], lo[:, k, :], start=False, stop=False)
                    i = T.matmul(out, w_lo_[:, j, :], hi[:, k, :], start=False, stop=(last and k == ks[-1]))
                i.then_inc(dense_done, 1)

            def chunks_of(count, base):
                return lambda k: pe.wait_ge(count, base + k + 1)

            pe.wait_ge(setup_in, 16)
            mean_of()
            for c in range(16):
                if 4 <= c < 12:
                    pe.wait_ge(v_ready, c - 3)
                elif c >= 12:
                    pe.wait_ge(u_ready, c - 11)
                product(B[c % 4], hA_hi, hA_lo, each=chunks_of(h_ready, 0) if c == 0 else None)
                if c == 8:
                    mean_of()
                if c == 12:
                    mean_of()
            pe.wait_ge(spatial_in, 48)
            pe.wait_ge(vn_ready, 8)
            for t, (a, z) in enumerate([(0, P), (P, NP), (NP, NT)]):
                if t:
                    pe.wait_ge(vt_ready, 2 * t)
                for half, bank in ((0, T0), (1, T1)):
                    for k in range(4):
                        i = T.transpose(bank[0:z - a, k * P:(k + 1) * P], vT[:, 4 * half + k, a:z], ident)
                    i.then_inc(vt_done, 1)
            pe.wait_ge(ws_ready, 2)
            pe.wait_ge(vt_ready, 6)
            for g in range(8):
                if g >= 4:
                    pe.wait_ge(mixed, g - 3)
                else:
                    pe.wait_ge(u_ready, 4 + g + 1)
                bank, cols = B[g % 4], slice(g * P, (g + 1) * P)
                T.matmul(bank[:, 0:P], vtok[:, 0, cols], wsT[:, g, :], start=True, stop=True)
                T.matmul(bank[:, P:NP], vtok[:, 1, cols], wsT[:, g, :], start=True, stop=True)
                T.matmul(bank[:, NP:NT], vtok[0:NS, 2, cols], dg[0:NS, g, :], start=True, stop=True).then_inc(mix_done, 1)
            for c in range(KC):
                if c < 4:
                    pe.wait_ge(mixed, c + 5)
                else:
                    pe.wait_ge(x_ready, c - 3)
                product(B[c % 4], hC_hi, hC_lo, each=chunks_of(gated_lo, 0) if c == 0 else None)
            mean_of()
            for f in range(FC):
                if f >= 2:
                    pe.wait_ge(hF_ready, f - 1)
                product(B[2 * (f % 2)], hA_hi, hA_lo, each=chunks_of(h_ready, 8) if f == 0 else None)
                product(B[2 * (f % 2) + 1], hA_hi, hA_lo)
            for half in range(2):
                for part in range(3):
                    ks = range(8 * part, min(8 * part + 8, FC))
                    for j in range(4):
                        if part == 0 and half:
                            pe.wait_ge(x_ready, 8 + j + 1)
                        if half == 0 and j == 0:
                            pe.wait_ge(hF_lo_ready, ks[-1] + 1)
                        if part == 0 and half == 0 and j < 2:
                            pe.wait_ge(hF_ready, FC)
                        product(B[j], hF_hi, hF_lo, ks, part == 0, part == 2)
            mean_of()
            for c in range(12):
                if c < 4:
                    pe.wait_ge(x_ready, 16)
                if c >= 4:
                    pe.wait_ge(kv_ready, c - 3)
                product(B[c % 4], hA_hi, hA_lo, each=chunks_of(h_ready, 16) if c == 0 else None)
            pe.wait_ge(h_ready, 32)
            pe.wait_ge(params_in, 32)
            for k in range(KC):
                i = T.matmul(MISC[0:48, 0:NT], w_gate[:, k, :], hB[:, k, :], start=(k == 0), stop=(k == KC - 1))
            i.then_inc(gp_done, 1)
            for c in range(KC):
                if c < 4:
                    pe.wait_ge(kv_ready, 8 + c + 1)
                else:
                    pe.wait_ge(q_even, c - 3)
                    pe.wait_ge(q_odd, c - 3)
                product(B[c % 4], hC_hi, hC_lo)
            pe.wait_ge(sig_ready, 1)
            for t, (a, z) in enumerate([(0, P), (P, NP), (NP, NT)]):
                i = T.transpose(MISC[0:z - a, 48 * t:48 * t + 48], gT[0:48, a:z], ident[0:48, 0:48])
            i.then_inc(gt_done, 1)
            for t, (a, z) in enumerate([(0, P), (P, NP), (NP, NT)]):
                if t == 2:
                    pe.wait_ge(vp_ready, 1)
                for j, c in enumerate((6, 7, 10, 11)):
                    i = T.transpose((T0, T1)[t % 2][0:z - a, j * P:(j + 1) * P], kvT[:, c, a:z], ident)
                i.then_inc(vp_done, 1)
            NSEG = NS * PAGES * NG * 8
            pe.wait_ge(q_even, KC)
            pe.wait_ge(q_odd, KC)
            for v in range(2):
                pe.wait_ge(cmp_in[v], 16 * NS * PAGES)
                pe.wait_ge(x2_ready, 9 * v + 9)
                for m in range(8):
                    T.matmul(B[2 * v][:, :], w1[:, v, m, :], X2[v][:, m:8 * NSEG:8], start=(m == 0), stop=(m == 7))
                    i = T.matmul(B[2 * v + 1][:, 0:66], w1[:, v, m, :], X2[v][:, 8 * NSEG + m:8 * NSEG + 528:8],
                                 start=(m == 0), stop=(m == 7))
                i.then_inc(cmp_done, 1)
            pe.wait_ge(vp_ready, 3)
            pe.wait_ge(hid_ready, 1)
            hid_s = hid[0:64, 0:32, :].rearrange("p (c g b) n -> p c g (b n)", c=2, g=2)
            for g2 in range(2):
                T.matmul(T0[:, 0:240], w2k[0:64, g2, :], hid_s[:, :, g2, :], start=(g2 == 0), stop=(g2 == 1))
            for g2 in range(2):
                i = T.matmul(T0[:, 240:270], w2k[0:64, g2, :], hid[0:64, 32 + g2:36:2, :], start=(g2 == 0), stop=(g2 == 1))
            i.then_inc(cmp2_done, 1)

            def sample_scores(n, t):
                arrived(pe, t)
                keys = tile(t).rearrange("p (b c k) -> p b c k", b=NS, c=2)
                for j in range(16):
                    i = T.matmul(B[n][:, 0:PAST], Qz[:, j % 2, j // 2, :], keys[:, j // 2, j % 2, :], start=(j == 0), stop=(j == 15))
                i.then_inc(sk_used, 1)
                for c in range(2):
                    T.matmul(B[n][:, PAST:PAST + NS], Qc[:, c, :], kvT[:, 4 + 4 * n + c, NP:NT], start=(c == 0), stop=(c == 1))

            pe.wait_ge(q_rows, 2)
            pe.wait_ge(pre_ready, 1)
            sample_scores(0, "SK")
            pe.wait_ge(hid_ready, 2)
            for g in range(NG):
                cols = slice(64 * g, 64 * g + 64)
                T.matmul(T1[0:NS * NCMP, cols], hid[0:64, 8 * g:8 * g + 8, :].rearrange("p b n -> p (b n)"), par("w2v")[0:64, :],
                         start=True, stop=True)
                i = T.matmul(T1[0:NCMP, 256 + 64 * g:320 + 64 * g], hid[0:64, 32 + g, :], par("w2v")[0:64, :], start=True, stop=True)
            i.then_inc(cmp2_done, 1)
            sample_scores(1, "WK")
            pe.wait_ge(pre_ready, 2)
            pe.wait_ge(cmp2_ready, 1)
            for c in range(2):
                i = T.matmul(B[2][:, 0:NS * NCMP], Qc[:, c, :], kcT[:, 8 * c:8 * c + 8, :], start=(c == 0), stop=(c == 1))
            i.then_inc(ss_done, 1)

            def scores(h):
                c, b = h // 8, h % 2
                if h == 0:
                    pe.wait_ge(ss_max, 1)
                if h >= 2:
                    pe.wait_ge(s_biased, h - 1)
                q0, q1 = Q[:, h, 0:P], Q[:, h, P:NP]
                slc, win = B[2 * b], B[2 * b + 1]
                T.matmul(slc[:, 0:P], q0, kvT[:, 4 + c, 0:P], start=True, stop=True)
                T.matmul(slc[:, 384:399], q0, kcT[:, 16 + c, :], start=True, stop=True)
                T.matmul(win[:, 0:P], q0, kvT[:, 8 + c, 0:P], start=True, stop=True)
                T.matmul(slc[:, P:384], q1, kvT[:, 4 + c, 0:NP], start=True, stop=True)
                T.matmul(slc[:, 399:414], q1, kcT[:, 16 + c, :], start=True, stop=True)
                T.matmul(win[:, P:384], q1, kvT[:, 8 + c, 0:NP], start=True, stop=True).then_inc(s_done, 1)

            def turn(h):
                S = Sh[:, h % 3, :]
                pe.wait_ge(p_ready, h + 1)
                if h:
                    pe.wait_ge(pt_ready, 2 * h)
                for n, bank in enumerate((T0, T1)):
                    for j in range(3):
                        T.transpose(bank[:, j * P:(j + 1) * P], S[:, 414 * n + j * P:414 * n + (j + 1) * P], ident)
                    T.transpose(bank[0:NCMP, 384:512], S[:, 384 + 15 * n:399 + 15 * n], ident).then_inc(pt_done, 1)

            def weigh(h):
                g, bank = h // 4, (STAT, MISC)[h % 2]
                cols = slice(HD * g, HD * g + HD)
                pe.wait_ge(pt_ready, 2 * h + 2)
                if h == 0:
                    pe.wait_ge(so_ready, 1)
                if h >= 2:
                    pe.wait_ge(o_ready, h - 1)
                for n in range(2):
                    T.matmul(bank[0:HD, 0:NP], vtp[:, 0, n, cols], PT[:, h % 2, n, 0:NP], start=(n == 0), stop=False)
                    T.matmul(bank[0:HD, P:NP], vtp[:, 1, n, cols], PT[:, h % 2, n, NP:384], start=False, stop=False)
                T.matmul(bank[0:HD, 0:P], vcp[0:NCMP, cols], PT[0:NCMP, h % 2, 0, 384:512], start=False, stop=False)
                T.matmul(bank[0:HD, P:NP], vcp[0:NCMP, cols], PT[0:NCMP, h % 2, 1, 384:512], start=False, stop=True).then_inc(o_done, 1)

            pe.wait_ge(vp_ready, 3)
            pe.wait_ge(t_zeroed, 2)
            pe.wait_ge(gtok_ready, 2)
            scores(0)
            scores(1)
            W = PAST + NS
            pe.wait_ge(sp_ready, 1)
            for j in range(4):
                a = W * (j // 2) + P * (j % 2)
                T.transpose(T0[:, j * P:(j + 1) * P], Ss[:, a:a + P], ident)
            T.transpose(T1[0:NS, 0:P], Ss[:, PAST:W], ident)
            T.transpose(T1[0:NS, P:2 * P], Ss[:, W + PAST:2 * W], ident)
            T.transpose(T1[0:NS * NCMP, 2 * P:3 * P], Ss[:, 2 * W:2 * W + NS * NCMP], ident).then_inc(spt_done, 1)
            pe.wait_ge(spt_ready, 1)
            pe.wait_ge(past_v_in, 16 * (NS * PAGES + 1))
            pe.wait_ge(s_biased, 2)
            vals = [v[:, 0:SLOT].rearrange("p (b i v) -> p b i v", b=NS, i=PAGES) for v in (slc_v, win_v_past)]
            for b in range(NS):
                out = B[b // 2][0:NH, 256 * (b % 2):256 * (b % 2) + 256]
                for j in range(4):
                    i = T.matmul(out, PTs[:, j, b * NH:(b + 1) * NH], vals[j // 2][:, b, j % 2, :], start=(j == 0), stop=(j == 3))
                if b % 2:
                    i.then_inc(orow_done, 1)
            for c in range(2):
                rows_, v = STAT[:, c * P:(c + 1) * P], slice(c * P, (c + 1) * P)
                T.matmul(rows_, vcs[0:NS * NCMP, v], PTs[0:NS * NCMP, 6, :], start=True, stop=False)
                T.matmul(rows_, vnew[0:NS, 0, v], PTs[0:NS, 4, :], start=False, stop=False)
                if c == 0:
                    pe.wait_ge(orow_ready, 4)
                for b in range(NS):
                    T.matmul(rows_[:, b * NH:(b + 1) * NH], orow[:, 256 * b + c * P:256 * b + c * P + P], ident[0:NH, 0:NH],
                             start=False, stop=False, skip_group_check=True)
                i = T.matmul(rows_, vnew[0:NS, 1, v], PTs[0:NS, 5, :], start=False, stop=True)
            i.then_inc(so_done, 1)
            for h in range(NH):
                if h + 2 < NH:
                    scores(h + 2)
                turn(h)
                if h:
                    weigh(h - 1)
            weigh(NH - 1)
            for c in range(KC):
                if c >= 4:
                    pe.wait_ge(x_ready, 16 + c - 3)
                product(B[c % 4], hA_hi, hA_lo, each=chunks_of(out_lo, 0) if c == 0 else None)
            mean_of()
            for k in range(KC):
                pe.wait_ge(h_ready, 32 + k + 1)
                i = T.matmul(MISC[0:NE, 0:NT], w_router[:, k, :], hB[:, k, :], start=(k == 0), stop=(k == KC - 1))
            i.then_inc(lT_done, 1)
            spans = [(0, P), (P, NP), (NP, NT)]
            for t, (a, z) in enumerate(spans):
                for half in range(2):
                    for k in range(4):
                        i = T.transpose(HT[2 * t + half][0:z - a, k * P:(k + 1) * P], hB[:, 4 * half + k, a:z], ident)
                    i.then_inc(ht_done, 1)
                if t == 0:
                    pe.wait_ge(lT_ready, 1)
                    for u, (a_, z_) in enumerate(spans):
                        i = T.transpose(MISC[0:z_ - a_, 8 * u:8 * u + 8], lgT[:, a_:z_], ident[0:NE, 0:NE])
                    i.then_inc(route_done, 1)
            pe.wait_ge(rank_in, 1)
            both = [lg[0:z - a, t, 40:48] for t, (a, z) in enumerate(spans)]
            before, ones = const("before"), const("ones")
            for t, (a, z) in enumerate(spans):
                r = z - a
                out = MISC[0:r, 24 + 8 * t:32 + 8 * t]
                for u in range(t):
                    T.matmul(out, ones[:, 0:r], both[u], start=(u == 0), stop=False)
                T.matmul(out, before[0:r, 0:r], both[t], start=(t == 0), stop=True)
            for t, (a, z) in enumerate(spans):
                i = T.matmul(MISC[:, 48:56], ones[0:z - a, 0:P], both[t], start=(t == 0), stop=(t == 2))
            i.then_inc(rank_done, 1)
            pe.wait_ge(ht_ready, 6)

            def gather(t):
                pe.wait_ge(sel_ready, 3 * t + 3)
                for k in range(KC):
                    out = (STAT, MISC)[k // 4][:, (k % 4) * P:(k % 4 + 1) * P]
                    for u, (a, z) in enumerate(spans):
                        i = T.matmul(out, htok[0:z - a, u, k * P:(k + 1) * P], Gm[0:z - a, u, :], start=(u == 0), stop=(u == 2))
                    if k % 4 == 3:
                        i.then_inc(xg_done, 1)

            def combine(t, c):
                if c == 0:
                    pe.wait_ge(yrow_ready, 2 * t + 2)
                    pe.wait_ge(gwT_ready, t + 1)
                if c >= 2:
                    pe.wait_ge(comb_added, t * KC + c - 1)
                T.matmul((STAT, MISC)[c % 2][:, 0:NT], yrow[:, c * P:(c + 1) * P], GwT[:, :], start=True, stop=True)\
                    .then_inc(comb_done, 1)

            gather(0)
            pe.wait_ge(blk_ready, 1)
            nblk = pe.value_load(blkinfo[0:1, MAXB:MAXB + 1], min_val=1, max_val=MAXB)
            with pe.Fori(0, nblk) as t:

                def turn_hidden(f):
                    pe.wait_ge(hm_ready, t * FT + f + 1)
                    for j in range(2):
                        i = T.transpose((T0, T1)[f % 2][:, j * P:(j + 1) * P], hm[:, f % 2, j * P:(j + 1) * P], ident)
                    i.then_inc(hmT_done, 1)

                n = 0

                def item():
                    nonlocal n
                    pe.wait_ge(lo_ready, t * ITEMS + 2 * NRAW + n + 1)
                    n += 1
                    return (n - 1) % NSPLIT

                def expert_product(out, lhs_hi, lhs_lo, cols, slot, first, last):
                    hi, lo = w_hi[:, slot, cols], w_lo[:, slot, cols]
                    T.matmul(out, lhs_hi, hi, start=first, stop=False)
                    T.matmul(out, lhs_hi, lo, start=False, stop=False)
                    return T.matmul(out, lhs_lo, hi, start=False, stop=last)

                def down(f):
                    pe.wait_ge(hmT_lo, t * FT + f + 1)
                    for j in range(2):
                        slot = item()
                        for half in range(2):
                            i = expert_product(B[2 + half][:, :], hm_hi[:, f % 2, j, :], hm_lo[:, f % 2, j, :],
                                        slice(512 * half, 512 * half + 512), slot, f == 0 and j == 0, f == FT - 1 and j == 1)
                        i.then_inc(item_used, 1)

                for f in range(FT):
                    if f >= 2:
                        pe.wait_ge(hm_ready, t * FT + f - 1)
                    for q in range(4):
                        if f == 0 and q % 2 == 0:
                            pe.wait_ge(xg_lo_ready, 2 * t + q // 2 + 1)
                        slot = item()
                        for k in (2 * q, 2 * q + 1):
                            i = expert_product(B[f % 2][:, :], xg_hi[:, k, :], xg_lo[:, k, :],
                                        slice(512 * (k % 2), 512 * (k % 2) + 512), slot, k == 0, k == KC - 1)
                        i.then_inc(item_used, 1)
                    if f < 4:
                        combine(t, 2 * f)
                        combine(t, 2 * f + 1)
                    if f == 4:
                        pe.wait_ge(comb_added, t * KC + KC)
                        pe.wait_ge(gw_sel, 4 * t + 3)
                        for u, (a, z) in enumerate(spans):
                            i = T.transpose(MISC[:, a:z], Gw[0:z - a, u, :], ident[0:z - a, 0:z - a])
                        i.then_inc(gw_done, 1)
                    if f == FT - 1:
                        pe.wait_ge(gwT_ready, t + 2)
                        gather(t + 1)
                    if f >= 1:
                        turn_hidden(f - 1)
                    if f >= 2:
                        down(f - 2)
                turn_hidden(FT - 1)
                down(FT - 2)
                down(FT - 1)
            for c in range(KC):
                combine(nblk, c)
            mean_of()


def kernel(**inputs):
    import concourse.bacc as bacc
    from concourse.bass_utils import run_bass_kernel_spmd as run

    a = {k: np.asarray(v) for k, v in inputs.items()}

    def cat(*xs):
        return np.concatenate(xs, axis=-1)

    def chunks(w):
        return w.reshape(-1, P, w.shape[-1]).transpose(1, 0, 2)

    def vec(v):
        return v.reshape(KC, P).T

    def part(rows):
        return np.concatenate([rows, np.zeros((P - rows.shape[0],) + rows.shape[1:], np.float32)], axis=0)

    arrays = {}
    tokens = np.concatenate([a["x_prompt"][0], a["x_sample"][:, 0]], axis=0)
    arrays["x"] = chunks(np.ascontiguousarray(tokens.T))
    ain, aout = chunks(a["a_w_in"][0]), chunks(a["a_w_out"][0])
    fg, fu, fd = chunks(a["f_w_gate"][0]), chunks(a["f_w_up"][0]), chunks(a["f_w_down"][0])
    wkv, bin_, bout = chunks(a["w_kv"]), chunks(a["b_w_in"][0]), chunks(a["b_w_out"][0])

    def columns(w, *firsts):
        w = np.concatenate([w[:, :, c:c + P] for c in firsts], axis=1)
        return w.reshape(P, SLOT)

    def four(w, c):
        return columns(w, c, c + P, c + 2 * P, c + 3 * P)

    tiles = [four(ain, c) for c in (1024, 1536, 0, 512)] + [four(aout, c) for c in (0, 512)]
    gate_up = np.concatenate([fg, fu], axis=2)
    tiles += [columns(gate_up, c, FF + c, c + P, FF + c + P) for c in range(0, FF, 256)]
    down = np.concatenate([fd, np.zeros((P, 24 - FC, DM), np.float32)], axis=1)
    tiles += [four(down[:, 8 * i:8 * i + 8], c) for c in (0, 512) for i in range(3)]
    tiles += [four(wkv, c) for c in (0, 512, 1024)] + [four(bin_, c) for c in (0, 512)] + [four(bout, c) for c in (0, 512)]
    arrays["wd"] = np.stack(tiles)
    mg, mu, md = a["m_w_gate"][0], a["m_w_up"][0], a["m_w_down"][0]
    moe = np.empty((NE, UNITS, P, UNIT), np.float32)
    for u, (f, kind) in enumerate(USE):
        if kind == "d":
            f -= 2
            moe[:, u] = md[:, 256 * f:256 * f + 256].reshape(NE, 2, P, DM).transpose(0, 2, 1, 3).reshape(NE, P, UNIT)
        else:
            k = 512 * (kind == "b")
            for w, o in ((mg, 0), (mu, 256)):
                moe[:, u].reshape(NE, P, 4, 512)[..., o:o + 256] = \
                    w[:, k:k + 512, 256 * f:256 * f + 256].reshape(NE, 4, P, 256).transpose(0, 2, 1, 3)
    arrays["moe"] = moe
    bw, w1_, w2_ = a["b_w_in"][0], a["cmp_w1"], a["cmp_w2"]
    zero = np.zeros((64, 64), np.float32)
    fields = {
        "mean": np.full((P, P), 1.0 / DM, np.float32), "eps": np.tile(np.array([[RMS_EPS, LN_EPS]], np.float32), (P, 1)),
        "mix0": vec(a["norm_mix"][0]), "mix1": vec(a["norm_mix"][1]), "ffn0": vec(a["norm_ffn"][0]),
        "lng": vec(a["a_ln_g"][0]), "lnb": vec(a["a_ln_b"][0]), "kvn": vec(a["kv_norm"]),
        "pe": a["cmp_pe"].reshape(32, P).T, "w00": np.broadcast_to(a["a_w_s"][0, :, 0, 0][None, :], (P, 8)),
        "gate": chunks(bw[:, 1024:]).reshape(P, -1),
        "w1": w1_.reshape(2, 2, 8, P, 64).transpose(3, 0, 2, 1, 4).reshape(P, -1),
        "w2k": part(np.concatenate([w2_[0], zero, zero, w2_[0]], axis=1)), "w2v": part(w2_[1]),
        "bgate": part(a["b_b_gate"].reshape(48, 1)),
    }
    arrays["vectors"] = cat(*[fields[k] for k in VECTORS])
    arrays["params"] = cat(*[fields[k] for k in PARAMS])
    arrays["late"] = cat(vec(a["norm_ffn"][1]), vec(a["norm_final"]), chunks(a["m_w_router"][0]).reshape(P, -1),
                         np.broadcast_to(a["m_b_router"], (P, NE)))
    bs = a["a_b_s"][0]
    arrays["spatial"] = a["a_w_s"][0].transpose(2, 0, 1)
    arrays["spatial_bias"] = np.broadcast_to(cat(bs, bs, np.repeat(bs[:, 0:1], NS, axis=1))[None], (P, 8, NT))
    arrays["consts"] = constants()
    cache = a["cache_kv"]
    n_phys = cache.shape[0]
    arrays["cmp_pages"] = cache[:, :, 0:2].reshape(n_phys, 64, 2, 2, NG, HD).transpose(0, 2, 5, 3, 4, 1).reshape(n_phys, P, 2, NG * 64)
    arrays["k_pages"] = cache[:, :, 2].reshape(n_phys, P, 2, P).transpose(0, 3, 2, 1)
    arrays["v_pages"] = cache[:, :, 3].reshape(n_phys, P, NG * HD)
    win = a["state_win_kv"]
    arrays["win_k"] = win[:, :, 0].reshape(NS, PAST, 2, P).transpose(3, 0, 2, 1).reshape(P, SLOT)
    arrays["win_v"] = win[:, :, 1].reshape(NS, PAGES, P, NG * HD).transpose(2, 0, 1, 3).reshape(P, SLOT)
    arrays["state_win"] = win.reshape(P, -1)
    arrays["page_table"] = a["page_table"].reshape(1, -1)

    nc = bacc.Bacc("TRN2", target_bir_lowering=False, num_devices=1)
    args = []
    for name in list(arrays):
        arrays[name] = np.ascontiguousarray(arrays[name])
        args.append(nc.dram_tensor(f"in_{name}", arrays[name].shape, mybir.dt.from_np(arrays[name].dtype), kind="ExternalInput").ap())
    outs = [("y", (P, KC, NT)), ("v", (P, KC, NT)), ("kv", (P, 12, NT)), ("past", (P, NS * PAST * 512 // P))]
    for name, shape in outs:
        args.append(nc.dram_tensor(f"out_{name}", shape, F32, kind="ExternalOutput").ap())
    build(nc, *args)
    r = run(nc, [{f"in_{k}": v for k, v in arrays.items()}], core_ids=[0]).results[0]
    y, v, kv, past = (np.asarray(r[f"out_{name}"]) for name, _ in outs)

    def tokens_of(z):
        return z.transpose(2, 1, 0).reshape(NT, -1)

    y, v, kv = tokens_of(y), tokens_of(v), tokens_of(kv)
    kv_rows, win_rows = kv[:, 0:1024].reshape(NT, 4, NG, HD), kv[:, 1024:1536].reshape(NT, 2, NG, HD)
    win_sample = np.concatenate([past.reshape(NS, PAST, 2, NG, HD), win_rows[NP:][:, None]], axis=1)
    return (y[None, 0:NP], y[NP:][:, None], kv_rows[None, 0:NP], kv_rows[NP:][:, None], win_rows[None, 0:NP], win_sample,
            v[None, None, P:NP], v[NP:][None, :, None])
```
